# Optimizing a Trainium2 kernel written in Bass

```python
import math
import jax, jax.numpy as jnp
from jax import lax
import numpy as np
import jax
import jax.numpy as jnp

D_MODEL = 1024
BATCH = 1
SEQ = 512
DEPTH = 1

MLA_HEADS = 8
MLA_Q_LORA = 256
MLA_KV_LORA = 128
MLA_NOPE = 64
MLA_ROPE = 32
MLA_V = 64
MLA_QK = MLA_NOPE + MLA_ROPE
MLA_WIDTH = MLA_HEADS * MLA_V
ROPE_THETA = 10000.0
FOX_HEADS = 8
FOX_HEAD_DIM = 64
FOX_WIDTH = FOX_HEADS * FOX_HEAD_DIM
Q_BLOCK = 128
IN_SPLIT_SIZES = (MLA_Q_LORA, MLA_KV_LORA, MLA_ROPE, FOX_WIDTH, FOX_WIDTH, FOX_WIDTH, FOX_HEADS, D_MODEL, D_MODEL)
IN_COLS = MLA_Q_LORA + MLA_KV_LORA + MLA_ROPE + 3 * FOX_WIDTH + FOX_HEADS + 2 * D_MODEL
N_EXPERTS = 64
N_GROUPS = 8
TOPK_GROUPS = 4
TOP_K = 6
D_EXPERT = 256
D_SHARED = 256
ROUTED_SCALE = 2.5
EXPERT_BLOCK = 128
N_MOD = 6
NORM_EPS = 1e-6
NEG_INF = -1e30


def rms_norm(x, gain):
    xf = x.astype(jnp.float32)
    y = xf * lax.rsqrt(jnp.mean(xf * xf, axis=-1, keepdims=True) + NORM_EPS)
    return (y * gain.astype(jnp.float32)).astype(x.dtype)

def split_cols(t, sizes):
    out, start = [], 0
    for n in sizes:
        out.append(t[..., start:start + n])
        start += n
    return out

def apply_rope(x, positions):
    half = x.shape[-1] // 2
    inv_freq = jnp.power(ROPE_THETA, -jnp.arange(half, dtype=jnp.float32) / half)
    ang = positions.astype(jnp.float32)[:, None, :, None] * inv_freq
    cos = jnp.cos(ang).astype(x.dtype)
    sin = jnp.sin(ang).astype(x.dtype)
    x1, x2 = x[..., :half], x[..., half:]
    return jnp.concatenate([x1 * cos - x2 * sin, x2 * cos + x1 * sin], axis=-1)

def causal_block_attention(q, k, v, scale, decay=None):
    B, H, S, _ = q.shape
    dv = v.shape[-1]
    nblk = S // Q_BLOCK

    def to_blocks(t):
        return jnp.moveaxis(t.reshape((B, H, nblk, Q_BLOCK) + t.shape[3:]), 2, 0)

    key_pos = jnp.arange(S)

    def one_block(xs):
        i, qb = xs[0], xs[1]
        logits = jnp.einsum('bhqd,bhkd->bhqk', qb, k).astype(jnp.float32) * scale
        if decay is not None:
            logits = logits + xs[2][..., :, None] - decay[:, :, None, :]
        q_pos = i * Q_BLOCK + jnp.arange(Q_BLOCK)
        logits = jnp.where(key_pos[None, :] <= q_pos[:, None], logits, NEG_INF)
        p = jax.nn.softmax(logits, axis=-1).astype(v.dtype)
        return jnp.einsum('bhqk,bhkd->bhqd', p, v)

    xs = (jnp.arange(nblk), to_blocks(q))
    if decay is not None:
        xs = xs + (to_blocks(decay),)
    out = lax.map(one_block, xs)
    return jnp.moveaxis(out, 0, 2).reshape(B, H, S, dv)

def hybrid_mixer(h, positions, w_in, b_forget, g_q_lat, w_q_up, g_kv_lat, w_kv_up, w_o_mla, w_o_fox, w_out):
    B, S, _ = h.shape
    proj = h @ w_in
    q_lat, kv_lat, k_rope, fq, fk, fv, f_logit, gate_a, gate_b = split_cols(proj, IN_SPLIT_SIZES)

    q = (rms_norm(q_lat, g_q_lat) @ w_q_up).reshape(B, S, MLA_HEADS, MLA_QK).transpose(0, 2, 1, 3)
    q_nope, q_pe = q[..., :MLA_NOPE], apply_rope(q[..., MLA_NOPE:], positions)
    kv = (rms_norm(kv_lat, g_kv_lat) @ w_kv_up).reshape(B, S, MLA_HEADS, MLA_NOPE + MLA_V).transpose(0, 2, 1, 3)
    k_nope, v_mla = kv[..., :MLA_NOPE], kv[..., MLA_NOPE:]
    k_pe = apply_rope(k_rope[:, None, :, :], positions)
    q_mla = jnp.concatenate([q_nope, q_pe], axis=-1)
    k_mla = jnp.concatenate([k_nope, jnp.broadcast_to(k_pe, (B, MLA_HEADS, S, MLA_ROPE))], axis=-1)
    o_mla = causal_block_attention(q_mla, k_mla, v_mla, 1.0 / math.sqrt(MLA_QK))
    o_mla = o_mla.transpose(0, 2, 1, 3).reshape(B, S, MLA_WIDTH)

    def heads(t):
        return t.reshape(B, S, FOX_HEADS, FOX_HEAD_DIM).transpose(0, 2, 1, 3)

    log_f = jax.nn.log_sigmoid((f_logit + b_forget).astype(jnp.float32))
    cum_log_f = jnp.cumsum(log_f, axis=1).transpose(0, 2, 1)
    o_fox = causal_block_attention(heads(fq), heads(fk), heads(fv), 1.0 / math.sqrt(FOX_HEAD_DIM), cum_log_f)
    o_fox = o_fox.transpose(0, 2, 1, 3).reshape(B, S, FOX_WIDTH)

    merged = jax.nn.sigmoid(gate_a) * (o_mla @ w_o_mla) + jax.nn.sigmoid(gate_b) * (o_fox @ w_o_fox)
    return merged @ w_out

def moe_ffn(h, w_router, b_router, w_exp_gate, w_exp_up, w_exp_down, w_sh_gate, w_sh_up, w_sh_down):
    B, S, D = h.shape
    T = B * S
    xf = h.reshape(T, D)

    scores = jax.nn.sigmoid((xf @ w_router).astype(jnp.float32))
    choice = scores + b_router.astype(jnp.float32)
    group_score = lax.top_k(choice.reshape(T, N_GROUPS, N_EXPERTS // N_GROUPS), 2)[0].sum(-1)
    _, group_idx = lax.top_k(group_score, TOPK_GROUPS)
    group_keep = (group_idx[..., None] == jnp.arange(N_GROUPS)).any(axis=-2)
    expert_keep = jnp.repeat(group_keep, N_EXPERTS // N_GROUPS, axis=-1)
    _, expert_idx = lax.top_k(jnp.where(expert_keep, choice, NEG_INF), TOP_K)
    gate = jnp.take_along_axis(scores, expert_idx, axis=-1)
    gate = (gate / gate.sum(-1, keepdims=True) * ROUTED_SCALE).astype(h.dtype)

    n_assign = T * TOP_K
    flat_e = expert_idx.reshape(-1).astype(jnp.int32)
    flat_tok = jnp.arange(n_assign, dtype=jnp.int32) // TOP_K
    order = jnp.argsort(flat_e)
    se, stok, sgate = flat_e[order], flat_tok[order], gate.reshape(-1)[order]
    counts = jnp.zeros((N_EXPERTS,), jnp.int32).at[flat_e].add(1)
    padded = (counts + EXPERT_BLOCK - 1) // EXPERT_BLOCK * EXPERT_BLOCK
    start = jnp.cumsum(counts) - counts
    pend = jnp.cumsum(padded)
    pstart = pend - padded
    dest = pstart[se] + jnp.arange(n_assign, dtype=jnp.int32) - start[se]
    n_blocks = (n_assign + EXPERT_BLOCK - 1) // EXPERT_BLOCK + N_EXPERTS
    n_rows = n_blocks * EXPERT_BLOCK
    row_tok = jnp.full((n_rows,), T, jnp.int32).at[dest].set(stok)
    row_gate = jnp.zeros((n_rows,), h.dtype).at[dest].set(sgate)
    block_e = jnp.minimum(
        jnp.searchsorted(pend, jnp.arange(n_blocks, dtype=jnp.int32) * EXPERT_BLOCK, side='right'),
        N_EXPERTS - 1)
    x_pad = jnp.concatenate([xf, jnp.zeros((1, D), xf.dtype)], axis=0)

    def expert_block(xs):
        tok, g, e = xs
        xb = x_pad[tok]
        hb = jax.nn.silu(xb @ w_exp_gate[e]) * (xb @ w_exp_up[e])
        return (hb @ w_exp_down[e]) * g[:, None]

    yb = lax.map(expert_block, (row_tok.reshape(n_blocks, EXPERT_BLOCK),
                                row_gate.reshape(n_blocks, EXPERT_BLOCK), block_e))
    routed = jax.ops.segment_sum(yb.reshape(n_rows, D), row_tok, num_segments=T + 1)[:T]
    shared = (jax.nn.silu(xf @ w_sh_gate) * (xf @ w_sh_up)) @ w_sh_down
    return (shared + routed).reshape(B, S, D)

def dense_init(k, shape, fan_in, scale=1.0):
    return scale * fan_in ** -0.5 * jax.random.normal(k, shape, jnp.float32)

def first_inputs(seed: int = 0) -> dict:
    key = jax.random.key(seed)
    ks = jax.random.split(key, 25)
    L, D, E = DEPTH, D_MODEL, N_EXPERTS

    def gain(k, shape):
        return 1.0 + 0.02 * jax.random.normal(k, shape, jnp.float32)

    offset = jax.random.randint(ks[2], (BATCH, 1), 0, 1024, dtype=jnp.int32)
    return {
        'x': jax.random.normal(ks[0], (BATCH, SEQ, D), jnp.float32),
        'c': jax.random.normal(ks[1], (BATCH, D), jnp.float32),
        'positions': jnp.arange(SEQ, dtype=jnp.int32)[None, :] + offset,
        'w_mod': dense_init(ks[3], (L, D, N_MOD * D), D, 0.5),
        'b_mod': 0.02 * jax.random.normal(ks[4], (L, N_MOD * D), jnp.float32),
        'g_mix_norm': gain(ks[5], (L, D)),
        'w_in': dense_init(ks[6], (L, D, IN_COLS), D),
        'b_forget': 1.0 + 3.0 * jax.random.uniform(ks[7], (L, FOX_HEADS), jnp.float32),
        'g_q_lat': gain(ks[8], (L, MLA_Q_LORA)),
        'w_q_up': dense_init(ks[9], (L, MLA_Q_LORA, MLA_HEADS * MLA_QK), MLA_Q_LORA),
        'g_kv_lat': gain(ks[10], (L, MLA_KV_LORA)),
        'w_kv_up': dense_init(ks[11], (L, MLA_KV_LORA, MLA_HEADS * (MLA_NOPE + MLA_V)), MLA_KV_LORA),
        'w_o_mla': dense_init(ks[12], (L, MLA_WIDTH, D), MLA_WIDTH),
        'w_o_fox': dense_init(ks[13], (L, FOX_WIDTH, D), FOX_WIDTH),
        'w_out': dense_init(ks[14], (L, D, D), D),
        'g_ffn_norm': gain(ks[15], (L, D)),
        'w_router': dense_init(ks[16], (L, D, E), D),
        'b_router': 0.01 * jax.random.normal(ks[17], (L, E), jnp.float32),
        'w_exp_gate': dense_init(ks[18], (L, E, D, D_EXPERT), D),
        'w_exp_up': dense_init(ks[19], (L, E, D, D_EXPERT), D),
        'w_exp_down': dense_init(ks[20], (L, E, D_EXPERT, D), D_EXPERT),
        'w_sh_gate': dense_init(ks[21], (L, D, D_SHARED), D),
        'w_sh_up': dense_init(ks[22], (L, D, D_SHARED), D),
        'w_sh_down': dense_init(ks[23], (L, D_SHARED, D), D_SHARED),
        'g_final': gain(ks[24], (D,)),
    }

def first_block(x, c, positions, w_mod, b_mod, g_mix_norm, w_in, b_forget, g_q_lat, w_q_up, g_kv_lat,
              w_kv_up, w_o_mla, w_o_fox, w_out, g_ffn_norm, w_router, b_router, w_exp_gate, w_exp_up,
              w_exp_down, w_sh_gate, w_sh_up, w_sh_down, g_final):
    cond = jax.nn.silu(c)
    for l in range(DEPTH):
        mod = cond @ w_mod[l] + b_mod[l]
        shift_m, scale_m, gate_m, shift_f, scale_f, gate_f = [m[:, None, :] for m in jnp.split(mod, N_MOD, axis=-1)]
        h = rms_norm(x, g_mix_norm[l]) * (1.0 + scale_m) + shift_m
        x = x + gate_m * hybrid_mixer(h, positions, w_in[l], b_forget[l], g_q_lat[l], w_q_up[l], g_kv_lat[l],
                                      w_kv_up[l], w_o_mla[l], w_o_fox[l], w_out[l])
        h = rms_norm(x, g_ffn_norm[l]) * (1.0 + scale_f) + shift_f
        x = x + gate_f * moe_ffn(h, w_router[l], b_router[l], w_exp_gate[l], w_exp_up[l], w_exp_down[l],
                                 w_sh_gate[l], w_sh_up[l], w_sh_down[l])
    return rms_norm(x, g_final)


HEAD_DIM = 64
H_NSA = 4
H_DIL = 6
H_SB = 6
DIL_PAIRS = ((128, 1), (512, 4), (2048, 16))
N_DIL_GROUPS = len(DIL_PAIRS)
H_PER_DIL = H_DIL // N_DIL_GROUPS
CMP_LEN = 32
CMP_STRIDE = 16
CMP_HIDDEN = 128
SEL_BLOCK = 64
SEL_TOPK = 16
WIN_NSA = 512
D_FF = 4 * D_MODEL
N_SOFTMAX_HEADS = H_NSA + H_DIL
RMS_EPS = 1e-6
NEG_INF_2 = -1e30
FORCE_BONUS = 1e4

NSA_Q_W = H_NSA * HEAD_DIM
NSA_KV_W = 6 * HEAD_DIM
NSA_GATE_W = 3 * H_NSA
DIL_W = 3 * H_DIL * HEAD_DIM
SB_W = 3 * H_SB * HEAD_DIM
D_PROJ = NSA_Q_W + NSA_KV_W + NSA_GATE_W + DIL_W + SB_W
PROJ_SPLITS = (NSA_Q_W, NSA_Q_W + NSA_KV_W, NSA_Q_W + NSA_KV_W + NSA_GATE_W,
               NSA_Q_W + NSA_KV_W + NSA_GATE_W + DIL_W)
D_CAT = (H_NSA + H_PER_DIL + H_SB) * HEAD_DIM


def rms_norm_2(x, g):
    xf = x.astype(jnp.float32)
    y = xf * lax.rsqrt(jnp.mean(xf * xf, axis=-1, keepdims=True) + RMS_EPS)
    return (y * g.astype(jnp.float32)).astype(x.dtype)

def alibi_slopes():
    i = jnp.arange(1, N_SOFTMAX_HEADS + 1, dtype=jnp.float32)
    return jnp.exp2(-8.0 * i / N_SOFTMAX_HEADS)

def masked_softmax(s, mask):
    s = jnp.where(mask, s, NEG_INF_2)
    m = jnp.max(s, axis=-1, keepdims=True)
    p = jnp.where(mask, jnp.exp(s - m), 0.0)
    l = jnp.maximum(jnp.sum(p, axis=-1, keepdims=True), 1e-30)
    return p / l, (m + jnp.log(l))[..., 0]

def unblock(y):
    y = jnp.moveaxis(y, 0, 1)
    return y.reshape((y.shape[0], y.shape[1] * y.shape[2]) + y.shape[3:])

def nsa_mixer(q, kv, gate_logits, qk_gain, cmp_pe, cmp_w1, cmp_w2, slopes):
    B, S = q.shape[0], q.shape[1]
    dt = q.dtype
    scale = HEAD_DIM ** -0.5
    q = rms_norm_2(q, qk_gain[0])
    k_sel = rms_norm_2(kv[:, :, 2], qk_gain[2])
    v_sel = kv[:, :, 3]
    k_win = rms_norm_2(kv[:, :, 4], qk_gain[3])
    v_win = kv[:, :, 5]
    n_cmp = (S - CMP_LEN) // CMP_STRIDE + 1
    cmp_start = CMP_STRIDE * jnp.arange(n_cmp)
    cmp_end = cmp_start + CMP_LEN - 1
    cmp_idx = cmp_start[:, None] + jnp.arange(CMP_LEN)[None]
    raw = kv[:, :, 0:2].transpose(0, 2, 1, 3)[:, :, cmp_idx]
    raw = (raw + cmp_pe[None, :, None]).reshape(B, 2, n_cmp, CMP_LEN * HEAD_DIM)
    hid = jax.nn.gelu(jnp.einsum('bcnf,cfh->bcnh', raw, cmp_w1))
    kv_c = jnp.einsum('bcnh,chd->bcnd', hid, cmp_w2)
    k_c = rms_norm_2(kv_c[:, 0], qk_gain[1])
    v_c = kv_c[:, 1]
    n_sel = S // SEL_BLOCK
    sel_start = SEL_BLOCK * jnp.arange(n_sel)
    overlap = ((cmp_start[:, None] <= sel_start[None] + SEL_BLOCK - 1)
               & (cmp_end[:, None] >= sel_start[None])).astype(jnp.float32)
    k_top = min(SEL_TOPK, n_sel)
    sel_offsets = jnp.arange(SEL_BLOCK)
    sel_ids = jnp.arange(n_sel)
    k_win_p = jnp.pad(k_win, ((0, 0), (WIN_NSA, 0), (0, 0)))
    v_win_p = jnp.pad(v_win, ((0, 0), (WIN_NSA, 0), (0, 0)))
    win_offsets = jnp.arange(WIN_NSA + Q_BLOCK)
    gates = jax.nn.sigmoid(gate_logits.astype(jnp.float32)).astype(dt)
    gather_rows = jax.vmap(lambda a, i: a[i])

    def block(n):
        t0 = n * Q_BLOCK
        t = t0 + jnp.arange(Q_BLOCK)
        qb = lax.dynamic_slice_in_dim(q, t0, Q_BLOCK, axis=1)
        d_c = (t[:, None] - cmp_end[None]).astype(jnp.float32)
        s = jnp.einsum('bqhd,bnd->bhqn', qb, k_c).astype(jnp.float32) * scale - slopes[:, None, None] * d_c
        p_c, _ = masked_softmax(s, d_c >= 0)
        o_c = jnp.einsum('bhqn,bnd->bqhd', p_c.astype(dt), v_c)
        imp = jnp.einsum('bhqn,nj->bqj', p_c, overlap)
        cur = t // SEL_BLOCK
        forced = (sel_ids[None] == 0) | (sel_ids[None] == cur[:, None]) | (sel_ids[None] == cur[:, None] - 1)
        imp = jnp.where(forced, imp + FORCE_BONUS, imp)
        imp = jnp.where(sel_start[None] <= t[:, None], imp, NEG_INF_2)
        _, top = lax.top_k(imp, k_top)
        tok = (top[..., None] * SEL_BLOCK + sel_offsets).reshape(B, Q_BLOCK, k_top * SEL_BLOCK)
        k_g = gather_rows(k_sel, tok)
        v_g = gather_rows(v_sel, tok)
        d_s = (t[None, :, None] - tok).astype(jnp.float32)
        s = jnp.einsum('bqhd,bqkd->bhqk', qb, k_g).astype(jnp.float32) * scale - slopes[None, :, None, None] * d_s[:, None]
        p_s, _ = masked_softmax(s, (d_s >= 0)[:, None])
        o_s = jnp.einsum('bhqk,bqkd->bqhd', p_s.astype(dt), v_g)
        k_w = lax.dynamic_slice_in_dim(k_win_p, t0, WIN_NSA + Q_BLOCK, axis=1)
        v_w = lax.dynamic_slice_in_dim(v_win_p, t0, WIN_NSA + Q_BLOCK, axis=1)
        kpos = t0 - WIN_NSA + win_offsets
        d_w = (t[:, None] - kpos[None]).astype(jnp.float32)
        mask_w = (d_w >= 0) & (d_w < WIN_NSA) & (kpos[None] >= 0)
        s = jnp.einsum('bqhd,bkd->bhqk', qb, k_w).astype(jnp.float32) * scale - slopes[:, None, None] * d_w
        p_w, _ = masked_softmax(s, mask_w)
        o_w = jnp.einsum('bhqk,bkd->bqhd', p_w.astype(dt), v_w)
        g = lax.dynamic_slice_in_dim(gates, t0, Q_BLOCK, axis=1)
        return g[..., 0:1] * o_c + g[..., 1:2] * o_s + g[..., 2:3] * o_w

    return unblock(lax.map(block, jnp.arange(S // Q_BLOCK)))

def dilated_mixer(qkv, qk_gain, slopes):
    S = qkv.shape[1]
    dt = qkv.dtype
    scale = HEAD_DIM ** -0.5
    q = rms_norm_2(qkv[:, :, 0], qk_gain[0])
    k = rms_norm_2(qkv[:, :, 1], qk_gain[1])
    v = qkv[:, :, 2]
    k_groups = [k[:, :, g] for g in range(N_DIL_GROUPS)]
    v_groups = [v[:, :, g] for g in range(N_DIL_GROUPS)]
    slopes_g = slopes.reshape(N_DIL_GROUPS, H_PER_DIL)

    def block(n):
        t0 = n * Q_BLOCK
        t = t0 + jnp.arange(Q_BLOCK)
        qb = lax.dynamic_slice_in_dim(q, t0, Q_BLOCK, axis=1)
        outs, lses = [], []
        for g, (w, r) in enumerate(DIL_PAIRS):
            dist = r * jnp.arange(w // r + 1)
            kidx = t[:, None] - dist[None]
            valid = kidx >= 0
            kidx = jnp.maximum(kidx, 0)
            k_g = k_groups[g][:, kidx]
            v_g = v_groups[g][:, kidx]
            s = (jnp.einsum('bqhd,bqjhd->bhqj', qb[:, :, g], k_g).astype(jnp.float32) * scale
                 - slopes_g[g][:, None, None] * dist.astype(jnp.float32))
            p, lse = masked_softmax(s, valid)
            outs.append(jnp.einsum('bhqj,bqjhd->bqhd', p.astype(dt), v_g))
            lses.append(lse)
        alpha = jax.nn.softmax(jnp.stack(lses), axis=0)
        alpha = jnp.transpose(alpha, (0, 1, 3, 2))[..., None].astype(dt)
        return jnp.sum(alpha * jnp.stack(outs), axis=0)

    return unblock(lax.map(block, jnp.arange(S // Q_BLOCK)))

def stick_breaking_mixer(qkv):
    S = qkv.shape[1]
    dt = qkv.dtype
    scale = HEAD_DIM ** -0.5
    q, k, v = qkv[:, :, 0], qkv[:, :, 1], qkv[:, :, 2]
    kpos = jnp.arange(S)

    def block(n):
        t0 = n * Q_BLOCK
        t = t0 + jnp.arange(Q_BLOCK)
        qb = lax.dynamic_slice_in_dim(q, t0, Q_BLOCK, axis=1)
        z = jnp.einsum('bqhd,bshd->bhqs', qb, k).astype(jnp.float32) * scale
        causal = kpos[None] < t[:, None]
        log_beta = jax.nn.log_sigmoid(z)
        log_fail = jnp.where(causal, jax.nn.log_sigmoid(-z), 0.0)
        after = lax.cumsum(log_fail, axis=3, reverse=True) - log_fail
        a = jnp.where(causal, jnp.exp(log_beta + after), 0.0)
        return jnp.einsum('bhqs,bshd->bqhd', a.astype(dt), v)

    return unblock(lax.map(block, jnp.arange(S // Q_BLOCK)))

def second_inputs(seed: int = 0) -> dict:
    key = jax.random.key(seed)
    ks = jax.random.split(key, 12)
    f32 = jnp.float32

    def nrm(k, shape, fan_in):
        return jax.random.normal(k, shape, f32) * (fan_in ** -0.5)

    def gain(k, shape):
        return 1.0 + 0.02 * jax.random.normal(k, shape, f32)

    return {
        'x': jax.random.normal(ks[0], (BATCH, SEQ, D_MODEL), f32),
        'norm_mix': gain(ks[1], (DEPTH, D_MODEL)),
        'norm_mlp': gain(ks[2], (DEPTH, D_MODEL)),
        'w_in': nrm(ks[3], (DEPTH, D_MODEL, D_PROJ), D_MODEL),
        'qk_gain_nsa': gain(ks[4], (DEPTH, 4, HEAD_DIM)),
        'qk_gain_dil': gain(ks[5], (DEPTH, 2, HEAD_DIM)),
        'cmp_pe': 0.1 * jax.random.normal(ks[6], (DEPTH, 2, CMP_LEN, HEAD_DIM), f32),
        'cmp_w1': nrm(ks[7], (DEPTH, 2, CMP_LEN * HEAD_DIM, CMP_HIDDEN), CMP_LEN * HEAD_DIM),
        'cmp_w2': nrm(ks[8], (DEPTH, 2, CMP_HIDDEN, HEAD_DIM), CMP_HIDDEN),
        'w_out': nrm(ks[9], (DEPTH, D_CAT, D_MODEL), D_CAT),
        'w_up': nrm(ks[10], (DEPTH, D_MODEL, D_FF), D_MODEL),
        'w_down': nrm(ks[11], (DEPTH, D_FF, D_MODEL), D_FF),
    }

def second_block(x, norm_mix, norm_mlp, w_in, qk_gain_nsa, qk_gain_dil, cmp_pe, cmp_w1, cmp_w2,
              w_out, w_up, w_down):
    B, S, _ = x.shape
    slopes = alibi_slopes()
    slopes_dil = slopes[:H_DIL]
    slopes_nsa = slopes[H_DIL:]
    for l in range(DEPTH):
        h = rms_norm_2(x, norm_mix[l])
        proj = h @ w_in[l]
        a_q, a_kv, a_g, b_qkv, c_qkv = jnp.split(proj, PROJ_SPLITS, axis=-1)
        o_a = nsa_mixer(a_q.reshape(B, S, H_NSA, HEAD_DIM), a_kv.reshape(B, S, 6, HEAD_DIM),
                        a_g.reshape(B, S, H_NSA, 3), qk_gain_nsa[l], cmp_pe[l], cmp_w1[l],
                        cmp_w2[l], slopes_nsa)
        o_b = dilated_mixer(b_qkv.reshape(B, S, 3, N_DIL_GROUPS, H_PER_DIL, HEAD_DIM),
                            qk_gain_dil[l], slopes_dil)
        o_c = stick_breaking_mixer(c_qkv.reshape(B, S, 3, H_SB, HEAD_DIM))
        cat = jnp.concatenate([o_a.reshape(B, S, -1), o_b.reshape(B, S, -1),
                               o_c.reshape(B, S, -1)], axis=-1)
        x = x + cat @ w_out[l]
        h = rms_norm_2(x, norm_mlp[l])
        x = x + jnp.square(jax.nn.relu(h @ w_up[l])) @ w_down[l]
    return x


def setup_inputs(seed=0):
    out = dict(first_inputs(seed))
    for name, value in second_inputs(seed + 1).items():
        if name != "x":
            out[name + "_2"] = value
    return out


def reference(
    x, c, positions, w_mod, b_mod, g_mix_norm, w_in, b_forget, g_q_lat, w_q_up, g_kv_lat,
    w_kv_up, w_o_mla, w_o_fox, w_out, g_ffn_norm, w_router, b_router, w_exp_gate, w_exp_up,
    w_exp_down, w_sh_gate, w_sh_up, w_sh_down, g_final, norm_mix_2, norm_mlp_2, w_in_2,
    qk_gain_nsa_2, qk_gain_dil_2, cmp_pe_2, cmp_w1_2, cmp_w2_2, w_out_2, w_up_2, w_down_2,
):
    x = first_block(
        x, c, positions, w_mod, b_mod, g_mix_norm, w_in, b_forget, g_q_lat, w_q_up, g_kv_lat,
        w_kv_up, w_o_mla, w_o_fox, w_out, g_ffn_norm, w_router, b_router, w_exp_gate, w_exp_up,
        w_exp_down, w_sh_gate, w_sh_up, w_sh_down, g_final,
    )
    return second_block(
        x, norm_mix_2, norm_mlp_2, w_in_2, qk_gain_nsa_2, qk_gain_dil_2, cmp_pe_2, cmp_w1_2,
        cmp_w2_2, w_out_2, w_up_2, w_down_2,
    )


_drawn_inputs = setup_inputs


def setup_inputs(seed=0):
    import zlib

    import numpy as np

    out = dict(_drawn_inputs(seed))
    spreads = {}
    factors = {'g_mix_norm': 3.141,
     'g_q_lat': 8.0,
     'g_kv_lat': 6.682,
     'norm_mix_2': 4.624,
     'norm_mlp_2': 3.387,
     'qk_gain_nsa_2': 8.0,
     'qk_gain_dil_2': 8.0,
     'cmp_pe_2': 2.871}
    for name, (base, spread) in spreads.items():
        noise = np.random.default_rng([zlib.crc32(name.encode()), seed]).standard_normal(out[name].shape)
        drawn = base * np.exp(spread * noise) if base else spread * noise
        out[name] = jnp.asarray(drawn.astype(out[name].dtype))
    for name, factor in factors.items():
        out[name] = (out[name] * factor).astype(out[name].dtype)
    return out
```

```python
from contextlib import ExitStack, contextmanager

import concourse.bass as bass
from concourse import mybir

F32 = mybir.dt.float32
F32R = mybir.dt.float32r
BF16 = mybir.dt.bfloat16
I32 = mybir.dt.int32
U32 = mybir.dt.uint32
ACT = mybir.ActivationFunctionType
ALU = mybir.AluOpType
AX = mybir.AxisListType

P = 128
S = 512
NT = S // P
D = 1024
KD = D // P
EPS = 1e-6
NEG = -1e30

H1 = 8
Q_LORA, KV_LORA, ROPE, NOPE, DH = 256, 128, 32, 64, 64
HW = H1 * DH
C_KV, C_KR, C_FQ = 256, 384, 416
C_FK, C_FV, C_FL, C_GA = 928, 1440, 1952, 1960

E = 64
NG = 8
TOPG = 4
TOPK = 6
F = 256
BLOCKS = S * TOPK // P + E
ROUTED_SCALE = 2.5

H_NSA, H_DIL, H_SB = 4, 6, 6
N_CMP = (S - 32) // 16 + 1
W2 = 2956
C2_KV, C2_G, C2_B, C2_C = 256, 640, 652, 1804
D_CAT = 768
FF = 4 * D


class Chain:

    def __init__(self, eng, sem):
        self.eng, self.sem, self.base, self.n = eng, sem, 0, 0

    def __call__(self, ins):
        self.n += 1
        ins.then_inc(self.sem, 1)
        self.eng.wait_ge(self.sem, self.base + self.n)


class Ctx:

    def __init__(self, nc, ctx):
        self.nc, self.ctx, self.stage_sems = nc, ctx, []

    def sem(self, name):
        self.stage_sems.append(self.nc.alloc_semaphore(name))
        return self.stage_sems[-1]

    @contextmanager
    def stage(self):
        with ExitStack() as st:
            yield st
        self.nc.clear_and_free_semaphores(self.stage_sems)
        self.stage_sems = []
        self.nc.all_engine_barrier()

    def sb(self, name, shape, dt=F32, ctx=None):
        return (ctx or self.ctx).enter_context(self.nc.sbuf_tensor(name, shape, dt))

    def dram(self, name, shape, dt=F32):
        return self.nc.dram_tensor(name, shape, dt).ap()


def bcast_rows(row, n):
    return row.broadcast_to([P, n])


def split_product(nc, out, left, right, start, stop):
    for i, (a, b) in enumerate(((0, 0), (0, 1), (1, 0))):
        mm = nc.tensor.matmul(out, left[a], right[b], start=start and i == 0, stop=stop and i == 2)
    return mm


def low_part(nc, dst, x, high):
    return nc.vector.tensor_tensor(dst, x, high.bitcast(F32), ALU.subtract)


class SplitWeights:

    def __init__(self, g, name, ctx, kt=4):
        self.nc = g.nc
        self.raw = g.sb(name + "_raw", [P, 2, kt, 512], ctx=ctx)
        self.parts = g.sb(name + "_parts", [P, 2, 2, kt, 512], F32R, ctx=ctx)
        self.s_raw = [g.sem(f"{name}_loaded{i}") for i in range(2)]
        self.s_high = g.sem(name + "_high_ready")
        self.s_low = g.sem(name + "_low_ready")

    def load(self, eng, src, base, u, width=512):
        at_least(eng, self.s_high, base, u - 1)
        at_least(eng, self.s_low, base, u - 1)
        eng.dma_start(self.raw[:, u % 2, :, 0:width], src).then_inc(self.s_raw[u % 2], 16)

    def high(self, act, base, u, s_used, per_slab, width=512):
        act.wait_ge(self.s_raw[u % 2], 8 * base + 16 * (u // 2) + 16)
        at_least(act, s_used, per_slab * base, per_slab * (u - 1))
        self.nc.scalar.copy(self.parts[:, u % 2, 0, :, 0:width], self.raw[:, u % 2, :, 0:width]).then_inc(self.s_high, 1)

    def low(self, dve, base, u, s_used, per_slab, width=512):
        dve.wait_ge(self.s_high, base + u + 1)
        at_least(dve, s_used, per_slab * base, per_slab * (u - 1))
        low_part(self.nc, self.parts[:, u % 2, 1, :, 0:width], self.raw[:, u % 2, :, 0:width],
                 self.parts[:, u % 2, 0, :, 0:width]).then_inc(self.s_low, 1)

    def ready(self, pe, base, u):
        pe.wait_ge(self.s_high, base + u + 1)
        pe.wait_ge(self.s_low, base + u + 1)

    def at(self, u, k, c0, c1):
        return [self.parts[:, u % 2, a, k, c0:c1] for a in range(2)]


def parts_of(cols, k, c0=0, c1=S):
    return [cols[:, a, k, c0:c1] for a in range(2)]


def setup_stage(g, io):
    nc = g.nc
    with g.stage() as st:
        w = g.sb("modw", [P, 3, KD, 512], ctx=st)
        ccol = g.sb("ccol", [P, 3, KD], ctx=st)
        cond = g.sb("cond", [P, KD, P], ctx=st)
        maskf = g.sb("maskf", [P, 5, 512], ctx=st)
        s_const = g.sem("const_loaded")
        s_w = [g.sem(f"modw_loaded{i}") for i in range(3)]
        s_sig = g.sem("cond_sigmoid")
        s_cond = g.sem("cond_ready")
        s_ps = g.sem("mod_psum_ready")
        s_ev = g.sem("mod_evacuated")
        s_dve = g.sem("setup_dve_steps")
        wmod = io["w_mod"][0].rearrange("(k p) n -> p k n", p=P)
        NS = 6 * D // 512
        loads = 8
        block = st.enter_context(nc.Block())

        @block.sync
        def _(sp):
            sp.dma_start(ccol[:, 0, :], io["c"].rearrange("a (k p) -> p (a k)", p=P),
                         allow_slow_non_contiguous=True).then_inc(s_const, 16)
            sp.dma_start(g.ident[:], io["const_ident"]).then_inc(s_const, 16)
            sp.dma_start(g.tri[:], io["const_tri"]).then_inc(s_const, 16)
            sp.dma_start(maskf[:], io["const_mask"]).then_inc(s_const, 16)
            sp.dma_start(g.iota[:], io["const_iota"]).then_inc(s_const, 16)
            sp.dma_start(g.ropec[:], io["const_rope"]).then_inc(s_const, 16)
            sp.dma_start(g.mod[:], bcast_rows(io["b_mod"], 6 * D)).then_inc(s_const, 16)
            sp.dma_start(g.x[:], io["x"][0].rearrange("(t p) d -> p t d", p=P)).then_inc(s_const, 16)
            for i in range(3):
                sp.dma_start(w[:, i], wmod[:, :, i * 512:i * 512 + 512]).then_inc(s_w[i], 16)
            with sp.Fori(0, NS // 3 - 1) as i:
                for j in range(3):
                    sp.wait_ge(s_ps, 3 * i + j + 1)
                    sp.dma_start(w[:, j], wmod[:, :, bass.ds((3 * i + j + 3) * 512, 512)]).then_inc(s_w[j], 16)

        @block.scalar
        def _(act):
            act.wait_ge(s_const, 16 * loads)
            nc.scalar.activation(ccol[:, 1, :], ccol[:, 0, :], ACT.Sigmoid).then_inc(s_sig, 1)

        @block.vector
        def _(dve):
            link = Chain(dve, s_dve)
            dve.wait_ge(s_const, 16 * loads)
            nc.vector.tensor_copy(g.mask[:], maskf[:])
            nc.vector.tensor_copy(g.identb[:], g.ident[:])
            link(nc.vector.memset(g.ones[:], 1.0))
            dve.wait_ge(s_sig, 1)
            link(nc.vector.tensor_tensor(ccol[:, 2, :], ccol[:, 0, :], ccol[:, 1, :], ALU.mult))
            nc.vector.tensor_copy(cond[:], ccol[:, 2, :].unsqueeze(2).broadcast_to([P, KD, P])).then_inc(s_cond, 1)
            with dve.Fori(0, NS // 3) as i:
                for j in range(3):
                    dve.wait_ge(s_ps, 3 * i + j + 1)
                    m = g.mod[:, bass.ds((3 * i + j) * 512, 512)]
                    nc.vector.tensor_tensor(m, g.ps[:, j, :], m, ALU.add).then_inc(s_ev, 1)

        @block.tensor
        def _(pe):
            pe.wait_ge(s_cond, 1)
            for j in range(3):
                pe.wait_ge(s_w[j], 16)
                for k in range(KD):
                    mm = nc.tensor.matmul(g.ps[:, j, :], cond[:, k, :], w[:, j, k, :], start=k == 0, stop=k == KD - 1)
                mm.then_inc(s_ps, 1)
            with pe.Fori(1, NS // 3) as i:
                for j in range(3):
                    pe.wait_ge(s_w[j], 16 * i + 16)
                    pe.wait_ge(s_ev, 3 * i + j - 2)
                    for k in range(KD):
                        mm = nc.tensor.matmul(g.ps[:, j, :], cond[:, k, :], w[:, j, k, :], start=k == 0, stop=k == KD - 1)
                    mm.then_inc(s_ps, 1)


def norm_stage(g, name, gain, hT, scale=None, shift=None, h_dram=None, out_x=None):
    nc = g.nc
    with g.stage() as st:
        h = g.x if out_x else g.sb(name + "_h", [P, NT, D], ctx=st)
        junk = g.sb(name + "_junk", [P, NT, D], ctx=st) if out_x else h
        gain_sb = g.sb(name + "_gain", [P, D], ctx=st)
        stat = g.sb(name + "_stat", [P, 3, NT], ctx=st)
        s_gain = g.sem(name + "_gain_loaded")
        s_sq = g.sem(name + "_squares_summed")
        s_ms = g.sem(name + "_mean_square_ready")
        s_h = g.sem(name + "_h_ready")
        s_t = g.sem(name + "_turned")
        s_hi = g.sem(name + "_high_ready")
        s_out = g.sem(name + "_h_stored")
        s_dve = g.sem(name + "_dve_steps")
        block = st.enter_context(nc.Block())

        @block.sync
        def _(sp):
            sp.dma_start(gain_sb[:], bcast_rows(gain, D)).then_inc(s_gain, 16)
            if h_dram is not None:
                for t in range(NT):
                    sp.wait_ge(s_h, t + 1)
                    sp.dma_start(h_dram[t * P:t * P + P, :], h[:, t, :]).then_inc(s_out, 16)
                sp.wait_ge(s_out, 16 * NT)

        @block.scalar
        def _(act):
            for t in range(NT):
                nc.scalar.activation(junk[:, t, :], g.x[:, t, :], ACT.Square,
                                     accum_out=stat[:, 0, t:t + 1]).then_inc(s_sq, 1)
            act.wait_ge(s_ms, 1)
            nc.scalar.activation(stat[:, 2, :], stat[:, 1, :], ACT.Sqrt).then_inc(s_sq, 1)
            if not out_x:
                for b in range(2 * NT):
                    act.wait_ge(s_t, b + 1)
                    k, t = 4 * (b % 2), b // 2
                    nc.scalar.copy(hT[:, 0, k:k + 4, t * P:t * P + P],
                                   g.ps[:, b, :].rearrange("p (k q) -> p k q", k=4)).then_inc(s_hi, 1)

        @block.vector
        def _(dve):
            link = Chain(dve, s_dve)
            dve.wait_ge(s_gain, 16)
            if scale is not None:
                link(nc.vector.scalar_tensor_tensor(gain_sb[:], scale, 1.0, gain_sb[:], ALU.add, ALU.mult))
            dve.wait_ge(s_sq, NT)
            nc.vector.tensor_scalar(stat[:, 1, :], stat[:, 0, :], 1.0 / D, EPS, ALU.mult, ALU.add).then_inc(s_ms, 1)
            dve.wait_ge(s_sq, NT + 1)
            link(nc.vector.reciprocal(stat[:, 1, :], stat[:, 2, :]))
            for t in range(NT):
                ins = nc.vector.scalar_tensor_tensor(h[:, t, :], g.x[:, t, :], stat[:, 1, t:t + 1], gain_sb[:],
                                                     ALU.mult, ALU.mult)
                if shift is not None:
                    link(ins)
                    ins = nc.vector.tensor_tensor(h[:, t, :], h[:, t, :], shift, ALU.add)
                ins.then_inc(s_h, 1)
            if not out_x:
                for b in range(2 * NT):
                    dve.wait_ge(s_hi, b + 1)
                    k, t = 4 * (b % 2), b // 2
                    low_part(nc, hT[:, 1, k:k + 4, t * P:t * P + P], g.ps[:, b, :].rearrange("p (k q) -> p k q", k=4),
                             hT[:, 0, k:k + 4, t * P:t * P + P])

        if not out_x:
            @block.tensor
            def _(pe):
                for t in range(NT):
                    pe.wait_ge(s_h, t + 1)
                    for half in range(2):
                        for k in range(4):
                            c = (4 * half + k) * P
                            tr = nc.tensor.transpose(g.ps[:, 2 * t + half, k * P:k * P + P], h[:, t, c:c + P], g.ident[:])
                        tr.then_inc(s_t, 1)


def turn_stage(g, name, rows, width, cols, dram=None):
    nc = g.nc
    n = width // P
    with g.stage() as st:
        s_t = g.sem(name + "_turned")
        s_act = g.sem(name + "_act_evacuated")
        s_dve = g.sem(name + "_dve_evacuated")
        s_st = g.sem(name + "_stored")
        block = st.enter_context(nc.Block())

        if dram is not None:
            @block.sync
            def _(sp):
                for k in range(n):
                    sp.wait_ge((s_act, s_dve)[k % 2], k // 2 + 1)
                    sp.dma_start(dram[k * P:k * P + P, :], cols[:, k, :]).then_inc(s_st, 16)
                sp.wait_ge(s_st, 16 * n)

        @block.tensor
        def _(pe):
            for k in range(n):
                if k >= 8:
                    pe.wait_ge((s_act, s_dve)[k % 2], (k - 8) // 2 + 1)
                for t in range(NT):
                    tr = nc.tensor.transpose(g.ps[:, k % 8, t * P:t * P + P], rows[:, t, k * P:k * P + P], g.ident[:])
                tr.then_inc(s_t, 1)

        @block.scalar
        def _(act):
            for k in range(0, n, 2):
                act.wait_ge(s_t, k + 1)
                nc.scalar.copy(cols[:, k, :], g.ps[:, k % 8, :]).then_inc(s_act, 1)

        @block.vector
        def _(dve):
            for k in range(1, n, 2):
                dve.wait_ge(s_t, k + 1)
                nc.vector.tensor_copy(cols[:, k, :], g.ps[:, k % 8, :]).then_inc(s_dve, 1)


def turn_parts_stage(g, name, rows, width, cols):
    nc = g.nc
    n = width // P
    with g.stage() as st:
        s_t = g.sem(name + "_turned")
        s_hi = g.sem(name + "_high_ready")
        block = st.enter_context(nc.Block())

        @block.tensor
        def _(pe):
            for k in range(n):
                for t in range(NT):
                    tr = nc.tensor.transpose(g.ps[:, k, t * P:t * P + P], rows[:, t, k * P:k * P + P], g.ident[:])
                tr.then_inc(s_t, 1)

        @block.scalar
        def _(act):
            for k in range(n):
                act.wait_ge(s_t, k + 1)
                nc.scalar.copy(cols[:, 0, k, :], g.ps[:, k, :]).then_inc(s_hi, 1)

        @block.vector
        def _(dve):
            for k in range(n):
                dve.wait_ge(s_hi, k + 1)
                low_part(nc, cols[:, 1, k, :], g.ps[:, k, :], cols[:, 0, k, :])


def project1_stage(g, io, hT, t1):
    nc = g.nc
    w_in = io["w_in"][0].rearrange("(k p) n -> p k n", p=P)
    slabs = [("rows", 0, 416), ("cols", C_FQ, 512), ("cols", C_FK, 512), ("rows", C_FV, 512)]
    slabs += [("rows", C_GA + 512 * i, 512) for i in range(4)]
    with g.stage() as st:
        w = SplitWeights(g, "win", st)
        small = g.sb("wsmall", [P, KD, 72], ctx=st)
        smallp = g.sb("wsmall_parts", [P, 2, KD, 72], F32R, ctx=st)
        qk = g.sb("fox_qk", [P, NT, 512], ctx=st)
        bf = g.sb("bforget", [8, 1], ctx=st)
        s_small = g.sem("wsmall_loaded")
        s_smallp = g.sem("wsmall_parts_ready")
        s_ps = g.sem("proj1_ready")
        s_act = g.sem("proj1_act_evacuated")
        s_dve = g.sem("proj1_dve_evacuated")
        s_st = g.sem("fox_qk_stored")
        n = len(slabs)

        def owner(s, t):
            return "act" if s >= 4 or t < 2 else "dve"

        def done(s, t):
            who = owner(s, t)
            count = sum(owner(a, b) == who for a in range(n) for b in range(NT) if (a, b) <= (s, t))
            return (s_act if who == "act" else s_dve), count

        def evacuate(copy, s, t):
            src = g.ps[:, (s % 2) * 4 + t, :]
            if s == 0:
                return copy(t1["lat"][:, t, :], src[:, 0:416])
            if s == 1:
                return nc.scalar.mul(qk[:, t, :], src, DH ** -0.5) if owner(s, t) == "act" else \
                    nc.vector.tensor_scalar(qk[:, t, :], src, DH ** -0.5, None, ALU.mult)
            if s == 2:
                return copy(qk[:, t, :], src)
            if s == 3:
                return copy(t1["v_fox"][:, t, :], src)
            c = (s - 4) * 512
            return nc.scalar.activation(t1["gates"][:, t, c:c + 512], src, ACT.Sigmoid)

        block = st.enter_context(nc.Block())

        @block.sync
        def _(sp):
            for s, (_, c, width) in enumerate(slabs):
                for half in range(2):
                    w.load(sp, w_in[:, 4 * half:4 * half + 4, c:c + width], 0, 2 * s + half, width)
                if s in (3, 4):
                    for eng_done in (done(s - 2, 1), done(s - 2, 3)):
                        sp.wait_ge(*eng_done)
                    dst = (t1["fq_dram"], t1["fk_dram"])[s - 3].rearrange("(t p) s -> p t s", p=P)
                    sp.dma_start(dst, qk[:]).then_inc(s_st, 16)
            sp.wait_ge(s_st, 32)

        @block.gpsimd
        def _(pool):
            pool.dma_start(small[:, :, 0:8], w_in[:, :, C_FL:C_FL + 8]).then_inc(s_small, 16)
            pool.dma_start(small[:, :, 8:40], w_in[:, :, C_KR:C_KR + 32]).then_inc(s_small, 16)
            pool.dma_start(small[:, :, 40:56], w_in[:, :, C_KR + 16:C_KR + 32]).then_inc(s_small, 16)
            pool.dma_start(small[:, :, 56:72], w_in[:, :, C_KR:C_KR + 16]).then_inc(s_small, 16)
            pool.dma_start(bf[:], io["b_forget"].rearrange("a h -> h a"), allow_slow_non_contiguous=True).then_inc(s_small, 16)

        @block.tensor
        def _(pe):
            for s, (kind, _, width) in enumerate(slabs):
                for half in range(2):
                    q = 2 * s + half
                    w.ready(pe, 0, q)
                    for t in range(NT):
                        if s >= 2 and half == 0:
                            pe.wait_ge(*done(s - 2, t))
                        for j in range(4):
                            k = 4 * half + j
                            if kind == "rows":
                                left, right = parts_of(hT, k, t * P, t * P + P), w.at(q, j, 0, width)
                            else:
                                left, right = w.at(q, j, t * P, t * P + P), parts_of(hT, k)
                            mm = split_product(nc, g.ps[:, (s % 2) * 4 + t, 0:width], left, right, k == 0, k == KD - 1)
                        mm.then_inc(s_ps, 1)
            pe.wait_ge(s_smallp, 2)
            for j, (c, m) in enumerate([(0, 8), (8, 32), (40, 32)]):
                pe.wait_ge(*done(n - 2, j))
                for k in range(KD):
                    mm = split_product(nc, g.ps[0:m, j, :], parts_of(smallp, k, c, c + m), parts_of(hT, k), k == 0, k == KD - 1)
                mm.then_inc(s_ps, 1)

        @block.scalar
        def _(act):
            for half in range(2):
                w.high(act, 0, half, s_ps, 4, slabs[0][2])
            for s in range(n):
                for half in range(2):
                    if s + 1 < n:
                        w.high(act, 0, 2 * s + 2 + half, s_ps, 4, slabs[s + 1][2])
                for t in range(NT):
                    if owner(s, t) == "act":
                        act.wait_ge(s_ps, 8 * s + 4 + t + 1)
                        if s == 2 and t == 0:
                            act.wait_ge(s_st, 16)
                        evacuate(nc.scalar.copy, s, t).then_inc(s_act, 1)

        @block.vector
        def _(dve):
            for half in range(2):
                w.low(dve, 0, half, s_ps, 4, slabs[0][2])
            dve.wait_ge(s_small, 80)
            nc.vector.tensor_copy(smallp[:, 0], small[:]).then_inc(s_smallp, 1)
            dve.wait_ge(s_smallp, 1)
            low_part(nc, smallp[:, 1], small[:], smallp[:, 0]).then_inc(s_smallp, 1)
            for s in range(n):
                for half in range(2):
                    if s + 1 < n:
                        w.low(dve, 0, 2 * s + 2 + half, s_ps, 4, slabs[s + 1][2])
                for t in range(2, NT):
                    if owner(s, t) == "dve":
                        dve.wait_ge(s_ps, 8 * s + 4 + t + 1)
                        if s == 2 and t == 2:
                            dve.wait_ge(s_st, 16)
                        evacuate(nc.vector.tensor_copy, s, t).then_inc(s_dve, 1)
            dve.wait_ge(s_ps, 8 * n + 3)
            nc.vector.tensor_scalar(t1["fl"][:], g.ps[0:8, 0, :], bf[:, 0:1], None, ALU.add)
            nc.vector.tensor_copy(t1["kr"][:, 0, :], g.ps[0:32, 1, :])
            nc.vector.tensor_copy(t1["kr"][:, 1, :], g.ps[0:32, 2, :])


def latent_stage(g, io, t1):
    nc = g.nc
    lat, rope = t1["lat"], t1["rope"]
    with g.stage() as st:
        junk = g.sb("lat_junk", [P, NT, 384], ctx=st)
        gains = g.sb("lat_gain", [P, 384], ctx=st)
        stat = g.sb("lat_stat", [P, 3, 2 * NT], ctx=st)
        posi = g.sb("posi", [P, S], I32, ctx=st)
        pos = g.sb("posf", [P, S], ctx=st)
        ang = g.sb("ang", [P, 4, S], ctx=st)
        fg = g.sb("forget", [8, 6, S], ctx=st)
        kpe = g.sb("kpe", [32, 2, S], ctx=st)
        s_ld = g.sem("latent_loads")
        s_sq = g.sem("latent_squares")
        s_ms = g.sem("latent_mean_square")
        s_n = g.sem("latent_normed")
        s_t = g.sem("latent_turned")
        s_ang = g.sem("angles_ready")
        s_sin = g.sem("sines_ready")
        s_fa = g.sem("forget_abs_ready")
        s_fl = g.sem("forget_log_ready")
        s_acts = g.sem("latent_act_steps")
        s_k = g.sem("kpe_and_forget_ready")
        s_st = g.sem("kpe_and_forget_stored")
        s_dve = g.sem("latent_dve_steps")
        TWO_PI = 6.283185307179586
        C1 = 6.28125
        C2 = 0.0019350051879882812
        C3 = TWO_PI - C1 - C2
        MAGIC = 12582912.0
        block = st.enter_context(nc.Block())

        @block.sync
        def _(sp):
            sp.dma_start(posi[:], bcast_rows(io["positions"], S)).then_inc(s_ld, 16)
            sp.dma_start(gains[:, 0:256], bcast_rows(io["g_q_lat"], 256)).then_inc(s_ld, 16)
            sp.dma_start(gains[:, 256:384], bcast_rows(io["g_kv_lat"], 128)).then_inc(s_ld, 16)
            sp.wait_ge(s_k, 1)
            sp.dma_start(t1["kpe_dram"], kpe[:, 0, :]).then_inc(s_st, 16)
            sp.wait_ge(s_k, 2)
            sp.dma_start(t1["fqa_dram"][:, 0, :], fg[:, 4, :]).then_inc(s_st, 16)
            sp.dma_start(t1["fqa_dram"][:, 1, :], fg[:, 3, :]).then_inc(s_st, 16)
            sp.dma_start(t1["fka_dram"][:, 0, :], fg[:, 3, :]).then_inc(s_st, 16)
            sp.dma_start(t1["fka_dram"][:, 1, :], fg[:, 5, :]).then_inc(s_st, 16)
            sp.wait_ge(s_st, 80)

        @block.scalar
        def _(act):
            for t in range(NT):
                nc.scalar.activation(junk[:, t, 0:256], lat[:, t, 0:256], ACT.Square, accum_out=stat[:, 0, t:t + 1])
                nc.scalar.activation(junk[:, t, 256:384], lat[:, t, 256:384], ACT.Square,
                                     accum_out=stat[:, 0, NT + t:NT + t + 1]).then_inc(s_sq, 1)
            act.wait_ge(s_ms, 1)
            nc.scalar.activation(stat[:, 2, :], stat[:, 1, :], ACT.Sqrt).then_inc(s_sq, 1)
            act.wait_ge(s_fa, 1)
            nc.scalar.activation(fg[:, 1, :], fg[:, 0, :], ACT.Exp).then_inc(s_acts, 1)
            act.wait_ge(s_acts, 1)
            nc.scalar.activation(fg[:, 2, :], fg[:, 1, :], ACT.Ln, bias=1.0).then_inc(s_fl, 1)
            act.wait_ge(s_ang, 1)
            nc.scalar.activation(rope[:, 0, :], ang[:, 0, :], ACT.Sin).then_inc(s_sin, 1)
            nc.scalar.activation(rope[:, 1, :], ang[:, 1, :], ACT.Sin).then_inc(s_sin, 1)

        @block.vector
        def _(dve):
            link = Chain(dve, s_dve)
            dve.wait_ge(s_ld, 48)
            dve.wait_ge(s_sq, NT)
            link(nc.vector.tensor_scalar(stat[:, 1, 0:NT], stat[:, 0, 0:NT], 1.0 / Q_LORA, EPS, ALU.mult, ALU.add))
            nc.vector.tensor_scalar(stat[:, 1, NT:2 * NT], stat[:, 0, NT:2 * NT], 1.0 / KV_LORA, EPS,
                                    ALU.mult, ALU.add).then_inc(s_ms, 1)
            nc.vector.scalar_tensor_tensor(fg[:, 0, :], t1["fl"][:], -1.0, t1["fl"][:], ALU.mult, ALU.min).then_inc(s_fa, 1)
            link(nc.vector.tensor_copy(pos[:], posi[:]))
            link(nc.vector.tensor_scalar(ang[:, 2, :], pos[:], g.ropec[:, 0:1], None, ALU.mult))
            for row, turn in ((0, 0.25), (1, 0.0)):
                link(nc.vector.tensor_scalar(ang[:, 3, :], ang[:, 2, :], 1.0 / TWO_PI, turn, ALU.mult, ALU.add))
                link(nc.vector.tensor_scalar(ang[:, 3, :], ang[:, 3, :], MAGIC, None, ALU.add))
                link(nc.vector.tensor_scalar(ang[:, 3, :], ang[:, 3, :], -MAGIC, None, ALU.add))
                link(nc.vector.scalar_tensor_tensor(ang[:, row, :], ang[:, 3, :], -C1, ang[:, 2, :], ALU.mult, ALU.add))
                link(nc.vector.scalar_tensor_tensor(ang[:, row, :], ang[:, 3, :], -C2, ang[:, row, :], ALU.mult, ALU.add))
                link(nc.vector.scalar_tensor_tensor(ang[:, row, :], ang[:, 3, :], -C3, ang[:, row, :], ALU.mult, ALU.add))
                if turn:
                    link(nc.vector.tensor_scalar(ang[:, row, :], ang[:, row, :], TWO_PI / 4, None, ALU.add))
                last = nc.vector.tensor_scalar(ang[:, row, :], ang[:, row, :], 3.1415925, -3.1415925, ALU.min, ALU.max)
            last.then_inc(s_ang, 1)
            dve.wait_ge(s_fl, 1)
            link(nc.vector.scalar_tensor_tensor(fg[:, 0, :], t1["fl"][:], 0.0, fg[:, 2, :], ALU.min, ALU.subtract))
            link(nc.vector.memset(fg[:, 3, :], 1.0))
            link(nc.vector.tensor_tensor_scan(fg[:, 4, :], fg[:, 3, :], fg[:, 0, :], 0.0, ALU.mult, ALU.add))
            link(nc.vector.tensor_scalar(fg[:, 5, :], fg[:, 4, :], -1.0, None, ALU.mult))
            dve.wait_ge(s_sq, NT + 1)
            link(nc.vector.reciprocal(stat[:, 1, :], stat[:, 2, :]))
            for t in range(NT):
                nc.vector.scalar_tensor_tensor(lat[:, t, 0:256], lat[:, t, 0:256], stat[:, 1, t:t + 1],
                                               gains[:, 0:256], ALU.mult, ALU.mult)
                nc.vector.scalar_tensor_tensor(lat[:, t, 256:384], lat[:, t, 256:384], stat[:, 1, NT + t:NT + t + 1],
                                               gains[:, 256:384], ALU.mult, ALU.mult).then_inc(s_n, 1)
            dve.wait_ge(s_sin, 2)
            link(nc.vector.tensor_scalar(rope[:, 1, :], rope[:, 1, :], g.ropec[:, 1:2], None, ALU.mult))
            link(nc.vector.tensor_tensor(kpe[:, 0, :], t1["kr"][:, 0, :], rope[0:32, 0, :], ALU.mult))
            link(nc.vector.tensor_tensor(kpe[:, 1, :], t1["kr"][:, 1, :], rope[0:32, 1, :], ALU.mult))
            nc.vector.tensor_tensor(kpe[:, 0, :], kpe[:, 0, :], kpe[:, 1, :], ALU.add).then_inc(s_k, 2)
            for k in range(3):
                dve.wait_ge(s_t, k + 1)
                nc.vector.tensor_copy(t1["latT"][:, k, :], g.ps[:, k, :])

        @block.tensor
        def _(pe):
            pe.wait_ge(s_n, NT)
            for k in range(3):
                for t in range(NT):
                    tr = nc.tensor.transpose(g.ps[:, k, t * P:t * P + P], lat[:, t, k * P:k * P + P], g.ident[:])
                tr.then_inc(s_t, 1)


def up_stage(g, io, t1):
    nc = g.nc
    MLA_SCALE = 96 ** -0.5
    with g.stage() as st:
        wqn = g.sb("wqn", [P, 2, H1, NOPE], ctx=st)
        wqp = g.sb("wqp", [P, 2, H1, ROPE], ctx=st)
        wqs = g.sb("wqs", [P, 2, H1, ROPE], ctx=st)
        wk = g.sb("wk", [P, H1, NOPE], ctx=st)
        wv = g.sb("wv", [P, H1, DH], ctx=st)
        qn = g.sb("qn", [P, 4, S], ctx=st)
        kn = g.sb("kn", [P, 4, S], ctx=st)
        qp = g.sb("qp", [P, 2, 2, S], ctx=st)
        s_w = g.sem("up_weights_loaded")
        s_ps = g.sem("up_ready")
        s_act = g.sem("up_act_evacuated")
        s_dve = g.sem("up_dve_evacuated")
        s_rot = g.sem("rotated")
        s_dst = g.sem("up_dve_steps")
        s_st = g.sem("up_stored")
        wq = io["w_q_up"][0].rearrange("(k p) (h c) -> p k h c", p=P, c=96)
        wkv = io["w_kv_up"][0].rearrange("p (h c) -> p h c", c=128)
        latT = t1["latT"]
        block = st.enter_context(nc.Block())

        @block.sync
        def _(sp):
            sp.dma_start(wk[:], wkv[:, :, 0:64]).then_inc(s_w, 16)
            sp.dma_start(wv[:], wkv[:, :, 64:128]).then_inc(s_w, 16)
            for k in range(2):
                sp.dma_start(wqn[:, k], wq[:, k, :, 0:64]).then_inc(s_w, 16)
                sp.dma_start(wqp[:, k], wq[:, k, :, 64:96]).then_inc(s_w, 16)
                sp.dma_start(wqs[:, k, :, 0:16], wq[:, k, :, 80:96]).then_inc(s_w, 16)
                sp.dma_start(wqs[:, k, :, 16:32], wq[:, k, :, 64:80]).then_inc(s_w, 16)
            sp.wait_ge(s_act, 4)
            sp.dma_start(t1["qn_dram"].rearrange("(t p) s -> p t s", p=P), qn[:]).then_inc(s_st, 16)
            sp.wait_ge(s_act, 8)
            sp.dma_start(t1["kn_dram"].rearrange("(t p) s -> p t s", p=P), kn[:]).then_inc(s_st, 16)
            sp.wait_ge(s_rot, 2)
            sp.dma_start(t1["qp_dram"].rearrange("(t p) s -> p t s", p=P), qp[:, :, 0, :]).then_inc(s_st, 16)
            sp.wait_ge(s_st, 48)

        @block.tensor
        def _(pe):
            pe.wait_ge(s_w, 160)
            for m in range(4):
                for k in range(2):
                    mm = nc.tensor.matmul(g.ps[:, m, :], wqn[:, k, 2 * m:2 * m + 2, :], latT[:, k, :],
                                          start=k == 0, stop=k == 1)
                mm.then_inc(s_ps, 1)
            for m in range(4):
                wt = (wqp, wqs)[m % 2]
                h = 4 * (m // 2)
                for k in range(2):
                    mm = nc.tensor.matmul(g.ps[:, 4 + m, :], wt[:, k, h:h + 4, :], latT[:, k, :],
                                          start=k == 0, stop=k == 1)
                mm.then_inc(s_ps, 1)
            for m in range(4):
                pe.wait_ge(s_act, m + 1)
                nc.tensor.matmul(g.ps[:, m, :], wk[:, 2 * m:2 * m + 2, :], latT[:, 2, :],
                                 start=True, stop=True).then_inc(s_ps, 1)
            for t in range(NT):
                pe.wait_ge(s_rot, t // 2 + 1)
                nc.tensor.matmul(g.ps[:, 4 + t, :], latT[:, 2, t * P:t * P + P], wv[:],
                                 start=True, stop=True).then_inc(s_ps, 1)

        @block.scalar
        def _(act):
            for m in range(4):
                act.wait_ge(s_ps, m + 1)
                nc.scalar.mul(qn[:, m, :], g.ps[:, m, :], MLA_SCALE).then_inc(s_act, 1)
            for m in range(4):
                act.wait_ge(s_ps, 9 + m)
                nc.scalar.copy(kn[:, m, :], g.ps[:, m, :]).then_inc(s_act, 1)

        @block.vector
        def _(dve):
            link = Chain(dve, s_dst)
            for m in range(2):
                dve.wait_ge(s_ps, 4 + 2 * m + 2)
                link(nc.vector.scalar_tensor_tensor(qp[:, m, 0, :], g.ps[:, 4 + 2 * m, :], MLA_SCALE,
                                                    t1["rope"][:, 0, :], ALU.mult, ALU.mult))
                link(nc.vector.scalar_tensor_tensor(qp[:, m, 1, :], g.ps[:, 5 + 2 * m, :], MLA_SCALE,
                                                    t1["rope"][:, 1, :], ALU.mult, ALU.mult))
                nc.vector.tensor_tensor(qp[:, m, 0, :], qp[:, m, 0, :], qp[:, m, 1, :], ALU.add).then_inc(s_rot, 1)
            for t in range(NT):
                dve.wait_ge(s_ps, 13 + t)
                nc.vector.tensor_copy(t1["v_mla"][:, t, :], g.ps[:, 4 + t, :])


def at_least(eng, sem, base, value):
    if not isinstance(base, int) or base + value > 0:
        eng.wait_ge(sem, base + value)


def turns(eng, heads, body):
    n = heads // 2
    body(0, 0, False)
    if n > 1:
        with eng.Fori(1, n) as i:
            body(i, 8 * i, False)
    body(n, 8 * n, True)


def lagging(base, u, lag, drain):
    if (isinstance(base, int) and base == 0 and u < lag) or (drain and u >= lag):
        return None
    return (u - lag) % 8, u < lag


def fetch_heads(g, eng, heads, q, kk, q_parts, k_parts, s_qk, s_s):
    def fetch(head, j):
        for dst, parts in ((q, q_parts), (kk, k_parts)):
            r = 0
            for src, n, row in parts:
                eng.dma_start(dst[r:r + n, j, :], src[bass.ds(row(head), n), :]).then_inc(s_qk[j], 16)
                r += n

    fetch(0, 0)
    fetch(1, 1)
    with eng.Fori(1, heads // 2) as i:
        for j in range(2):
            eng.wait_ge(s_s, 8 * i - 4 + 4 * j)
            fetch(2 * i + j, j)


def attention_stage(g, name, heads, q_parts, k_parts, v, out, mask, stats=None):
    nc = g.nc
    K = sum(n for _, n, _ in q_parts)
    LT, LV = 2, 4
    with g.stage() as st:
        q = g.sb(name + "_q", [K, 2, S], ctx=st)
        kk = g.sb(name + "_k", [K, 2, S], ctx=st)
        p = g.sb(name + "_p", [P, 4, S], ctx=st)
        pt = g.sb(name + "_pt", [P, 4, NT, P], ctx=st)
        stats = g.sb(name + "_stats", [P, 2, 4 * heads], ctx=st) if stats is None else stats
        rl = g.sb(name + "_rl", [P, 8], ctx=st)
        s_qk = [g.sem(f"{name}_qk_loaded{i}") for i in range(2)]
        s_s = g.sem(name + "_scores_ready")
        s_m = g.sem(name + "_max_ready")
        s_p = g.sem(name + "_probs_ready")
        s_t = g.sem(name + "_turned")
        s_pt = g.sem(name + "_turned_copied")
        s_o = g.sem(name + "_values_ready")
        s_rl = g.sem(name + "_reciprocal_ready")
        s_od = g.sem(name + "_out_done")
        loads = 16 * (len(q_parts) + len(k_parts))
        block = st.enter_context(nc.Block())

        @block.sync
        def _(sp):
            fetch_heads(g, sp, heads, q, kk, q_parts, k_parts, s_qk, s_s)

        @block.tensor
        def _(pe):
            def body(i, base, drain):
                for u in range(8):
                    j, t = u // 4, u % 4
                    n = (t + 1) * P
                    if not drain:
                        if t == 0:
                            pe.wait_ge(s_qk[j], loads * i + loads)
                        at_least(pe, s_m, base, u - 3)
                        at_least(pe, s_p, base, u - 3)
                        mk, first = mask(i, t)
                        nc.tensor.matmul(g.ps[:, u % 4, 0:n], q[:, j, t * P:t * P + P], kk[:, j, 0:n],
                                         start=True, stop=False)
                        nc.tensor.matmul(g.ps[:, u % 4, first:n], g.identb[:], mk,
                                         start=False, stop=True).then_inc(s_s, 1)
                    if (at := lagging(base, u, LT, drain)) is not None:
                        a = at[0]
                        at_least(pe, s_p, base, u - LT + 1)
                        at_least(pe, s_pt, base, u - LT - 1)
                        for b in range(a % 4 + 1):
                            tr = nc.tensor.transpose(g.ps[:, 4 + a % 2, b * P:b * P + P], p[:, a % 4, b * P:b * P + P],
                                                     g.ident[:])
                        tr.then_inc(s_t, 1)
                    if (at := lagging(base, u, LV, drain)) is not None:
                        a, head = at[0], 2 * i + at[0] // 4 - 2 * at[1]
                        at_least(pe, s_pt, base, u - LV + 1)
                        at_least(pe, s_od, base, u - LV - 1)
                        for b in range(a % 4 + 1):
                            mm = nc.tensor.matmul(g.ps[:, 6 + a % 2, 0:DH], pt[:, a % 4, b, :], v(b, head),
                                                  start=b == 0, stop=b == a % 4)
                        mm.then_inc(s_o, 1)
            turns(pe, heads, body)

        @block.scalar
        def _(act):
            def body(i, base, drain):
                for u in range(8):
                    n = (u % 4 + 1) * P
                    if not drain:
                        at_least(act, s_t, base, u - 3)
                        at_least(act, s_m, base, u + 1)
                        col = bass.ds(8 * i + u, 1)
                        nc.scalar.activation(p[:, u % 4, 0:n], g.ps[:, u % 4, 0:n], ACT.Exp, bias=stats[:, 0, col],
                                             accum_out=stats[:, 1, col]).then_inc(s_p, 1)
                    if (at := lagging(base, u, LT, drain)) is not None:
                        a = at[0]
                        at_least(act, s_t, base, u - LT + 1)
                        at_least(act, s_o, base, u - LT - 3)
                        nc.scalar.copy(pt[:, a % 4, 0:a % 4 + 1, :],
                                       g.ps[:, 4 + a % 2, 0:(a % 4 + 1) * P].rearrange("p (b s) -> p b s", s=P)
                                       ).then_inc(s_pt, 1)
            turns(act, heads, body)

        @block.vector
        def _(dve):
            def body(i, base, drain):
                for u in range(8):
                    if not drain:
                        at_least(dve, s_s, base, u + 1)
                        nc.vector.tensor_reduce(stats[:, 0, bass.ds(8 * i + u, 1)], g.ps[:, u % 4, 0:(u % 4 + 1) * P],
                                                AX.X, ALU.max, negate=True).then_inc(s_m, 1)
                    if (at := lagging(base, u, LV, drain)) is not None:
                        a, head = at[0], 2 * i + at[0] // 4 - 2 * at[1]
                        at_least(dve, s_p, base, u - LV + 1)
                        nc.vector.reciprocal(rl[:, a:a + 1], stats[:, 1, bass.ds(8 * i + u - LV, 1)]).then_inc(s_rl, 1)
                        at_least(dve, s_rl, base, u - LV + 1)
                        at_least(dve, s_o, base, u - LV + 1)
                        nc.vector.tensor_scalar(out(a % 4, head), g.ps[:, 6 + a % 2, 0:DH], rl[:, a:a + 1], None,
                                                ALU.mult).then_inc(s_od, 1)
            turns(dve, heads, body)


def merge_stage(g, io, oT, gates, merged):
    nc = g.nc
    with g.stage() as st:
        w = SplitWeights(g, "wo", st)
        part = g.sb("merge_part", [P, 2, 2, 512], ctx=st)
        s_ps = g.sem("merge_ready")
        s_ev = g.sem("merge_evacuated")
        s_dve = g.sem("merge_dve_steps")
        block = st.enter_context(nc.Block())

        @block.sync
        def _(sp):
            for q in range(4):
                n, j = q // 2, q % 2
                src = io[("w_o_mla", "w_o_fox")[j]][0].rearrange("(k p) n -> p k n", p=P)
                w.load(sp, src[:, :, n * 512:n * 512 + 512], 0, q)

        @block.tensor
        def _(pe):
            for q in range(4):
                n, j = q // 2, q % 2
                w.ready(pe, 0, q)
                for t in range(NT):
                    if n:
                        pe.wait_ge(s_ev, t + 1)
                    for k in range(4):
                        mm = split_product(nc, g.ps[:, 4 * j + t, :], parts_of(oT, 4 * j + k, t * P, t * P + P),
                                           w.at(q, k, 0, 512), k == 0, k == 3)
                    mm.then_inc(s_ps, 1)

        @block.scalar
        def _(act):
            for q in range(4):
                w.high(act, 0, q, s_ps, NT)

        @block.vector
        def _(dve):
            link = Chain(dve, s_dve)
            for q in range(3):
                w.low(dve, 0, q, s_ps, NT)
            for n in range(2):
                for t in range(NT):
                    dve.wait_ge(s_ps, NT * (2 * n + 1) + t + 1)
                    for j in range(2):
                        col = j * D + n * 512
                        ins = nc.vector.tensor_tensor(part[:, t % 2, j, :], g.ps[:, 4 * j + t, :],
                                                      gates[:, t, col:col + 512], ALU.mult)
                        if j == 0:
                            link(ins)
                    link(ins)
                    nc.vector.tensor_tensor(merged[:, t, n * 512:n * 512 + 512], part[:, t % 2, 0, :],
                                            part[:, t % 2, 1, :], ALU.add).then_inc(s_ev, 1)
                if n == 0:
                    w.low(dve, 0, 3, s_ps, NT)


def add_product_stage(g, name, colsT, w_dram, kt, gate=None):
    nc = g.nc
    kh = kt // 2
    w_d = w_dram.rearrange("(k p) n -> p k n", p=P)
    with g.stage() as st:
        w = SplitWeights(g, name + "_w", st, kh)
        part = g.sb(name + "_part", [P, 4, 512], ctx=st)
        s_ps = g.sem(name + "_ready")
        s_dve = g.sem(name + "_dve_steps")
        block = st.enter_context(nc.Block())

        @block.sync
        def _(sp):
            for q in range(4):
                n, c = q // 2, q % 2
                w.load(sp, w_d[:, kh * c:kh * c + kh, n * 512:n * 512 + 512], 0, q)

        @block.tensor
        def _(pe):
            for q in range(4):
                n, c = q // 2, q % 2
                w.ready(pe, 0, q)
                for t in range(NT):
                    for j in range(kh):
                        k = kh * c + j
                        mm = split_product(nc, g.ps[:, 4 * n + t, :], parts_of(colsT, k, t * P, t * P + P),
                                           w.at(q, j, 0, 512), k == 0, k == kt - 1)
                    mm.then_inc(s_ps, 1)

        @block.scalar
        def _(act):
            for q in range(4):
                w.high(act, 0, q, s_ps, NT)

        @block.vector
        def _(dve):
            link = Chain(dve, s_dve)
            for q in range(4):
                w.low(dve, 0, q, s_ps, NT)
            for n in range(2):
                for t in range(NT):
                    xs = g.x[:, t, n * 512:n * 512 + 512]
                    dve.wait_ge(s_ps, NT * (2 * n + 1) + t + 1)
                    if gate is None:
                        nc.vector.tensor_tensor(xs, g.ps[:, 4 * n + t, :], xs, ALU.add)
                    else:
                        link(nc.vector.tensor_tensor(part[:, t, :], g.ps[:, 4 * n + t, :],
                                                     gate[:, n * 512:n * 512 + 512], ALU.mult))
                        nc.vector.tensor_tensor(xs, part[:, t, :], xs, ALU.add)


def dump(g, dst, src, nm):
    nc = g.nc
    with g.stage() as st:
        s_out = g.sem(nm)
        block = st.enter_context(nc.Block())

        @block.sync
        def _(sp):
            sp.dma_start(dst, src).then_inc(s_out, 16)
            sp.wait_ge(s_out, 16)


def block1_mixer(g, io, dbg):
    nc = g.nc
    with ExitStack() as a:
        fq, fk = g.dram("fq_T", [HW, S]), g.dram("fk_T", [HW, S])
        fqa, fka = g.dram("fq_extra", [H1, 2, S]), g.dram("fk_extra", [H1, 2, S])
        qn, kn, qp, kpe = (g.dram(n, [r, S]) for n, r in (("qn_T", HW), ("kn_T", HW), ("qp_T", H1 * ROPE), ("kpe_T", ROPE)))
        t1 = {"fq_dram": fq, "fk_dram": fk, "fqa_dram": fqa, "fka_dram": fka, "qn_dram": qn, "kn_dram": kn,
              "qp_dram": qp, "kpe_dram": kpe}
        gates = t1["gates"] = g.sb("gates", [P, NT, 2 * D], ctx=a)
        with ExitStack() as b:
            t1["v_fox"] = g.sb("v_fox", [P, NT, HW], ctx=b)
            t1["v_mla"] = g.sb("v_mla", [P, NT, HW], ctx=b)
            with ExitStack() as c:
                t1["lat"] = g.sb("lat", [P, NT, 416], ctx=c)
                t1["fl"] = g.sb("fl", [8, S], ctx=c)
                t1["kr"] = g.sb("kr", [32, 2, S], ctx=c)
                with ExitStack() as d:
                    hT = g.sb("h1T", [P, 2, KD, S], F32R, ctx=d)
                    norm_stage(g, "mix1", io["g_mix_norm"], hT, scale=g.mod[:, D:2 * D], shift=g.mod[:, 0:D])
                    project1_stage(g, io, hT, t1)
                t1["rope"] = g.sb("rope", [P, 2, S], ctx=c)
                t1["latT"] = g.sb("latT", [P, 3, S], ctx=c)
                latent_stage(g, io, t1)
                up_stage(g, io, t1)
            o = g.sb("o1", [P, NT, 2 * HW], ctx=b)

            def causal(i, t):
                return g.mask[:, 0, 384:512], t * P
            attention_stage(g, "mla", H1, [(qn, NOPE, lambda h: h * NOPE), (qp, ROPE, lambda h: h * ROPE)],
                            [(kn, NOPE, lambda h: h * NOPE), (kpe, ROPE, lambda h: h * 0)],
                            lambda b, h: t1["v_mla"][:, b, bass.ds(h * DH, DH)],
                            lambda t, h: o[:, t, bass.ds(h * DH, DH)], causal)
            fqa2, fka2 = fqa.rearrange("h r s -> (h r) s"), fka.rearrange("h r s -> (h r) s")
            attention_stage(g, "fox", H1, [(fq, DH, lambda h: h * DH), (fqa2, 2, lambda h: h * 2)],
                            [(fk, DH, lambda h: h * DH), (fka2, 2, lambda h: h * 2)],
                            lambda b, h: t1["v_fox"][:, b, bass.ds(h * DH, DH)],
                            lambda t, h: o[:, t, bass.ds(h * DH + HW, DH)], causal)
            if "o1" in dbg:
                dump(g, dbg["o1"].rearrange("(t p) d -> p t d", p=P), o[:], "dump_o1")
            oT = g.sb("o1T", [P, 2, KD, S], F32R, ctx=b)
            turn_parts_stage(g, "o1turn", o, 2 * HW, oT)
            merged = o
            merge_stage(g, io, oT, gates, merged)
            turn_parts_stage(g, "mergeturn", merged, D, oT)
            add_product_stage(g, "out1", oT, io["w_out"][0], KD, gate=g.mod[:, 2 * D:3 * D])


def shared_stage(g, io, hT, acc):
    nc = g.nc
    with g.stage() as st:
        w = g.sb("sh_w", [P, 3, 2 * D], ctx=st)
        wp = g.sb("sh_w_parts", [P, 3, 2, 2 * D], F32R, ctx=st)
        sg = g.sb("sh_sig", [P, 2, S], ctx=st)
        hid = g.sb("sh_hid", [P, 2, S], ctx=st)
        hidp = g.sb("sh_hid_parts", [P, 2, 2, S], F32R, ctx=st)
        s_w = [g.sem(f"shared_weights_loaded{i}") for i in range(3)]
        s_hi = g.sem("shared_high_ready")
        s_lo = g.sem("shared_low_ready")
        s_ps = g.sem("shared_ready")
        s_sg = g.sem("shared_sigmoid")
        s_h = g.sem("shared_hidden_ready")
        s_dve = g.sem("shared_dve_steps")
        block = st.enter_context(nc.Block())

        @block.sync
        def _(sp):
            for i, key in enumerate(("w_sh_gate", "w_sh_up", "w_sh_down")):
                sp.dma_start(w[:, i, :].rearrange("p (k n) -> p k n", k=(KD, KD, 2)[i]),
                             io[key][0].rearrange("(k p) n -> p k n", p=P)).then_inc(s_w[i], 16)

        @block.tensor
        def _(pe):
            for m in range(4):
                pe.wait_ge(s_hi, m // 2 + 1)
                pe.wait_ge(s_lo, m // 2 + 1)
                for k in range(KD):
                    c = k * F + (m % 2) * P
                    mm = split_product(nc, g.ps[:, m, :], [wp[:, m // 2, a, c:c + P] for a in range(2)], parts_of(hT, k),
                                       k == 0, k == KD - 1)
                mm.then_inc(s_ps, 1)
            pe.wait_ge(s_hi, 3)
            pe.wait_ge(s_lo, 3)
            pe.wait_ge(s_h, 2)
            for c in range(8):
                t, n = c // 2, c % 2
                for k in range(2):
                    col = k * D + n * 512
                    mm = split_product(nc, g.ps[:, c, :], parts_of(hidp, k, t * P, t * P + P),
                                       [wp[:, 2, a, col:col + 512] for a in range(2)], k == 0, k == 1)
                mm.then_inc(s_ps, 1)

        @block.scalar
        def _(act):
            for i in range(3):
                act.wait_ge(s_w[i], 16)
                nc.scalar.copy(wp[:, i, 0, :], w[:, i, :]).then_inc(s_hi, 1)
            for m in range(2):
                act.wait_ge(s_ps, m + 1)
                nc.scalar.activation(sg[:, m, :], g.ps[:, m, :], ACT.Sigmoid).then_inc(s_sg, 1)
            for c in range(0, 8, 2):
                act.wait_ge(s_ps, 5 + c)
                nc.scalar.copy(acc[:, c // 2, 0:512], g.ps[:, c, :])

        @block.vector
        def _(dve):
            link = Chain(dve, s_dve)
            for i in range(3):
                dve.wait_ge(s_hi, i + 1)
                low_part(nc, wp[:, i, 1, :], w[:, i, :], wp[:, i, 0, :]).then_inc(s_lo, 1)
            for m in range(2):
                dve.wait_ge(s_sg, m + 1)
                link(nc.vector.tensor_tensor(sg[:, m, :], g.ps[:, m, :], sg[:, m, :], ALU.mult))
                dve.wait_ge(s_ps, m + 3)
                link(nc.vector.tensor_tensor(hid[:, m, :], g.ps[:, 2 + m, :], sg[:, m, :], ALU.mult))
                link(nc.vector.tensor_copy(hidp[:, 0, m, :], hid[:, m, :]))
                low_part(nc, hidp[:, 1, m, :], hid[:, m, :], hidp[:, 0, m, :]).then_inc(s_h, 1)
            for c in range(1, 8, 2):
                dve.wait_ge(s_ps, 5 + c)
                nc.vector.tensor_copy(acc[:, c // 2, 512:1024], g.ps[:, c, :])


def route_stage(g, io, hT, r):
    nc = g.nc
    with g.stage() as st:
        w = g.sb("wrouter", [P, KD, E], ctx=st)
        wp = g.sb("wrouter_parts", [P, 2, KD, E], F32R, ctx=st)
        br = g.sb("brouter", [P, E], ctx=st)
        sc = g.sb("scores", [P, NT, E], ctx=st)
        ch = g.sb("choice", [P, NT, E], ctx=st)
        m8 = g.sb("top8", [P, NT, NG, 8], ctx=st)
        gs = g.sb("group_score", [P, NT, NG], ctx=st)
        gi = g.sb("group_index", [P, NT, 8], U32, ctx=st)
        gf = g.sb("group_index_f", [P, NT, 8], ctx=st)
        keep = g.sb("group_keep", [P, NT, NG], ctx=st)
        ei = g.sb("expert_index", [P, NT, 8], U32, ctx=st)
        ef = g.sb("expert_index_f", [P, NT, 8], ctx=st)
        oh = g.sb("onehot", [P, NT, TOPK, E], ctx=st)
        tmp = g.sb("route_tmp", [P, TOPK, E], ctx=st)
        A = g.sb("assigned", [P, NT, E], ctx=st)
        cnt = g.sb("counts", [P, 5, E], ctx=st)
        row = g.sb("expert_row", [P, NT, E], ctx=st)
        gsum = g.sb("gate_sum", [P, 2, NT], ctx=st)
        be = g.sb("block_expert", [P, E + 2], ctx=st)
        asg = g.sb("assignment_ids", [P, NT, TOPK], I32, ctx=st)
        lists = g.sb("row_lists", [P, BLOCKS + 4], I32, ctx=st)
        rb = g.sb("row_blocks", [BLOCKS + 4, P], I32, ctx=st)
        rbf = g.sb("row_blocks_f", [BLOCKS + 4, P], ctx=st)
        s_ld = g.sem("route_loads")
        s_wp = g.sem("wrouter_parts_ready")
        s_ps = g.sem("route_psum_ready")
        s_sc = g.sem("scores_ready")
        s_A = g.sem("assignments_ready")
        s_dve = g.sem("route_dve_steps")
        s_pad = g.sem("pad_rows_written")
        s_dest = g.sem("destinations_ready")
        s_scat = g.sem("rows_scattered")
        s_be = g.sem("block_experts_ready")
        s_bes = g.sem("block_experts_stored")
        s_rb = g.sem("row_blocks_loaded")
        s_rbf = g.sem("row_blocks_float")
        block = st.enter_context(nc.Block())
        NB = BLOCKS + 4

        @block.sync
        def _(sp):
            sp.dma_start(w[:], io["w_router"][0].rearrange("(k p) n -> p k n", p=P)).then_inc(s_ld, 16)
            sp.dma_start(br[:], bcast_rows(io["b_router"], E)).then_inc(s_ld, 16)
            sp.dma_start(asg[:], io["const_assignments"]).then_inc(s_ld, 16)
            sp.dma_start(r["row_asg"], io["const_pad_rows"]).then_inc(s_pad, 16)
            sp.wait_ge(s_be, 1)
            sp.dma_start(r["be_dram"], r["be_col"][0:NB, :]).then_inc(s_bes, 16)
            sp.dma_start(r["n_dram"], r["n_col"][0:1, :]).then_inc(s_bes, 16)
            sp.wait_ge(s_bes, 32)
            sp.dma_start(r["be_row"][:], r["be_dram"].rearrange("b a -> a b")).then_inc(s_bes, 16)
            sp.wait_ge(s_scat, 16 * NT * TOPK)
            sp.dma_start(rb[:], r["row_asg"].rearrange("(b p) a -> b (p a)", p=P)).then_inc(s_rb, 16)
            sp.wait_ge(s_bes, 48)

        @block.gpsimd
        def _(pool):
            pool.wait_ge(s_dest, 1)
            pool.wait_ge(s_ld, 48)
            pool.wait_ge(s_pad, 16)
            for t in range(NT):
                for k in range(TOPK):
                    pool.indirect_dma_start(
                        r["row_asg"], bass.IndirectOffsetOnAxis(ap=r["dest"][:, t, k:k + 1], axis=0),
                        asg[:, t, k:k + 1], None).then_inc(s_scat, 16)

        @block.tensor
        def _(pe):
            pe.wait_ge(s_wp, 2)
            for t in range(NT):
                for k in range(KD):
                    mm = split_product(nc, g.ps[:, t, 0:E], parts_of(hT, k, t * P, t * P + P), parts_of(wp, k, 0, E),
                                       k == 0, k == KD - 1)
                mm.then_inc(s_ps, 1)
            pe.wait_ge(s_A, 1)
            for t in range(NT):
                for b in range(t + 1):
                    mm = nc.tensor.matmul(g.ps[:, 4 + t, 0:E], g.tri[:] if b == t else g.ones[:], A[:, b, :],
                                          start=b == 0, stop=b == t)
                mm.then_inc(s_ps, 1)
            for b in range(NT):
                mm = nc.tensor.matmul(g.ps[:, 0, 0:E], g.ones[:], A[:, b, :], start=b == 0, stop=b == NT - 1)
            mm.then_inc(s_ps, 1)
            pe.wait_ge(s_rbf, 1)
            nc.tensor.transpose(g.ps[:, 1, 0:NB], rbf[:], g.ident[0:NB, 0:NB]).then_inc(s_ps, 1)

        @block.scalar
        def _(act):
            for t in range(NT):
                act.wait_ge(s_ps, t + 1)
                nc.scalar.activation(sc[:, t, :], g.ps[:, t, 0:E], ACT.Sigmoid).then_inc(s_sc, 1)

        @block.vector
        def _(dve):
            v = nc.vector
            link = Chain(dve, s_dve)
            dve.wait_ge(s_ld, 48)
            v.tensor_copy(wp[:, 0], w[:]).then_inc(s_wp, 1)
            dve.wait_ge(s_wp, 1)
            low_part(nc, wp[:, 1], w[:], wp[:, 0]).then_inc(s_wp, 1)
            for t in range(NT):
                dve.wait_ge(s_sc, t + 1)
                link(v.tensor_tensor(ch[:, t, :], sc[:, t, :], br[:], ALU.add))
                for n in range(NG):
                    ins = v.max(m8[:, t, n, :], ch[:, t, n * 8:n * 8 + 8])
                link(ins)
            link(v.tensor_tensor(gs[:], m8[:, :, :, 0], m8[:, :, :, 1], ALU.add))
            for t in range(NT):
                link(v.max(m8[:, t, 0, :], gs[:, t, :]))
                link(v.max_index(gi[:, t, :], m8[:, t, 0, :], gs[:, t, :]))
            link(v.tensor_copy(gf[:], gi[:]))
            link(v.memset(keep[:], 0.0))
            for t in range(NT):
                for k in range(TOPG):
                    link(v.scalar_tensor_tensor(keep[:, t, :], g.iota[:, 0:NG], gf[:, t, k:k + 1], keep[:, t, :],
                                                ALU.is_equal, ALU.add))
            for t in range(NT):
                kb = keep[:, t, :].unsqueeze(2).broadcast_to([P, NG, E // NG])
                c3 = ch[:, t, :].rearrange("p (a b) -> p a b", a=NG)
                link(v.tensor_tensor(c3, c3, kb, ALU.mult))
            link(v.tensor_scalar(keep[:], keep[:], -1.0, -NEG, ALU.add, ALU.mult))
            for t in range(NT):
                kb = keep[:, t, :].unsqueeze(2).broadcast_to([P, NG, E // NG])
                c3 = ch[:, t, :].rearrange("p (a b) -> p a b", a=NG)
                link(v.tensor_tensor(c3, c3, kb, ALU.add))
            for t in range(NT):
                link(v.max(m8[:, t, 0, :], ch[:, t, :]))
                link(v.max_index(ei[:, t, :], m8[:, t, 0, :], ch[:, t, :]))
            link(v.tensor_copy(ef[:], ei[:]))
            for t in range(NT):
                for k in range(TOPK):
                    ins = v.tensor_scalar(oh[:, t, k, :], g.iota[:, 0:E], ef[:, t, k:k + 1], None, ALU.is_equal)
                link(ins)
                ins = v.tensor_reduce(A[:, t, :], oh[:, t].rearrange("p k e -> p e k"), AX.X, ALU.add)
            link(ins)
            v.memset(cnt[:, 4, :], 1.0).then_inc(s_A, 1)
            for t in range(NT):
                link(v.tensor_tensor(tmp[:], oh[:, t], sc[:, t, :].unsqueeze(1).broadcast_to([P, TOPK, E]), ALU.mult))
                link(v.tensor_reduce(r["gate"][:, t, :], tmp[:], AX.X, ALU.add))
                link(v.tensor_reduce(gsum[:, 0, t:t + 1], r["gate"][:, t, :], AX.X, ALU.add))
                link(v.reciprocal(gsum[:, 1, t:t + 1], gsum[:, 0, t:t + 1]))
                link(v.tensor_scalar(r["gate"][:, t, :], r["gate"][:, t, :], gsum[:, 1, t:t + 1], ROUTED_SCALE,
                                     ALU.mult, ALU.mult))
            dve.wait_ge(s_ps, 2 * NT + 1)
            link(v.tensor_copy(cnt[:, 0, :], g.ps[:, 0, 0:E]))
            link(v.tensor_scalar(cnt[:, 1, :], cnt[:, 0, :], 0.0, None, ALU.is_gt))
            for j in range(1, NT):
                link(v.scalar_tensor_tensor(cnt[:, 1, :], cnt[:, 0, :], float(P * j), cnt[:, 1, :], ALU.is_gt, ALU.add))
            link(v.tensor_tensor_scan(cnt[:, 2, :], cnt[:, 4, :], cnt[:, 1, :], 0.0, ALU.mult, ALU.add))
            link(v.tensor_tensor(cnt[:, 3, :], cnt[:, 2, :], cnt[:, 1, :], ALU.subtract))
            link(v.tensor_scalar(cnt[:, 3, :], cnt[:, 3, :], float(P), None, ALU.mult))
            for t in range(NT):
                link(v.tensor_tensor(row[:, t, :], g.ps[:, 4 + t, 0:E], cnt[:, 3, :], ALU.add))
                link(v.tensor_tensor(tmp[:], oh[:, t], row[:, t, :].unsqueeze(1).broadcast_to([P, TOPK, E]), ALU.mult))
                link(v.tensor_reduce(gf[:, t, 0:TOPK], tmp[:], AX.X, ALU.add))
                link(v.tensor_copy(r["dest"][:, t, :], gf[:, t, 0:TOPK]))
            v.tensor_copy(r["n_col"][:], cnt[:, 2, E - 1:E]).then_inc(s_dest, 1)
            link(v.tensor_scalar(be[:, 0:E], cnt[:, 2, :], g.iota[:, P:P + 1], None, ALU.is_le))
            link(v.tensor_reduce(be[:, E:E + 1], be[:, 0:E], AX.X, ALU.add))
            link(v.tensor_scalar(be[:, E:E + 1], be[:, E:E + 1], float(E - 1), None, ALU.min))
            v.tensor_copy(r["be_col"][:], be[:, E:E + 1]).then_inc(s_be, 1)
            dve.wait_ge(s_rb, 16)
            v.tensor_copy(rbf[:], rb[:]).then_inc(s_rbf, 1)
            dve.wait_ge(s_ps, 2 * NT + 2)
            link(v.tensor_copy(lists[:], g.ps[:, 1, 0:NB]))
            v.tensor_copy(r["row_asg_cols"][:], lists[:])
            link(v.tensor_scalar(r["row_tok"][:], lists[:], S - 1, None, ALU.bitwise_and))
            link(v.tensor_scalar(lists[:], lists[:], float(TOPK * S), 4096.0, ALU.is_ge, ALU.mult))
            v.tensor_tensor(r["row_tok"][:], r["row_tok"][:], lists[:], ALU.add)


def expert_stage(g, io, r):
    nc = g.nc
    R = 4
    STEPS = BLOCKS + 4
    with g.stage() as st:
        wgu = g.sb("wgu", [P, R, KD, 2 * F], ctx=st)
        wd = g.sb("wd", [P, R, 2, D], ctx=st)
        idx = g.sb("row_index", [P, 2], I32, ctx=st)
        oidx = g.sb("out_index", [P, 2], U32, ctx=st)
        xg = g.sb("xg", [P, 2, D], ctx=st)
        xT = g.sb("xgT", [P, 2, KD, P], ctx=st)
        sg = g.sb("exp_sig", [P, F], ctx=st)
        h = g.sb("exp_h", [P, F], ctx=st)
        hT = g.sb("exp_hT", [P, 2, 2, P], ctx=st)
        y = g.sb("exp_y", [P, 2, D], ctx=st)
        s_w = [g.sem(f"expert_weights_loaded{i}") for i in range(R)]
        s_i = g.sem("row_index_ready")
        s_oi = g.sem("out_index_ready")
        s_seen = g.sem("index_seen")
        s_zero = g.sem("row_buffers_zeroed")
        s_x = [g.sem(f"rows_gathered{i}") for i in range(2)]
        s_xt = g.sem("rows_turned")
        s_xa = g.sem("rows_turned_act_copied")
        s_xd = g.sem("rows_turned_dve_copied")
        s_gu = g.sem("gate_up_ready")
        s_sg = g.sem("expert_sigmoid_ready")
        s_g = g.sem("expert_gate_ready")
        s_h = g.sem("expert_hidden_ready")
        s_ht = g.sem("hidden_turned")
        s_hc = g.sem("hidden_turned_copied")
        s_dn = g.sem("down_ready")
        s_ya = g.sem("y_act_copied")
        s_yd = g.sem("y_dve_copied")
        s_st = [g.sem(f"y_stored{i}") for i in range(2)]
        wg_d = io["w_exp_gate"][0].rearrange("e (k p) f -> e p k f", p=P)
        wu_d = io["w_exp_up"][0].rearrange("e (k p) f -> e p k f", p=P)
        wd_d = io["w_exp_down"][0].rearrange("e (k p) n -> e p k n", p=P)
        block = st.enter_context(nc.Block())

        def steps(eng, body, first_only=None):
            for u in range(R):
                body(u, u, True)
            with eng.Fori(1, STEPS // R) as i:
                for u in range(R):
                    body(R * i + u, u, False, i)

        def used_blocks(eng):
            return eng.value_load(r["n_col"][0:1, 0:1], min_val=24, max_val=BLOCKS)

        @block.sync
        def _(sp):
            used = used_blocks(sp)

            def fetch(b, u):
                e = sp.value_load(r["be_row"][0:1, bass.ds(b, 1)], min_val=0, max_val=E - 1)
                sp.dma_start(wgu[:, u, :, 0:F], wg_d[bass.ds(e, 1)].rearrange("a p k f -> p (a k) f")).then_inc(s_w[u], 16)
                sp.dma_start(wgu[:, u, :, F:2 * F], wu_d[bass.ds(e, 1)].rearrange("a p k f -> p (a k) f")).then_inc(s_w[u], 16)
                sp.dma_start(wd[:, u], wd_d[bass.ds(e, 1)].rearrange("a p k n -> p (a k) n")).then_inc(s_w[u], 16)

            def body(b, u, first, i=0):
                if first:
                    fetch(b, u)
                    return
                with sp.If(b < used):
                    sp.wait_ge(s_dn, b - 3)
                    fetch(b, u)
            steps(sp, body)

        @block.gpsimd
        def _(pool):
            used = used_blocks(pool)

            def gather(b, u, first, i=0):
                if not (first and u < 2):
                    pool.wait_ge(s_xt, b - 1)
                nc.gpsimd.tensor_copy(idx[:, u % 2:u % 2 + 1], r["row_tok"][:, bass.ds(b, 1)]).then_inc(s_i, 1)
                pool.wait_ge(s_i, b + 1)
                pool.sem_inc(s_seen, 1)
                pool.indirect_dma_start(xg[:, u % 2, :], None, r["h"],
                                        bass.IndirectOffsetOnAxis(ap=idx[:, u % 2:u % 2 + 1], axis=0),
                                        bounds_check=S - 1, oob_is_err=False).then_inc(s_x[u % 2], 16)

            def scatter(b, u):
                pool.wait_ge(s_ya, b - 3)
                pool.wait_ge(s_yd, b - 3)
                nc.gpsimd.tensor_copy(oidx[:, u % 2:u % 2 + 1], r["row_asg_cols"][:, bass.ds(b - 4, 1)]).then_inc(s_oi, 1)
                pool.wait_ge(s_oi, b - 3)
                pool.sem_inc(s_seen, 1)
                pool.indirect_dma_start(r["y"], bass.IndirectOffsetOnAxis(ap=oidx[:, u % 2:u % 2 + 1], axis=0),
                                        y[:, u % 2, :], None, bounds_check=TOPK * S - 1,
                                        oob_is_err=False).then_inc(s_st[u % 2], 16)

            def body(b, u, first, i=0):
                if first:
                    gather(b, u, first, i)
                    return
                with pool.If(b < used + 4):
                    scatter(b, u)
                with pool.If(b < used + 1):
                    gather(b, u, first, i)
            nc.gpsimd.memset(xg[:], 0.0).then_inc(s_zero, 1)
            pool.wait_ge(s_zero, 1)
            steps(pool, body)
            pool.wait_ge(s_st[0], ((used + 1) >> 1) * 16)
            pool.wait_ge(s_st[1], (used >> 1) * 16)

        @block.tensor
        def _(pe):
            used = used_blocks(pe)

            def turn_rows(b, u, i, first):
                pe.wait_ge(s_x[u % 2], 32 * i + 16 * (u // 2) + 16)
                if not (first and u == 0):
                    pe.wait_ge(s_xa, b)
                    pe.wait_ge(s_xd, b)
                for k in range(KD):
                    tr = nc.tensor.transpose(g.ps[:, k // 4, (k % 4) * P:(k % 4) * P + P],
                                             xg[:, u % 2, k * P:k * P + P], g.ident[:])
                tr.then_inc(s_xt, 1)

            def down(b, u, first):
                o = (u - 1) % R
                pe.wait_ge(s_hc, b)
                if not (first and u == 1):
                    pe.wait_ge(s_ya, b - 1)
                    pe.wait_ge(s_yd, b - 1)
                for n in range(2):
                    for k in range(2):
                        mm = nc.tensor.matmul(g.ps[:, 5 + n, :], hT[:, o % 2, k, :], wd[:, o, k, n * 512:n * 512 + 512],
                                              start=k == 0, stop=k == 1)
                mm.then_inc(s_dn, 1)

            def step(b, u, first, i):
                pe.wait_ge(s_w[u], 48 * i + 48)
                pe.wait_ge(s_xa, b + 1)
                pe.wait_ge(s_xd, b + 1)
                if not (first and u < 2):
                    pe.wait_ge(s_h, b - 1)
                for k in range(KD):
                    mm = nc.tensor.matmul(g.ps[:, 2 + u % 2, :], xT[:, u % 2, k, :], wgu[:, u, k, :],
                                          start=k == 0, stop=k == KD - 1)
                mm.then_inc(s_gu, 1)
                turn_rows(b + 1, u + 1, i, False)
                if not (first and u == 0):
                    down(b, u, first)
                pe.wait_ge(s_h, b + 1)
                for k in range(2):
                    tr = nc.tensor.transpose(g.ps[:, 4, k * P:k * P + P], h[:, k * P:k * P + P], g.ident[:])
                tr.then_inc(s_ht, 1)

            def body(b, u, first, i=0):
                if first:
                    if u == 0:
                        turn_rows(0, 0, 0, True)
                    step(b, u, first, 0)
                    return
                with pe.If(b < used):
                    step(b, u, first, i)
                with pe.If(b == used):
                    down(b, u, first)
            steps(pe, body)

        @block.scalar
        def _(act):
            used = used_blocks(act)

            def copy_rows(b, u):
                act.wait_ge(s_xt, b + 1)
                nc.scalar.copy(xT[:, u % 2, 0:4, :], g.ps[:, 0, :].rearrange("p (k q) -> p k q", k=4)).then_inc(s_xa, 1)

            def copy_y(b, u, first, i):
                o = (u - 1) % 2
                act.wait_ge(s_dn, b)
                if not (first and u < 3):
                    act.wait_ge(s_st[o], 32 * i + 16 * ((u - 3) // 2) + 16)
                nc.scalar.copy(y[:, o, 0:512], g.ps[:, 5, :]).then_inc(s_ya, 1)

            def step(b, u, first, i):
                act.wait_ge(s_gu, b + 1)
                if not (first and u == 0):
                    act.wait_ge(s_g, b)
                nc.scalar.activation(sg[:], g.ps[:, 2 + u % 2, 0:F], ACT.Sigmoid).then_inc(s_sg, 1)
                copy_rows(b + 1, u + 1)
                if not (first and u == 0):
                    copy_y(b, u, first, i)
                act.wait_ge(s_ht, b + 1)
                nc.scalar.copy(hT[:, u % 2], g.ps[:, 4, 0:2 * P].rearrange("p (k q) -> p k q", k=2)).then_inc(s_hc, 1)

            def body(b, u, first, i=0):
                if first:
                    if u == 0:
                        copy_rows(0, 0)
                    step(b, u, first, 0)
                    return
                with act.If(b < used):
                    step(b, u, first, i)
                with act.If(b == used):
                    copy_y(b, u, first, i)
            steps(act, body)

        @block.vector
        def _(dve):
            used = used_blocks(dve)

            def copy_rows(b, u):
                dve.wait_ge(s_xt, b + 1)
                nc.vector.tensor_copy(xT[:, u % 2, 4:8, :], g.ps[:, 1, :].rearrange("p (k q) -> p k q", k=4)).then_inc(s_xd, 1)

            def copy_y(b, u, first, i):
                o = (u - 1) % 2
                dve.wait_ge(s_dn, b)
                if not (first and u < 3):
                    dve.wait_ge(s_st[o], 32 * i + 16 * ((u - 3) // 2) + 16)
                nc.vector.tensor_copy(y[:, o, 512:1024], g.ps[:, 6, :]).then_inc(s_yd, 1)

            def step(b, u, first, i):
                bank = g.ps[:, 2 + u % 2, :]
                dve.wait_ge(s_sg, b + 1)
                if not (first and u == 0):
                    dve.wait_ge(s_ht, b)
                nc.vector.tensor_tensor(h[:], bank[:, 0:F], sg[:], ALU.mult).then_inc(s_g, 1)
                dve.wait_ge(s_g, b + 1)
                nc.vector.tensor_tensor(h[:], bank[:, F:2 * F], h[:], ALU.mult).then_inc(s_h, 1)
                copy_rows(b + 1, u + 1)
                if not (first and u == 0):
                    copy_y(b, u, first, i)

            def body(b, u, first, i=0):
                if first:
                    if u == 0:
                        copy_rows(0, 0)
                    step(b, u, first, 0)
                    return
                with dve.If(b < used):
                    step(b, u, first, i)
                with dve.If(b == used):
                    copy_y(b, u, first, i)
            steps(dve, body)


def combine_stage(g, r, acc, gate_f):
    nc = g.nc
    with g.stage() as st:
        yk = g.sb("yk", [P, 3, NT, D], ctx=st)
        s_y = [g.sem(f"y_loaded{i}") for i in range(3)]
        s_used = g.sem("y_added")
        s_dve = g.sem("combine_dve_steps")
        block = st.enter_context(nc.Block())

        @block.sync
        def _(sp):
            for k in range(TOPK):
                if k >= 3:
                    sp.wait_ge(s_used, 4 * (k - 2))
                sp.dma_start(yk[:, k % 3], r["y"][k * S:k * S + S, :].rearrange("(t p) d -> p t d", p=P)).then_inc(s_y[k % 3], 16)

        @block.vector
        def _(dve):
            link = Chain(dve, s_dve)
            for k in range(TOPK):
                dve.wait_ge(s_y[k % 3], 16 * (k // 3) + 16)
                for t in range(NT):
                    if k:
                        dve.wait_ge(s_used, 4 * (k - 1) + t + 1)
                    nc.vector.scalar_tensor_tensor(acc[:, t, :], yk[:, k % 3, t, :], r["gate"][:, t, k:k + 1],
                                                   acc[:, t, :], ALU.mult, ALU.add).then_inc(s_used, 1)
            for t in range(NT):
                dve.wait_ge(s_used, 4 * (TOPK - 1) + t + 1)
                link(nc.vector.tensor_tensor(acc[:, t, :], acc[:, t, :], gate_f, ALU.mult))
                nc.vector.tensor_tensor(g.x[:, t, :], g.x[:, t, :], acc[:, t, :], ALU.add)


def moe(g, io, dbg):
    with ExitStack() as a:
        r = {"row_asg": g.dram("row_assignments", [(BLOCKS + 4) * P, 1], I32), "be_dram": g.dram("be_d", [BLOCKS + 4, 1], I32),
             "n_dram": g.dram("n_d", [1, 1], I32), "h": g.dram("h2_rows", [S, D]),
             "y": g.dram("y_rows", [TOPK * S, D]),
             "be_row": g.sb("be_row", [1, BLOCKS + 4], I32, ctx=a), "be_col": g.sb("be_col", [P, 1], I32, ctx=a),
             "n_col": g.sb("n_col", [P, 1], I32, ctx=a), "gate": g.sb("gate6", [P, NT, TOPK], ctx=a),
             "dest": g.sb("dest6", [P, NT, TOPK], U32, ctx=a),
             "row_asg_cols": g.sb("row_asg_cols", [P, BLOCKS + 4], U32, ctx=a),
             "row_tok": g.sb("row_tok", [P, BLOCKS + 4], I32, ctx=a)}
        acc = g.sb("moe_acc", [P, NT, D], ctx=a)
        with ExitStack() as b:
            hT = g.sb("h2T", [P, 2, KD, S], F32R, ctx=b)
            norm_stage(g, "ffn1", io["g_ffn_norm"], hT, scale=g.mod[:, 4 * D:5 * D], shift=g.mod[:, 3 * D:4 * D],
                       h_dram=r["h"])
            shared_stage(g, io, hT, acc)
            route_stage(g, io, hT, r)
        expert_stage(g, io, r)
        combine_stage(g, r, acc, g.mod[:, 5 * D:6 * D])


def project2_stage(g, io, hT, p2):
    nc = g.nc
    w_in = io["w_in_2"][0].rearrange("(k p) n -> p k n", p=P)
    groups = [(c, min(512, W2 - c)) for c in range(0, W2, 512)]
    with g.stage() as st:
        w = SplitWeights(g, "win2", st)
        s_ps = g.sem("proj2_ready")
        s_act = g.sem("proj2_act_evacuated")
        s_dve = g.sem("proj2_dve_evacuated")
        block = st.enter_context(nc.Block())
        n = len(groups)

        @block.sync
        def _(sp):
            for s, (c, width) in enumerate(groups):
                for half in range(2):
                    w.load(sp, w_in[:, 4 * half:4 * half + 4, c:c + width], 0, 2 * s + half, width)

        @block.tensor
        def _(pe):
            for s, (_, width) in enumerate(groups):
                for half in range(2):
                    q = 2 * s + half
                    w.ready(pe, 0, q)
                    for t in range(NT):
                        if s >= 2 and half == 0:
                            pe.wait_ge((s_act, s_dve)[t // 2], 2 * (s - 2) + t % 2 + 1)
                        for j in range(4):
                            k = 4 * half + j
                            mm = split_product(nc, g.ps[:, (s % 2) * 4 + t, 0:width], parts_of(hT, k, t * P, t * P + P),
                                               w.at(q, j, 0, width), k == 0, k == KD - 1)
                        mm.then_inc(s_ps, 1)

        @block.scalar
        def _(act):
            for s in range(-1, n):
                for half in range(2):
                    if s + 1 < n:
                        w.high(act, 0, 2 * s + 2 + half, s_ps, 4, groups[s + 1][1])
                for t in range(2 if s >= 0 else 0):
                    c, width = groups[s]
                    act.wait_ge(s_ps, 8 * s + 4 + t + 1)
                    nc.scalar.copy(p2[:, t, c:c + width], g.ps[:, (s % 2) * 4 + t, 0:width]).then_inc(s_act, 1)

        @block.vector
        def _(dve):
            for s in range(-1, n):
                for half in range(2):
                    if s + 1 < n:
                        w.low(dve, 0, 2 * s + 2 + half, s_ps, 4, groups[s + 1][1])
                for t in range(2, NT if s >= 0 else 2):
                    c, width = groups[s]
                    dve.wait_ge(s_ps, 8 * s + 4 + t + 1)
                    nc.vector.tensor_copy(p2[:, t, c:c + width], g.ps[:, (s % 2) * 4 + t, 0:width]).then_inc(s_dve, 1)


Q_NSA, K_SEL, K_WIN, Q_DIL, K_DIL, Q_SB, K_SB, KV_CMP = 0, 4, 5, 6, 12, 18, 24, 30
N_COLS = 32


def heads2_stage(g, io, p2, qk, gates):
    nc = g.nc
    NH = Q_SB
    groups = [(0, Q_NSA, 4, 0), (C2_KV + 128, K_SEL, 1, 1), (C2_KV + 256, K_WIN, 1, 2), (C2_B, Q_DIL, 6, 3),
              (C2_B + 384, K_DIL, 6, 4)]
    with g.stage() as st:
        sq = g.sb("head_squares", [P, NT, NH * DH], ctx=st)
        gn = g.sb("head_gains", [P, 5, DH], ctx=st)
        ss = g.sb("head_stats", [P, 3, NT * NH], ctx=st)
        s_ld = g.sem("head_gains_loaded")
        s_ms = g.sem("head_mean_squares")
        s_rt = g.sem("head_roots")
        s_dve = g.sem("heads_dve_steps")
        block = st.enter_context(nc.Block())

        @block.sync
        def _(sp):
            for i, row in enumerate((io["qk_gain_nsa_2"][0, 0:1], io["qk_gain_nsa_2"][0, 2:3], io["qk_gain_nsa_2"][0, 3:4],
                                     io["qk_gain_dil_2"][0, 0:1], io["qk_gain_dil_2"][0, 1:2])):
                sp.dma_start(gn[:, i, :], bcast_rows(row, DH)).then_inc(s_ld, 16)

        @block.scalar
        def _(act):
            nc.scalar.mul(qk[:, :, Q_SB * DH:K_SB * DH], p2[:, :, C2_C:C2_C + 384], DH ** -0.5)
            nc.scalar.copy(qk[:, :, K_SB * DH:KV_CMP * DH], p2[:, :, C2_C + 384:C2_C + 768])
            nc.scalar.copy(qk[:, :, KV_CMP * DH:], p2[:, :, C2_KV:C2_KV + 128])
            nc.scalar.activation(gates[:], p2[:, :, C2_G:C2_G + 12], ACT.Sigmoid)
            act.wait_ge(s_ms, 1)
            nc.scalar.activation(ss[:, 2, :], ss[:, 1, :], ACT.Sqrt).then_inc(s_rt, 1)

        @block.vector
        def _(dve):
            link = Chain(dve, s_dve)
            v = nc.vector
            for src, dst, n, _ in groups:
                x = p2[:, :, src:src + n * DH]
                ins = v.tensor_tensor(sq[:, :, dst * DH:(dst + n) * DH], x, x, ALU.mult)
            link(ins)
            link(v.tensor_reduce(ss[:, 0, :], sq[:].rearrange("p t (h d) -> p (t h) d", d=DH), AX.X, ALU.add))
            v.tensor_scalar(ss[:, 1, :], ss[:, 0, :], 1.0 / DH, EPS, ALU.mult, ALU.add).then_inc(s_ms, 1)
            dve.wait_ge(s_ld, 80)
            v.tensor_scalar(gn[:, 0, :], gn[:, 0, :], DH ** -0.5, None, ALU.mult)
            v.tensor_scalar(gn[:, 3, :], gn[:, 3, :], DH ** -0.5, None, ALU.mult)
            dve.wait_ge(s_rt, 1)
            link(v.reciprocal(ss[:, 1, :], ss[:, 2, :]))
            for t in range(NT):
                for src, dst, n, _ in groups:
                    root = ss[:, 1, t * NH + dst:t * NH + dst + n].unsqueeze(2).broadcast_to([P, n, DH])
                    ins = v.tensor_tensor(qk[:, t, dst * DH:(dst + n) * DH].rearrange("p (h d) -> p h d", d=DH),
                                          p2[:, t, src:src + n * DH].rearrange("p (h d) -> p h d", d=DH), root, ALU.mult)
                link(ins)
                for src, dst, n, gain in groups:
                    y = qk[:, t, dst * DH:(dst + n) * DH].rearrange("p (h d) -> p h d", d=DH)
                    v.tensor_tensor(y, y, gn[:, gain:gain + 1, :].broadcast_to([P, n, DH]), ALU.mult)


def compressed_stage(g, io, kvT, qT, o_c):
    nc = g.nc
    N = N_CMP
    L = 32
    with g.stage() as st:
        w1 = g.sb("cmp_w1", [P, L, P], ctx=st)
        w2 = g.sb("cmp_w2", [P, 2, DH], ctx=st)
        pe_ = g.sb("cmp_pe", [P, L], ctx=st)
        un = g.sb("cmp_windows", [P, L, N], ctx=st)
        hid = g.sb("cmp_hidden", [P, 3, 2, N], ctx=st)
        kc = g.sb("kc_rows", [N, 3, DH], ctx=st)
        vc = g.sb("vc_rows", [N, DH], ctx=st)
        gain = g.sb("kc_gain", [N, DH], ctx=st)
        ms = g.sb("kc_stat", [N, 4], ctx=st)
        kcT = g.sb("kc_cols", [DH + 2, 32], ctx=st)
        q = g.sb("cmp_q", [DH + 2, H_NSA, S], ctx=st)
        mk = g.sb("cmp_mask", [P, 2, NT, 32], ctx=st)
        p = g.sb("cmp_p", [P, 4 * H_NSA, N], ctx=st)
        m = g.sb("cmp_max", [P, 3, 4 * H_NSA], ctx=st)
        pT = g.sb("cmp_pT", [N, 4 * H_NSA, P], ctx=st)
        s_w = g.sem("cmp_loads")
        s_un = g.sem("cmp_windows_ready")
        s_hid = g.sem("cmp_hidden_ready")
        s_th = g.sem("cmp_tanh_in")
        s_tg = g.sem("cmp_tanh_out")
        s_ge = g.sem("cmp_gelu_ready")
        s_kv = g.sem("cmp_kv_ready")
        s_ms = g.sem("kc_mean_square")
        s_rt = g.sem("kc_root")
        s_kn = g.sem("kc_normed")
        s_kt = g.sem("kc_turned")
        s_kc = g.sem("kc_cols_ready")
        s_s = g.sem("cmp_scores_ready")
        s_e = g.sem("cmp_exponents_ready")
        s_x = g.sem("cmp_exponentials_ready")
        s_p = g.sem("cmp_probs_ready")
        s_t = g.sem("cmp_turned")
        s_tc = g.sem("cmp_turned_copied")
        s_o = g.sem("cmp_values_ready")
        s_dve = g.sem("cmp_dve_steps")
        block = st.enter_context(nc.Block())

        @block.sync
        def _(sp):
            for c in range(2):
                sp.dma_start(w1[c * DH:c * DH + DH], io["cmp_w1_2"][0, c].rearrange("(l d) h -> d l h", d=DH)).then_inc(s_w, 16)
                sp.dma_start(pe_[c * DH:c * DH + DH, :], io["cmp_pe_2"][0, c].rearrange("l d -> d l"),
                             allow_slow_non_contiguous=True).then_inc(s_w, 16)
            sp.dma_start(w2[:], io["cmp_w2_2"][0].rearrange("c h d -> h c d")).then_inc(s_w, 16)
            sp.dma_start(gain[:], io["qk_gain_nsa_2"][0, 1:2].broadcast_to([N, DH])).then_inc(s_w, 16)
            sp.dma_start(kcT[DH:DH + 2, :], io["const_alibi_c"]).then_inc(s_w, 16)
            sp.dma_start(mk[:], io["const_cmp_mask"]).then_inc(s_w, 16)
            sp.dma_start(q[0:DH], qT[Q_NSA * DH:(Q_NSA + H_NSA) * DH, :].rearrange("(h d) s -> d h s", d=DH)).then_inc(s_w, 16)
            sp.dma_start(q[DH:DH + 2], io["const_alibi_q"][2 * H_DIL:2 * H_DIL + 2 * H_NSA, :].rearrange("(h r) s -> r h s", r=2)).then_inc(s_w, 16)

        @block.tensor
        def _(pe):
            pe.wait_ge(s_un, 1)
            for c in range(2):
                rows = slice(c * DH, c * DH + DH)
                for i in range(L):
                    mm = nc.tensor.matmul(g.ps[:, c, 0:N], w1[rows, i, :], un[rows, i, :], start=i == 0, stop=i == L - 1)
                mm.then_inc(s_hid, 1)
            pe.wait_ge(s_ge, 1)
            for c in range(2):
                nc.tensor.matmul(g.ps[0:N, 2 + c, 0:DH], hid[:, 0, c, :], w2[:, c, :], start=True, stop=True).then_inc(s_kv, 1)
            pe.wait_ge(s_kn, 1)
            nc.tensor.transpose(g.ps[0:DH, 4, 0:N], kc[:, 0, :], g.ident[0:N, 0:N]).then_inc(s_kt, 1)
            pe.wait_ge(s_kc, 1)
            for i in range(4 * H_NSA):
                mm = nc.tensor.matmul(g.ps[:, 5, i * N:i * N + N], q[:, i // 4, (i % 4) * P:(i % 4) * P + P],
                                      kcT[:, 0:N], start=True, stop=True)
            mm.then_inc(s_s, 1)
            pe.wait_ge(s_p, 1)
            for b in range(4):
                for i in range(4 * b, 4 * b + 4):
                    tr = nc.tensor.transpose(g.ps[0:N, b, (i % 4) * P:(i % 4) * P + P], p[:, i, :], g.ident[:])
                tr.then_inc(s_t, 1)
            for i in range(4 * H_NSA):
                if i % 4 == 0:
                    pe.wait_ge(s_tc, i // 4 + 1)
                mm = nc.tensor.matmul(g.ps[:, 6 + i // 8, (i % 8) * DH:(i % 8) * DH + DH], pT[:, i, :], vc[:],
                                      start=True, stop=True)
                if i % 8 == 7:
                    mm.then_inc(s_o, 1)

        @block.scalar
        def _(act):
            act.wait_ge(s_th, 1)
            nc.scalar.activation(hid[:, 1], hid[:, 1], ACT.Tanh, scale=0.7978845608028654).then_inc(s_tg, 1)
            act.wait_ge(s_ms, 1)
            nc.scalar.activation(ms[:, 2:3], ms[:, 1:2], ACT.Sqrt).then_inc(s_rt, 1)
            act.wait_ge(s_e, 1)
            nc.scalar.activation(p[:], p[:], ACT.Exp).then_inc(s_x, 1)
            for b in range(4):
                act.wait_ge(s_t, b + 1)
                nc.scalar.copy(pT[:, 4 * b:4 * b + 4, :], g.ps[0:N, b, :].rearrange("p (i q) -> p i q", q=P)).then_inc(s_tc, 1)

        @block.vector
        def _(dve):
            link = Chain(dve, s_dve)
            v = nc.vector
            dve.wait_ge(s_w, 160)
            src = kvT.rearrange("p (n b) -> p b n", b=16)
            for a in range(2):
                link(v.tensor_tensor(un[:, 16 * a:16 * a + 16, :], src[:, :, a:a + N],
                                     pe_[:, 16 * a:16 * a + 16].unsqueeze(2).broadcast_to([P, 16, N]), ALU.add))
            dve.sem_inc(s_un, 1)
            dve.wait_ge(s_hid, 2)
            link(v.tensor_copy(hid[:, 0], g.ps[:, 0:2, 0:N]))
            link(v.tensor_tensor(hid[:, 1], hid[:, 0], hid[:, 0], ALU.mult))
            link(v.tensor_scalar(hid[:, 1], hid[:, 1], 0.044715, 1.0, ALU.mult, ALU.add))
            v.tensor_tensor(hid[:, 1], hid[:, 1], hid[:, 0], ALU.mult).then_inc(s_th, 1)
            dve.wait_ge(s_tg, 1)
            link(v.tensor_scalar(hid[:, 1], hid[:, 1], 1.0, 0.5, ALU.add, ALU.mult))
            v.tensor_tensor(hid[:, 0], hid[:, 0], hid[:, 1], ALU.mult).then_inc(s_ge, 1)
            dve.wait_ge(s_kv, 2)
            v.tensor_copy(vc[:], g.ps[0:N, 3, 0:DH])
            link(v.tensor_copy(kc[:, 1, :], g.ps[0:N, 2, 0:DH]))
            link(v.tensor_tensor(kc[:, 2, :], kc[:, 1, :], kc[:, 1, :], ALU.mult))
            link(v.tensor_reduce(ms[:, 0:1], kc[:, 2, :], AX.X, ALU.add))
            v.tensor_scalar(ms[:, 1:2], ms[:, 0:1], 1.0 / DH, EPS, ALU.mult, ALU.add).then_inc(s_ms, 1)
            dve.wait_ge(s_rt, 1)
            link(v.reciprocal(ms[:, 3:4], ms[:, 2:3]))
            v.scalar_tensor_tensor(kc[:, 0, :], kc[:, 1, :], ms[:, 3:4], gain[:], ALU.mult, ALU.mult).then_inc(s_kn, 1)
            dve.wait_ge(s_kt, 1)
            v.tensor_copy(kcT[0:DH, 0:N], g.ps[0:DH, 4, 0:N]).then_inc(s_kc, 1)
            dve.wait_ge(s_s, 1)
            for h in range(H_NSA):
                ins = v.tensor_tensor(p[:, 4 * h:4 * h + 4, :], g.ps[:, 5, 4 * h * N:4 * (h + 1) * N].rearrange("p (i n) -> p i n", n=N),
                                      mk[:, 1, :, 0:N], ALU.add)
            link(ins)
            link(v.tensor_reduce(m[:, 0, :], p[:], AX.X, ALU.max))
            v.tensor_tensor(p[:], p[:], m[:, 0, :].unsqueeze(2).broadcast_to([P, 16, N]), ALU.subtract).then_inc(s_e, 1)
            dve.wait_ge(s_x, 1)
            for h in range(H_NSA):
                ins = v.tensor_tensor(p[:, 4 * h:4 * h + 4, :], p[:, 4 * h:4 * h + 4, :], mk[:, 0, :, 0:N], ALU.mult)
            link(ins)
            link(v.tensor_reduce(m[:, 1, :], p[:], AX.X, ALU.add))
            link(v.tensor_scalar(m[:, 1, :], m[:, 1, :], 1e-30, None, ALU.max))
            link(v.reciprocal(m[:, 2, :], m[:, 1, :]))
            v.tensor_tensor(p[:], p[:], m[:, 2, :].unsqueeze(2).broadcast_to([P, 16, N]), ALU.mult).then_inc(s_p, 1)
            for b in range(2):
                dve.wait_ge(s_o, b + 1)
                v.tensor_copy(o_c[:, 8 * b:8 * b + 8, :], g.ps[:, 6 + b, :].rearrange("p (i d) -> p i d", d=DH))


def stick_stage(g, heads, q_parts, k_parts, v, out, mask):
    nc = g.nc
    LT, LV = 3, 5
    with g.stage() as st:
        q = g.sb("sb_q", [DH, 2, S], ctx=st)
        kk = g.sb("sb_k", [DH, 2, S], ctx=st)
        la = g.sb("sb_log", [P, 4, S], ctx=st)
        sp_ = g.sb("sb_softplus", [P, 2, S], ctx=st)
        su = g.sb("sb_sums", [P, 4, S], ctx=st)
        ones = g.sb("sb_ones", [P, S], ctx=st)
        p = g.sb("sb_p", [P, 4, S], ctx=st)
        pt = g.sb("sb_pt", [P, 4, NT, P], ctx=st)
        s_qk = [g.sem(f"sb_qk_loaded{i}") for i in range(2)]
        s_s = g.sem("sb_scores_ready")
        s_ab = g.sem("sb_abs_ready")
        s_ex = g.sem("sb_exp_ready")
        s_ln = g.sem("sb_log_ready")
        s_sp = g.sem("sb_softplus_ready")
        s_su = g.sem("sb_sums_ready")
        s_x = g.sem("sb_exponents_ready")
        s_p = g.sem("sb_weights_ready")
        s_t = g.sem("sb_turned")
        s_pt = g.sem("sb_turned_copied")
        s_o = g.sem("sb_values_ready")
        s_od = g.sem("sb_out_done")
        s_one = g.sem("sb_ones_ready")
        loads = 16 * (len(q_parts) + len(k_parts))
        block = st.enter_context(nc.Block())

        @block.sync
        def _(sp):
            fetch_heads(g, sp, heads, q, kk, q_parts, k_parts, s_qk, s_s)

        @block.tensor
        def _(pe):
            def body(i, base, drain):
                for u in range(8):
                    j, t = u // 4, u % 4
                    n = (t + 1) * P
                    if not drain:
                        if t == 0:
                            pe.wait_ge(s_qk[j], loads * i + loads)
                        at_least(pe, s_ab, base, u - 3)
                        at_least(pe, s_x, base, u - 3)
                        mk, first = mask(i, t)
                        nc.tensor.matmul(g.ps[:, u % 4, 0:n], q[:, j, t * P:t * P + P], kk[:, j, 0:n],
                                         start=True, stop=False)
                        nc.tensor.matmul(g.ps[:, u % 4, first:n], g.identb[:], mk,
                                         start=False, stop=True).then_inc(s_s, 1)
                    if (at := lagging(base, u, LT, drain)) is not None:
                        a = at[0]
                        at_least(pe, s_p, base, u - LT + 1)
                        at_least(pe, s_pt, base, u - LT - 1)
                        for b in range(a % 4 + 1):
                            tr = nc.tensor.transpose(g.ps[:, 4 + a % 2, b * P:b * P + P], p[:, a % 4, b * P:b * P + P],
                                                     g.ident[:])
                        tr.then_inc(s_t, 1)
                    if (at := lagging(base, u, LV, drain)) is not None:
                        a, head = at[0], 2 * i + at[0] // 4 - 2 * at[1]
                        at_least(pe, s_pt, base, u - LV + 1)
                        at_least(pe, s_od, base, u - LV - 1)
                        for b in range(a % 4 + 1):
                            mm = nc.tensor.matmul(g.ps[:, 6 + a % 2, 0:DH], pt[:, a % 4, b, :], v(b, head),
                                                  start=b == 0, stop=b == a % 4)
                        mm.then_inc(s_o, 1)
            turns(pe, heads, body)

        @block.scalar
        def _(act):
            def body(i, base, drain):
                if drain:
                    return
                for first in (0, 4):
                    places = range(first, first + 4)
                    for u in places:
                        z, l = g.ps[:, u % 4, 0:(u % 4 + 1) * P], la[:, u % 4, 0:(u % 4 + 1) * P]
                        at_least(act, s_s, base, u + 1)
                        at_least(act, s_sp, base, u - 3)
                        nc.scalar.activation(l, z, ACT.Abs).then_inc(s_ab, 1)
                        at_least(act, s_ab, base, u + 1)
                        nc.scalar.activation(l, l, ACT.Exp, scale=-1.0).then_inc(s_ex, 1)
                    for u in places:
                        l = la[:, u % 4, 0:(u % 4 + 1) * P]
                        at_least(act, s_ex, base, u + 1)
                        nc.scalar.activation(l, l, ACT.Ln, bias=1.0).then_inc(s_ln, 1)
                    for u in places:
                        n = (u % 4 + 1) * P
                        at_least(act, s_x, base, u + 1)
                        at_least(act, s_t, base, u - 3)
                        nc.scalar.activation(p[:, u % 4, 0:n], su[:, u % 4, 0:n], ACT.Exp).then_inc(s_p, 1)
            turns(act, heads, body)

        @block.vector
        def _(dve):
            nc.vector.memset(ones[:], 1.0).then_inc(s_one, 1)
            dve.wait_ge(s_one, 1)

            def body(i, base, drain):
                for u in range(8):
                    n = (u % 4 + 1) * P
                    if (at := lagging(base, u, LT, drain)) is not None:
                        a = at[0]
                        at_least(dve, s_t, base, u - LT + 1)
                        at_least(dve, s_o, base, u - LT - 3)
                        nc.vector.tensor_copy(pt[:, a % 4, 0:a % 4 + 1, :],
                                              g.ps[:, 4 + a % 2, 0:(a % 4 + 1) * P].rearrange("p (b s) -> p b s", s=P)
                                              ).then_inc(s_pt, 1)
                    if (at := lagging(base, u, LV, drain)) is not None:
                        a, head = at[0], 2 * i + at[0] // 4 - 2 * at[1]
                        at_least(dve, s_o, base, u - LV + 1)
                        nc.vector.tensor_copy(out(a % 4, head), g.ps[:, 6 + a % 2, 0:DH]).then_inc(s_od, 1)
                    if not drain:
                        z = g.ps[:, u % 4, 0:n]
                        s, c = sp_[:, u % 2, 0:n], su[:, u % 4, 0:n]
                        at_least(dve, s_ln, base, u + 1)
                        nc.vector.scalar_tensor_tensor(s, z, 0.0, la[:, u % 4, 0:n], ALU.max, ALU.add).then_inc(s_sp, 1)
                        at_least(dve, s_sp, base, u + 1)
                        at_least(dve, s_p, base, u - 3)
                        nc.vector.tensor_tensor_scan(c[:, ::-1], ones[:, 0:n], s[:, ::-1], 0.0, ALU.mult,
                                                     ALU.add).then_inc(s_su, 1)
                        at_least(dve, s_su, base, u + 1)
                        nc.vector.tensor_tensor(c, z, c, ALU.subtract).then_inc(s_x, 1)
            turns(dve, heads, body)


def gather_heads_stage(g, o_c, o_nsa, o_dil, stats, gates, cat):
    nc = g.nc
    with g.stage() as st:
        lse = g.sb("lse", [P, 24], ctx=st)
        tmp = g.sb("gated", [P, 2, H_NSA, DH], ctx=st)
        al = g.sb("alpha", [P, 3, 8], ctx=st)
        mx = g.sb("lse_max", [P, 3, 8], ctx=st)
        s_ln = g.sem("log_sums_ready")
        s_e = g.sem("lse_exponents_ready")
        s_x = g.sem("lse_exponentials_ready")
        s_dve = g.sem("gather_dve_steps")
        block = st.enter_context(nc.Block())

        @block.scalar
        def _(act):
            nc.scalar.activation(lse[:], stats[:, 1, :], ACT.Ln).then_inc(s_ln, 1)
            act.wait_ge(s_e, 1)
            nc.scalar.activation(al[:], al[:], ACT.Exp).then_inc(s_x, 1)

        @block.vector
        def _(dve):
            link = Chain(dve, s_dve)
            v = nc.vector
            dve.wait_ge(s_ln, 1)
            link(v.tensor_tensor(lse[:], lse[:], stats[:, 0, :], ALU.subtract))
            link(v.tensor_tensor(mx[:, 0, :], lse[:, 0:8], lse[:, 8:16], ALU.max))
            link(v.tensor_tensor(mx[:, 0, :], mx[:, 0, :], lse[:, 16:24], ALU.max))
            v.tensor_tensor(al[:], lse[:].rearrange("p (g a) -> p g a", a=8), mx[:, 0:1, :].broadcast_to([P, 3, 8]),
                            ALU.subtract).then_inc(s_e, 1)
            for t in range(NT):
                gt = gates[:, t, :].rearrange("p (h b) -> p h b", b=3)
                c3 = cat[:, t, 0:256].rearrange("p (h d) -> p h d", d=DH)
                branches = [o_c[:].rearrange("p (h t) d -> p t h d", t=NT)[:, t]]
                branches += [o_nsa[:, t, 256 * j:256 * j + 256].rearrange("p (h d) -> p h d", d=DH) for j in range(2)]
                for j, o in enumerate(branches):
                    gb = gt[:, :, j:j + 1].broadcast_to([P, H_NSA, DH])
                    if j == 0:
                        link(v.tensor_tensor(c3, o, gb, ALU.mult))
                    else:
                        link(v.tensor_tensor(tmp[:, 0], o, gb, ALU.mult))
                        link(v.tensor_tensor(c3, c3, tmp[:, 0], ALU.add))
            dve.wait_ge(s_x, 1)
            link(v.tensor_tensor(mx[:, 1, :], al[:, 0, :], al[:, 1, :], ALU.add))
            link(v.tensor_tensor(mx[:, 1, :], mx[:, 1, :], al[:, 2, :], ALU.add))
            link(v.reciprocal(mx[:, 2, :], mx[:, 1, :]))
            link(v.tensor_tensor(al[:], al[:], mx[:, 2:3, :].broadcast_to([P, 3, 8]), ALU.mult))
            for t in range(NT):
                for h in range(2):
                    dst = cat[:, t, 256 + h * DH:256 + h * DH + DH]
                    a = 4 * h + t
                    for grp in range(3):
                        o = o_dil[:, t, (2 * grp + h) * DH:(2 * grp + h) * DH + DH]
                        if grp == 0:
                            link(v.tensor_scalar(dst, o, al[:, 0, a:a + 1], None, ALU.mult))
                        else:
                            link(v.scalar_tensor_tensor(dst, o, al[:, grp, a:a + 1], dst, ALU.mult, ALU.add))


def mlp_up_stage(g, io, hT, u):
    nc = g.nc
    TURNS = FF // 1024
    w_up = io["w_up_2"][0].rearrange("(k p) n -> p k n", p=P)
    with g.stage() as st:
        w = SplitWeights(g, "w_up", st)
        s_ps = g.sem("mlp_up_ready")
        s_re = g.sem("relu_ready")
        s_sq = g.sem("square_ready")
        block = st.enter_context(nc.Block())

        def turns_of(eng, body):
            body(0, 0)
            with eng.Fori(1, TURNS) as i:
                body(i, 4 * i)

        def strip(i, c):
            return u[:, bass.ds(8 * i + c, 1), :].rearrange("p a s -> p (a s)")

        @block.sync
        def _(sp):
            def body(i, base):
                for q in range(4):
                    half = q % 2
                    w.load(sp, w_up[:, 4 * half:4 * half + 4, bass.ds(1024 * i + 512 * (q // 2), 512)], base, q)
            turns_of(sp, body)

        @block.tensor
        def _(pe):
            def body(i, base):
                for q in range(4):
                    half = q % 2
                    w.ready(pe, base, q)
                    for m in range(4):
                        c = 4 * (q // 2) + m
                        if half == 0:
                            at_least(pe, s_sq, 2 * base, c - 7)
                        for j in range(4):
                            k = 4 * half + j
                            mm = split_product(nc, g.ps[:, c, :], w.at(q, j, m * P, m * P + P), parts_of(hT, k),
                                               k == 0, k == KD - 1)
                        mm.then_inc(s_ps, 1)
            turns_of(pe, body)

        @block.scalar
        def _(act):
            def relus(i, base, grp):
                for m in range(4):
                    c = 4 * grp + m
                    act.wait_ge(s_ps, 4 * base + 8 * grp + 4 + m + 1)
                    nc.scalar.activation(strip(i, c), g.ps[:, c % 8, :], ACT.Relu).then_inc(s_re, 1)

            def body(i, base):
                for grp in range(2):
                    w.high(act, base, 2 * grp, s_ps, 4)
                    w.high(act, base, 2 * grp + 1, s_ps, 4)
                    if grp or not isinstance(base, int):
                        relus(i, base, grp - 1)
            turns_of(act, body)
            relus(TURNS, 4 * TURNS, -1)

        @block.vector
        def _(dve):
            def squares(i, base, grp):
                for m in range(4):
                    c = 4 * grp + m
                    dve.wait_ge(s_re, 2 * base + c + 1)
                    nc.vector.tensor_tensor(strip(i, c), strip(i, c), strip(i, c), ALU.mult).then_inc(s_sq, 1)

            def body(i, base):
                for grp in range(2):
                    w.low(dve, base, 2 * grp, s_ps, 4)
                    w.low(dve, base, 2 * grp + 1, s_ps, 4)
                    if grp or not isinstance(base, int):
                        squares(i, base, grp - 1)
            turns_of(dve, body)
            squares(TURNS, 4 * TURNS, -1)


def mlp_down_stage(g, io, u, out):
    nc = g.nc
    TURNS = FF // P // 8
    w_down = io["w_down_2"][0].rearrange("(k p) n -> p k n", p=P)
    with g.stage() as st:
        w = SplitWeights(g, "w_down", st)
        up = g.sb("hidden2_parts", [P, 2, 2, 4, S], F32R, ctx=st)
        s_uh = g.sem("hidden2_high_ready")
        s_ul = g.sem("hidden2_low_ready")
        s_ps = g.sem("mlp_down_ready")
        s_x = g.sem("x_ready")
        s_out = g.sem("out_stored")
        out_d = out.rearrange("(t p) d -> p t d", p=P)
        block = st.enter_context(nc.Block())

        def turns_of(eng, body):
            body(0, 0, 0)
            with eng.Fori(1, TURNS - 1) as i:
                body(i, 4 * i, 1)
            body(TURNS - 1, 4 * (TURNS - 1), 2)

        @block.sync
        def _(sp):
            def body(i, base, place):
                for q in range(4):
                    n = q % 2
                    w.load(sp, w_down[:, bass.ds(8 * i + 4 * (q // 2), 4), n * 512:n * 512 + 512], base, q)
            turns_of(sp, body)
            for t in range(NT):
                sp.wait_ge(s_x, NT + t + 1)
                sp.dma_start(out_d[:, t, :], g.x[:, t, :]).then_inc(s_out, 16)
            sp.wait_ge(s_out, 16 * NT)

        @block.tensor
        def _(pe):
            def body(i, base, place):
                for q in range(4):
                    c, n = q // 2, q % 2
                    if n == 0:
                        pe.wait_ge(s_uh, 2 * i + c + 1)
                        pe.wait_ge(s_ul, 2 * i + c + 1)
                    w.ready(pe, base, q)
                    for t in range(NT):
                        for k in range(4):
                            left = [up[:, c, a, k, t * P:t * P + P] for a in range(2)]
                            mm = split_product(nc, g.ps[:, 4 * n + t, :], left, w.at(q, k, 0, 512),
                                               place == 0 and c == 0 and k == 0, place == 2 and c == 1 and k == 3)
                        mm.then_inc(s_ps, 1)
            turns_of(pe, body)

        @block.scalar
        def _(act):
            def body(i, base, place):
                for c in range(2):
                    at_least(act, s_ps, 4 * base, 8 * c - 8)
                    nc.scalar.copy(up[:, c, 0], u[:, bass.ds(8 * i + 4 * c, 4), :]).then_inc(s_uh, 1)
                    w.high(act, base, 2 * c, s_ps, 4)
                    w.high(act, base, 2 * c + 1, s_ps, 4)
            turns_of(act, body)

        @block.vector
        def _(dve):
            def body(i, base, place):
                for c in range(2):
                    at_least(dve, s_ps, 4 * base, 8 * c - 8)
                    dve.wait_ge(s_uh, 2 * i + c + 1)
                    low_part(nc, up[:, c, 1], u[:, bass.ds(8 * i + 4 * c, 4), :], up[:, c, 0]).then_inc(s_ul, 1)
                    w.low(dve, base, 2 * c, s_ps, 4)
                    w.low(dve, base, 2 * c + 1, s_ps, 4)
            turns_of(dve, body)
            for n in range(2):
                for t in range(NT):
                    dve.wait_ge(s_ps, 16 * TURNS - 8 + 4 * n + t + 1)
                    xs = g.x[:, t, n * 512:n * 512 + 512]
                    nc.vector.tensor_tensor(xs, g.ps[:, 4 * n + t, :], xs, ALU.add).then_inc(s_x, 1)


def block2(g, io, dbg, out):
    colsT = g.dram("heads_T", [N_COLS * DH, S])
    with ExitStack() as a:
        o_c = g.sb("o_cmp", [P, 4 * H_NSA, DH], ctx=a)
        gates = g.sb("nsa_gates", [P, NT, 12], ctx=a)
        p2 = g.sb("p2", [P, NT, W2], ctx=a)
        with ExitStack() as b:
            hT = g.sb("h3T", [P, 2, KD, S], F32R, ctx=b)
            norm_stage(g, "mix2", io["norm_mix_2"], hT)
            project2_stage(g, io, hT, p2)
        with ExitStack() as b:
            cols = g.sb("cols2", [P, N_COLS // 2, S], ctx=b)
            with ExitStack() as c:
                qk = g.sb("qk2", [P, NT, N_COLS * DH], ctx=c)
                heads2_stage(g, io, p2, qk, gates)
                turn_stage(g, "heads2", qk, N_COLS * DH, cols, dram=colsT)
            compressed_stage(g, io, cols[:, N_COLS // 2 - 1, :], colsT, o_c)
        o_nsa = g.sb("o_nsa", [P, NT, 2 * H_NSA * DH], ctx=a)
        o_dil = g.sb("o_dil", [P, NT, H_DIL * DH], ctx=a)
        cat = g.sb("cat", [P, NT, D_CAT], ctx=a)
        stats = g.sb("dil_stats", [P, 2, 4 * H_DIL], ctx=a)
        aq, ak = io["const_alibi_q"], io["const_alibi_k"]

        def causal(i, t):
            return g.mask[:, 0, 384:512], t * P
        for j, (nm, kh) in enumerate((("sel", K_SEL), ("win", K_WIN))):
            attention_stage(g, nm, H_NSA, [(colsT, DH, lambda h: (h + Q_NSA) * DH), (aq, 2, lambda h: (h + H_DIL) * 2)],
                            [(colsT, DH, lambda h, kh=kh: h * 0 + kh * DH), (ak, 2, lambda h: h * 0)],
                            lambda b, h, j=j: p2[:, b, C2_KV + (3 + 2 * j) * DH:C2_KV + (4 + 2 * j) * DH],
                            lambda t, h, j=j: o_nsa[:, t, bass.ds(h * DH + 256 * j, DH)], causal)
        attention_stage(g, "dil", H_DIL, [(colsT, DH, lambda h: (h + Q_DIL) * DH), (aq, 2, lambda h: h * 2)],
                        [(colsT, DH, lambda h: (h + K_DIL) * DH), (ak, 2, lambda h: h * 0)],
                        lambda b, h: p2[:, b, bass.ds(h * DH + C2_B + 768, DH)],
                        lambda t, h: o_dil[:, t, bass.ds(h * DH, DH)],
                        lambda i, t: (g.mask[:, bass.ds(i + 2, 1), 384 - t * P:512].rearrange("p a s -> p (a s)"), 0),
                        stats=stats)
        stick_stage(g, H_SB, [(colsT, DH, lambda h: (h + Q_SB) * DH)], [(colsT, DH, lambda h: (h + K_SB) * DH)],
                    lambda b, h: p2[:, b, bass.ds(h * DH + C2_C + 768, DH)],
                    lambda t, h: cat[:, t, bass.ds(h * DH + 384, DH)],
                    lambda i, t: (g.mask[:, 1, 384:512], t * P))
        gather_heads_stage(g, o_c, o_nsa, o_dil, stats, gates, cat)
        if "cat" in dbg:
            dump(g, dbg["cat"].rearrange("(t p) d -> p t d", p=P), cat[:], "dump_cat")
        with ExitStack() as b:
            catT = g.sb("catT", [P, 2, D_CAT // P, S], F32R, ctx=b)
            turn_parts_stage(g, "catturn", cat, D_CAT, catT)
            add_product_stage(g, "out2", catT, io["w_out_2"][0], D_CAT // P)
    if "x4" in dbg:
        dump(g, dbg["x4"].rearrange("(t p) d -> p t d", p=P), g.x[:], "dump_x4")
    with ExitStack() as a:
        u = g.sb("hidden2", [P, FF // P, S], ctx=a)
        with ExitStack() as b:
            hT = g.sb("h4T", [P, 2, KD, S], F32R, ctx=b)
            norm_stage(g, "mlp2", io["norm_mlp_2"], hT)
            mlp_up_stage(g, io, hT, u)
        mlp_down_stage(g, io, u, out)


def build(nc, io, out, dbg={}, upto=9):
    with ExitStack() as ctx:
        g = Ctx(nc, ctx)
        g.ps = ctx.enter_context(nc.psum_tensor("ps", [P, 8, 512], F32))
        g.x = g.sb("x", [P, NT, D])
        g.ident = g.sb("ident", [P, P])
        g.identb = g.sb("identb", [P, P], BF16)
        g.tri = g.sb("tri", [P, P])
        g.ones = g.sb("ones", [P, P])
        g.mask = g.sb("mask", [P, 5, 512], BF16)
        g.iota = g.sb("iota", [P, P + 8])
        g.ropec = g.sb("ropec", [P, 2])
        with ExitStack() as b1:
            g.mod = g.sb("mod", [P, 6 * D], ctx=b1)
            setup_stage(g, io)
            block1_mixer(g, io, dbg)
            if "x1" in dbg:
                dump(g, dbg["x1"].rearrange("(t p) d -> p t d", p=P), g.x[:], "dump_x1")
            if upto >= 2:
                moe(g, io, dbg)
        if upto >= 2:
            norm_stage(g, "final1", io["g_final"].rearrange("(a d) -> a d", a=1), None, out_x=True)
            if "x3" in dbg:
                dump(g, dbg["x3"].rearrange("(t p) d -> p t d", p=P), g.x[:], "dump_x3")
        if upto >= 3:
            block2(g, io, dbg, out)
        else:
            dump(g, out.rearrange("(t p) d -> p t d", p=P), g.x[:], "stored_x")


_INS = ["x", "c", "positions", "w_mod", "b_mod", "g_mix_norm", "w_in", "b_forget", "g_q_lat", "w_q_up", "g_kv_lat",
        "w_kv_up", "w_o_mla", "w_o_fox", "w_out", "g_ffn_norm", "w_router", "b_router", "w_exp_gate", "w_exp_up",
        "w_exp_down", "w_sh_gate", "w_sh_up", "w_sh_down", "g_final", "norm_mix_2", "norm_mlp_2", "w_in_2",
        "qk_gain_nsa_2", "qk_gain_dil_2", "cmp_pe_2", "cmp_w1_2", "cmp_w2_2", "w_out_2", "w_up_2", "w_down_2"]


def constants():
    import numpy as np
    f = np.float32
    q = np.arange(P)[:, None]
    dist = q - (np.arange(512)[None, :] - 384)
    keep = [dist >= 0, dist > 0, (dist >= 0) & (dist <= 128), (dist >= 0) & (dist % 4 == 0), (dist >= 0) & (dist % 16 == 0)]
    mask = np.stack([np.where(m, 0, NEG) for m in keep], axis=1).astype(f)
    freq = np.power(f(10000.0), -(np.arange(16, dtype=f) / f(16)))
    rope = np.stack([freq[np.arange(P) % 16], np.where(np.arange(P) % 32 < 16, -1, 1)], axis=1).astype(f)
    iota = np.concatenate([np.broadcast_to(np.arange(P), (P, P)), np.arange(P)[:, None] + P * np.arange(8)[None]], axis=1).astype(f)
    slopes = np.exp2(f(-8.0) * np.arange(1, 11, dtype=f) / f(10)).astype(f)
    t = np.arange(S, dtype=f)
    alibi_q = np.stack([-slopes[:, None] * t, np.broadcast_to(slopes[:, None], (10, S))], axis=1).astype(f)
    alibi_k = np.stack([np.ones(S), t]).astype(f)
    ends = 16 * np.arange(32) + 31
    alibi_c = np.stack([np.ones(32), ends]).astype(f)
    tok = np.arange(S).reshape(NT, P).T[:, :, None]
    seen = ((tok >= ends) & (np.arange(32) < N_CMP))
    cmp_mask = np.stack([seen.astype(f), np.where(seen, 0, NEG).astype(f)], axis=1)
    return {"const_ident": np.eye(P, dtype=f), "const_tri": np.triu(np.ones((P, P), f), 1), "const_mask": mask,
            "const_rope": rope, "const_iota": iota, "const_alibi_q": alibi_q.reshape(20, S), "const_alibi_k": alibi_k,
            "const_alibi_c": alibi_c, "const_cmp_mask": cmp_mask.astype(f),
            "const_assignments": (np.arange(TOPK * S, dtype=np.int32).reshape(TOPK, NT, P).transpose(2, 1, 0)).copy(),
            "const_pad_rows": TOPK * S + np.arange((BLOCKS + 4) * P, dtype=np.int32)[:, None]}


def kernel(**inputs):
    import numpy as _np
    import concourse.bacc as _bacc
    from concourse.bass_utils import run_bass_kernel_spmd as _run

    nc = _bacc.Bacc("TRN2", target_bir_lowering=False, num_devices=1)
    arrays, io = {}, {}
    for name, a in [(n, inputs[n]) for n in _INS] + list(constants().items()):
        a = _np.ascontiguousarray(a)
        arrays[f"in_{name}"] = a
        io[name] = nc.dram_tensor(f"in_{name}", a.shape, mybir.dt.from_np(a.dtype), kind="ExternalInput").ap()
    out = nc.dram_tensor("out_0", (S, D), F32, kind="ExternalOutput").ap()
    build(nc, io, out)
    r = _run(nc, [arrays], core_ids=[0])
    return r.results[0]["out_0"].reshape(1, S, D)
```

```python
from contextlib import ExitStack, contextmanager

import concourse.bass as bass
from concourse import mybir

F32 = mybir.dt.float32
F32R = mybir.dt.float32r
BF16 = mybir.dt.bfloat16
I32 = mybir.dt.int32
U32 = mybir.dt.uint32
ACT = mybir.ActivationFunctionType
ALU = mybir.AluOpType
AX = mybir.AxisListType

P = 128
S = 512
NT = S // P
D = 1024
KD = D // P
EPS = 1e-6
NEG = -1e30

H1 = 8
Q_LORA, KV_LORA, ROPE, NOPE, DH = 256, 128, 32, 64, 64
HW = H1 * DH
C_KV, C_KR, C_FQ = 256, 384, 416
C_FK, C_FV, C_FL, C_GA = 928, 1440, 1952, 1960

E = 64
NG = 8
TOPG = 4
TOPK = 6
F = 256
BLOCKS = S * TOPK // P + E
ROUTED_SCALE = 2.5

H_NSA, H_DIL, H_SB = 4, 6, 6
N_CMP = (S - 32) // 16 + 1
W2 = 2956
C2_KV, C2_G, C2_B, C2_C = 256, 640, 652, 1804
D_CAT = 768
FF = 4 * D


class Chain:

    def __init__(self, eng, sem):
        self.eng, self.sem, self.base, self.n = eng, sem, 0, 0

    def __call__(self, ins):
        self.n += 1
        ins.then_inc(self.sem, 1)
        self.eng.wait_ge(self.sem, self.base + self.n)


class Ctx:

    def __init__(self, nc, ctx):
        self.nc, self.ctx, self.stage_sems = nc, ctx, []

    def sem(self, name):
        self.stage_sems.append(self.nc.alloc_semaphore(name))
        return self.stage_sems[-1]

    @contextmanager
    def stage(self):
        with ExitStack() as st:
            yield st
        self.nc.clear_and_free_semaphores(self.stage_sems)
        self.stage_sems = []
        self.nc.all_engine_barrier()

    def sb(self, name, shape, dt=F32, ctx=None):
        return (ctx or self.ctx).enter_context(self.nc.sbuf_tensor(name, shape, dt))

    def dram(self, name, shape, dt=F32):
        return self.nc.dram_tensor(name, shape, dt).ap()


def bcast_rows(row, n):
    return row.broadcast_to([P, n])


def split_product(nc, out, left, right, start, stop):
    for i, (a, b) in enumerate(((0, 0), (0, 1), (1, 0))):
        mm = nc.tensor.matmul(out, left[a], right[b], start=start and i == 0, stop=stop and i == 2)
    return mm


def low_part(nc, dst, x, high):
    return nc.vector.tensor_tensor(dst, x, high.bitcast(F32), ALU.subtract)


class SplitWeights:

    def __init__(self, g, name, ctx, kt=4):
        self.nc = g.nc
        self.raw = g.sb(name + "_raw", [P, 2, kt, 512], ctx=ctx)
        self.parts = g.sb(name + "_parts", [P, 2, 2, kt, 512], F32R, ctx=ctx)
        self.s_raw = [g.sem(f"{name}_loaded{i}") for i in range(2)]
        self.s_high = g.sem(name + "_high_ready")
        self.s_low = g.sem(name + "_low_ready")

    def load(self, eng, src, base, u, width=512):
        at_least(eng, self.s_high, base, u - 1)
        at_least(eng, self.s_low, base, u - 1)
        eng.dma_start(self.raw[:, u % 2, :, 0:width], src).then_inc(self.s_raw[u % 2], 16)

    def high(self, act, base, u, s_used, per_slab, width=512):
        act.wait_ge(self.s_raw[u % 2], 8 * base + 16 * (u // 2) + 16)
        at_least(act, s_used, per_slab * base, per_slab * (u - 1))
        self.nc.scalar.copy(self.parts[:, u % 2, 0, :, 0:width], self.raw[:, u % 2, :, 0:width]).then_inc(self.s_high, 1)

    def low(self, dve, base, u, s_used, per_slab, width=512):
        dve.wait_ge(self.s_high, base + u + 1)
        at_least(dve, s_used, per_slab * base, per_slab * (u - 1))
        low_part(self.nc, self.parts[:, u % 2, 1, :, 0:width], self.raw[:, u % 2, :, 0:width],
                 self.parts[:, u % 2, 0, :, 0:width]).then_inc(self.s_low, 1)

    def ready(self, pe, base, u):
        pe.wait_ge(self.s_high, base + u + 1)
        pe.wait_ge(self.s_low, base + u + 1)

    def at(self, u, k, c0, c1):
        return [self.parts[:, u % 2, a, k, c0:c1] for a in range(2)]


def parts_of(cols, k, c0=0, c1=S):
    return [cols[:, a, k, c0:c1] for a in range(2)]


def setup_stage(g, io):
    nc = g.nc
    NS = 2 * D // 512
    with g.stage() as st:
        w = g.sb("modw", [P, NS, KD, 512], ctx=st)
        ccol = g.sb("ccol", [P, 2, KD], ctx=st)
        cond = g.sb("cond", [P, KD, P], ctx=st)
        maskf = g.sb("maskf", [P, 5, 512], ctx=st)
        s_c = g.sem("c_loaded")
        s_const = g.sem("const_loaded")
        s_w = [g.sem(f"modw_loaded{i}") for i in range(NS)]
        s_sig = g.sem("cond_sigmoid")
        s_cond = g.sem("cond_ready")
        s_ps = g.sem("mod_psum_ready")
        s_dve = g.sem("setup_dve_steps")
        wmod = io["w_mod"][0].rearrange("(k p) n -> p k n", p=P)
        block = st.enter_context(nc.Block())

        @block.sync
        def _(sp):
            sp.dma_start(ccol[:, 0, :], io["c"].rearrange("a (k p) -> p (a k)", p=P),
                         allow_slow_non_contiguous=True).then_inc(s_c, 16)
            for i in range(NS):
                sp.dma_start(w[:, i], wmod[:, :, i * 512:i * 512 + 512]).then_inc(s_w[i], 16)

        @block.gpsimd
        def _(pool):
            pool.dma_start(g.mod[:, 0:2 * D], bcast_rows(io["b_mod"][:, 0:2 * D], 2 * D)).then_inc(s_const, 16)
            pool.dma_start(g.ident[:], io["const_ident"]).then_inc(s_const, 16)
            pool.dma_start(g.tri[:], io["const_tri"]).then_inc(s_const, 16)
            pool.dma_start(maskf[:], io["const_mask"]).then_inc(s_const, 16)
            pool.dma_start(g.iota[:], io["const_iota"]).then_inc(s_const, 16)
            pool.dma_start(g.ropec[:], io["const_rope"]).then_inc(s_const, 16)
            pool.dma_start(g.x[:], io["x"][0].rearrange("(t p) d -> p t d", p=P)).then_inc(s_const, 16)

        @block.scalar
        def _(act):
            act.wait_ge(s_c, 16)
            nc.scalar.activation(ccol[:, 1, :], ccol[:, 0, :], ACT.Sigmoid).then_inc(s_sig, 1)

        @block.vector
        def _(dve):
            link = Chain(dve, s_dve)
            dve.wait_ge(s_c, 16)
            dve.wait_ge(s_sig, 1)
            link(nc.vector.tensor_tensor(g.cond[:], ccol[:, 0, :], ccol[:, 1, :], ALU.mult))
            nc.vector.tensor_copy(cond[:], g.cond[:].unsqueeze(2).broadcast_to([P, KD, P])).then_inc(s_cond, 1)
            nc.vector.memset(g.ones[:], 1.0)
            dve.wait_ge(s_const, 16 * 7)
            nc.vector.tensor_copy(g.mask[:], maskf[:])
            nc.vector.tensor_copy(g.identb[:], g.ident[:])
            for i in range(NS):
                dve.wait_ge(s_ps, i + 1)
                m = g.mod[:, i * 512:i * 512 + 512]
                nc.vector.tensor_tensor(m, g.ps[:, i, :], m, ALU.add)

        @block.tensor
        def _(pe):
            pe.wait_ge(s_cond, 1)
            for i in range(NS):
                pe.wait_ge(s_w[i], 16)
                for k in range(KD):
                    mm = nc.tensor.matmul(g.ps[:, i, :], cond[:, k, :], w[:, i, k, :], start=k == 0, stop=k == KD - 1)
                mm.then_inc(s_ps, 1)


class ModRest:

    def __init__(self, g, io, name, first):
        self.g, self.io, self.name, self.slabs = g, io, name, range(first, first + 2 * D, 512)

    def reserve(self, st):
        self.w = self.g.sb(self.name, [P, 2, KD, 512], ctx=st)
        self.s_w = [self.g.sem(f"{self.name}_loaded{i}") for i in range(2)]
        self.s_acc = self.g.sem(self.name + "_steps")

    def run(self, pool):
        nc, g = self.g.nc, self.g
        wmod = self.io["w_mod"][0].rearrange("(k p) n -> p k n", p=P)
        link = Chain(pool, self.s_acc)
        slabs = self.slabs

        def fetch(i):
            pool.dma_start(self.w[:, i % 2], wmod[:, :, slabs[i]:slabs[i] + 512]).then_inc(self.s_w[i % 2], 16)

        fetch(0)
        fetch(1)
        for i, c in enumerate(slabs):
            pool.wait_ge(self.s_w[i % 2], 16 * (i // 2) + 16)
            w = self.w[:, i % 2]
            link(nc.gpsimd.tensor_tensor(w, w, g.cond[:].unsqueeze(2).broadcast_to([P, KD, 512]), ALU.mult))
            link(nc.gpsimd.tensor_tensor(w[:, 0:4, :], w[:, 0:4, :], w[:, 4:8, :], ALU.add))
            link(nc.gpsimd.tensor_tensor(w[:, 0:2, :], w[:, 0:2, :], w[:, 2:4, :], ALU.add))
            link(nc.gpsimd.tensor_tensor(g.mod[:, c:c + 512], w[:, 0, :], w[:, 1, :], ALU.add))
            if i + 2 < len(slabs):
                fetch(i + 2)


def mod_rest_stage(g, io):
    nc = g.nc
    with g.stage() as st:
        bias = g.sb("mod_bias", [P, 4 * D], ctx=st)
        s_b = g.sem("mod_bias_loaded")
        s_ps = g.sem("mod_rest_ready")
        block = st.enter_context(nc.Block())

        @block.sync
        def _(sp):
            sp.dma_start(bias[:], bcast_rows(io["b_mod"][:, 2 * D:6 * D], 4 * D)).then_inc(s_b, 16)

        @block.tensor
        def _(pe):
            for i in range(8):
                c = 2 * D + 512 * i
                nc.tensor.matmul(g.ps[:, i, :], g.ones[:], g.mod[:, c:c + 512], start=True, stop=True).then_inc(s_ps, 1)

        @block.vector
        def _(dve):
            dve.wait_ge(s_b, 16)
            for i in range(8):
                dve.wait_ge(s_ps, i + 1)
                c = 2 * D + 512 * i
                nc.vector.tensor_tensor(g.mod[:, c:c + 512], g.ps[:, i, :], bias[:, 512 * i:512 * i + 512], ALU.add)


def norm_stage(g, name, gain, hT, scale=None, shift=None, h_dram=None, out_x=None):
    nc = g.nc
    with g.stage() as st:
        h = g.x if out_x else g.sb(name + "_h", [P, NT, D], ctx=st)
        junk = g.sb(name + "_junk", [P, NT, D], ctx=st) if out_x else h
        gain_sb = g.sb(name + "_gain", [P, D], ctx=st)
        stat = g.sb(name + "_stat", [P, 3, NT], ctx=st)
        s_gain = g.sem(name + "_gain_loaded")
        s_sq = g.sem(name + "_squares_summed")
        s_ms = g.sem(name + "_mean_square_ready")
        s_h = g.sem(name + "_h_ready")
        s_t = g.sem(name + "_turned")
        s_hi = g.sem(name + "_high_ready")
        s_out = g.sem(name + "_h_stored")
        s_dve = g.sem(name + "_dve_steps")
        block = st.enter_context(nc.Block())

        @block.sync
        def _(sp):
            sp.dma_start(gain_sb[:], bcast_rows(gain, D)).then_inc(s_gain, 16)
            if h_dram is not None:
                for t in range(NT):
                    sp.wait_ge(s_h, t + 1)
                    sp.dma_start(h_dram[t * P:t * P + P, :], h[:, t, :]).then_inc(s_out, 16)
                sp.wait_ge(s_out, 16 * NT)

        @block.scalar
        def _(act):
            for t in range(NT):
                nc.scalar.activation(junk[:, t, :], g.x[:, t, :], ACT.Square,
                                     accum_out=stat[:, 0, t:t + 1]).then_inc(s_sq, 1)
            act.wait_ge(s_ms, 1)
            nc.scalar.activation(stat[:, 2, :], stat[:, 1, :], ACT.Sqrt).then_inc(s_sq, 1)
            if not out_x:
                for b in range(2 * NT):
                    act.wait_ge(s_t, b + 1)
                    k, t = 4 * (b % 2), b // 2
                    nc.scalar.copy(hT[:, 0, k:k + 4, t * P:t * P + P],
                                   g.ps[:, b, :].rearrange("p (k q) -> p k q", k=4)).then_inc(s_hi, 1)

        @block.vector
        def _(dve):
            link = Chain(dve, s_dve)
            dve.wait_ge(s_gain, 16)
            if scale is not None:
                link(nc.vector.scalar_tensor_tensor(gain_sb[:], scale, 1.0, gain_sb[:], ALU.add, ALU.mult))
            dve.wait_ge(s_sq, NT)
            nc.vector.tensor_scalar(stat[:, 1, :], stat[:, 0, :], 1.0 / D, EPS, ALU.mult, ALU.add).then_inc(s_ms, 1)
            dve.wait_ge(s_sq, NT + 1)
            link(nc.vector.reciprocal(stat[:, 1, :], stat[:, 2, :]))
            for t in range(NT):
                ins = nc.vector.scalar_tensor_tensor(h[:, t, :], g.x[:, t, :], stat[:, 1, t:t + 1], gain_sb[:],
                                                     ALU.mult, ALU.mult)
                if shift is not None:
                    link(ins)
                    ins = nc.vector.tensor_tensor(h[:, t, :], h[:, t, :], shift, ALU.add)
                ins.then_inc(s_h, 1)
            if not out_x:
                for b in range(2 * NT):
                    dve.wait_ge(s_hi, b + 1)
                    k, t = 4 * (b % 2), b // 2
                    low_part(nc, hT[:, 1, k:k + 4, t * P:t * P + P], g.ps[:, b, :].rearrange("p (k q) -> p k q", k=4),
                             hT[:, 0, k:k + 4, t * P:t * P + P])

        if not out_x:
            @block.tensor
            def _(pe):
                for t in range(NT):
                    pe.wait_ge(s_h, t + 1)
                    for half in range(2):
                        for k in range(4):
                            c = (4 * half + k) * P
                            tr = nc.tensor.transpose(g.ps[:, 2 * t + half, k * P:k * P + P], h[:, t, c:c + P], g.ident[:])
                        tr.then_inc(s_t, 1)


def turn_stage(g, name, rows, width, cols, dram=None):
    nc = g.nc
    n = width // P
    with g.stage() as st:
        s_t = g.sem(name + "_turned")
        s_act = g.sem(name + "_act_evacuated")
        s_dve = g.sem(name + "_dve_evacuated")
        s_st = g.sem(name + "_stored")
        block = st.enter_context(nc.Block())

        if dram is not None:
            @block.sync
            def _(sp):
                for k in range(n):
                    sp.wait_ge((s_act, s_dve)[k % 2], k // 2 + 1)
                    sp.dma_start(dram[k * P:k * P + P, :], cols[:, k, :]).then_inc(s_st, 16)
                sp.wait_ge(s_st, 16 * n)

        @block.tensor
        def _(pe):
            for k in range(n):
                if k >= 8:
                    pe.wait_ge((s_act, s_dve)[k % 2], (k - 8) // 2 + 1)
                for t in range(NT):
                    tr = nc.tensor.transpose(g.ps[:, k % 8, t * P:t * P + P], rows[:, t, k * P:k * P + P], g.ident[:])
                tr.then_inc(s_t, 1)

        @block.scalar
        def _(act):
            for k in range(0, n, 2):
                act.wait_ge(s_t, k + 1)
                nc.scalar.copy(cols[:, k, :], g.ps[:, k % 8, :]).then_inc(s_act, 1)

        @block.vector
        def _(dve):
            for k in range(1, n, 2):
                dve.wait_ge(s_t, k + 1)
                nc.vector.tensor_copy(cols[:, k, :], g.ps[:, k % 8, :]).then_inc(s_dve, 1)


def turn_parts_stage(g, name, rows, width, cols):
    nc = g.nc
    n = width // P
    with g.stage() as st:
        s_t = g.sem(name + "_turned")
        s_hi = g.sem(name + "_high_ready")
        block = st.enter_context(nc.Block())

        @block.tensor
        def _(pe):
            for k in range(n):
                for t in range(NT):
                    tr = nc.tensor.transpose(g.ps[:, k, t * P:t * P + P], rows[:, t, k * P:k * P + P], g.ident[:])
                tr.then_inc(s_t, 1)

        @block.scalar
        def _(act):
            for k in range(n):
                act.wait_ge(s_t, k + 1)
                nc.scalar.copy(cols[:, 0, k, :], g.ps[:, k, :]).then_inc(s_hi, 1)

        @block.vector
        def _(dve):
            for k in range(n):
                dve.wait_ge(s_hi, k + 1)
                low_part(nc, cols[:, 1, k, :], g.ps[:, k, :], cols[:, 0, k, :])


def project1_stage(g, io, hT, t1):
    nc = g.nc
    w_in = io["w_in"][0].rearrange("(k p) n -> p k n", p=P)
    slabs = [("rows", 0, 416), ("cols", C_FQ, 512), ("cols", C_FK, 512), ("rows", C_FV, 512)]
    slabs += [("rows", C_GA + 512 * i, 512) for i in range(4)]
    with g.stage() as st:
        w = SplitWeights(g, "win", st)
        small = g.sb("wsmall", [P, KD, 72], ctx=st)
        smallp = g.sb("wsmall_parts", [P, 2, KD, 72], F32R, ctx=st)
        qk = g.sb("fox_qk", [P, NT, 512], ctx=st)
        bf = g.sb("bforget", [8, 1], ctx=st)
        s_small = g.sem("wsmall_loaded")
        s_smallp = g.sem("wsmall_parts_ready")
        s_ps = g.sem("proj1_ready")
        s_act = g.sem("proj1_act_evacuated")
        s_dve = g.sem("proj1_dve_evacuated")
        s_st = g.sem("fox_qk_stored")
        n = len(slabs)

        def owner(s, t):
            return "act" if s >= 4 or t < 2 else "dve"

        def done(s, t):
            who = owner(s, t)
            count = sum(owner(a, b) == who for a in range(n) for b in range(NT) if (a, b) <= (s, t))
            return (s_act if who == "act" else s_dve), count

        def evacuate(copy, s, t):
            src = g.ps[:, (s % 2) * 4 + t, :]
            if s == 0:
                return copy(t1["lat"][:, t, :], src[:, 0:416])
            if s == 1:
                return nc.scalar.mul(qk[:, t, :], src, DH ** -0.5) if owner(s, t) == "act" else \
                    nc.vector.tensor_scalar(qk[:, t, :], src, DH ** -0.5, None, ALU.mult)
            if s == 2:
                return copy(qk[:, t, :], src)
            if s == 3:
                return copy(t1["v_fox"][:, t, :], src)
            c = (s - 4) * 512
            return nc.scalar.activation(t1["gates"][:, t, c:c + 512], src, ACT.Sigmoid)

        block = st.enter_context(nc.Block())

        @block.sync
        def _(sp):
            for s, (_, c, width) in enumerate(slabs):
                for half in range(2):
                    w.load(sp, w_in[:, 4 * half:4 * half + 4, c:c + width], 0, 2 * s + half, width)
                if s in (3, 4):
                    for eng_done in (done(s - 2, 1), done(s - 2, 3)):
                        sp.wait_ge(*eng_done)
                    dst = (t1["fq_dram"], t1["fk_dram"])[s - 3].rearrange("(t p) s -> p t s", p=P)
                    sp.dma_start(dst, qk[:]).then_inc(s_st, 16)
            sp.wait_ge(s_st, 32)

        @block.gpsimd
        def _(pool):
            pool.dma_start(small[:, :, 0:8], w_in[:, :, C_FL:C_FL + 8]).then_inc(s_small, 16)
            pool.dma_start(small[:, :, 8:40], w_in[:, :, C_KR:C_KR + 32]).then_inc(s_small, 16)
            pool.dma_start(small[:, :, 40:56], w_in[:, :, C_KR + 16:C_KR + 32]).then_inc(s_small, 16)
            pool.dma_start(small[:, :, 56:72], w_in[:, :, C_KR:C_KR + 16]).then_inc(s_small, 16)
            pool.dma_start(bf[:], io["b_forget"].rearrange("a h -> h a"), allow_slow_non_contiguous=True).then_inc(s_small, 16)

        @block.tensor
        def _(pe):
            for s, (kind, _, width) in enumerate(slabs):
                for half in range(2):
                    q = 2 * s + half
                    w.ready(pe, 0, q)
                    for t in range(NT):
                        if s >= 2 and half == 0:
                            pe.wait_ge(*done(s - 2, t))
                        for j in range(4):
                            k = 4 * half + j
                            if kind == "rows":
                                left, right = parts_of(hT, k, t * P, t * P + P), w.at(q, j, 0, width)
                            else:
                                left, right = w.at(q, j, t * P, t * P + P), parts_of(hT, k)
                            mm = split_product(nc, g.ps[:, (s % 2) * 4 + t, 0:width], left, right, k == 0, k == KD - 1)
                        mm.then_inc(s_ps, 1)
            pe.wait_ge(s_smallp, 2)
            for j, (c, m) in enumerate([(0, 8), (8, 32), (40, 32)]):
                pe.wait_ge(*done(n - 2, j))
                for k in range(KD):
                    mm = split_product(nc, g.ps[0:m, j, :], parts_of(smallp, k, c, c + m), parts_of(hT, k), k == 0, k == KD - 1)
                mm.then_inc(s_ps, 1)

        @block.scalar
        def _(act):
            for half in range(2):
                w.high(act, 0, half, s_ps, 4, slabs[0][2])
            for s in range(n):
                for half in range(2):
                    if s + 1 < n:
                        w.high(act, 0, 2 * s + 2 + half, s_ps, 4, slabs[s + 1][2])
                for t in range(NT):
                    if owner(s, t) == "act":
                        act.wait_ge(s_ps, 8 * s + 4 + t + 1)
                        if s == 2 and t == 0:
                            act.wait_ge(s_st, 16)
                        evacuate(nc.scalar.copy, s, t).then_inc(s_act, 1)

        @block.vector
        def _(dve):
            for half in range(2):
                w.low(dve, 0, half, s_ps, 4, slabs[0][2])
            dve.wait_ge(s_small, 80)
            nc.vector.tensor_copy(smallp[:, 0], small[:]).then_inc(s_smallp, 1)
            dve.wait_ge(s_smallp, 1)
            low_part(nc, smallp[:, 1], small[:], smallp[:, 0]).then_inc(s_smallp, 1)
            for s in range(n):
                for half in range(2):
                    if s + 1 < n:
                        w.low(dve, 0, 2 * s + 2 + half, s_ps, 4, slabs[s + 1][2])
                for t in range(2, NT):
                    if owner(s, t) == "dve":
                        dve.wait_ge(s_ps, 8 * s + 4 + t + 1)
                        if s == 2 and t == 2:
                            dve.wait_ge(s_st, 16)
                        evacuate(nc.vector.tensor_copy, s, t).then_inc(s_dve, 1)
            dve.wait_ge(s_ps, 8 * n + 3)
            nc.vector.tensor_scalar(t1["fl"][:], g.ps[0:8, 0, :], bf[:, 0:1], None, ALU.add)
            nc.vector.tensor_copy(t1["kr"][:, 0, :], g.ps[0:32, 1, :])
            nc.vector.tensor_copy(t1["kr"][:, 1, :], g.ps[0:32, 2, :])


def latent_stage(g, io, t1):
    nc = g.nc
    lat, rope = t1["lat"], t1["rope"]
    with g.stage() as st:
        junk = g.sb("lat_junk", [P, NT, 384], ctx=st)
        gains = g.sb("lat_gain", [P, 384], ctx=st)
        stat = g.sb("lat_stat", [P, 3, 2 * NT], ctx=st)
        posi = g.sb("posi", [P, S], I32, ctx=st)
        pos = g.sb("posf", [P, S], ctx=st)
        ang = g.sb("ang", [P, 4, S], ctx=st)
        fg = g.sb("forget", [8, 6, S], ctx=st)
        kpe = g.sb("kpe", [32, 2, S], ctx=st)
        s_ld = g.sem("latent_loads")
        s_sq = g.sem("latent_squares")
        s_ms = g.sem("latent_mean_square")
        s_n = g.sem("latent_normed")
        s_t = g.sem("latent_turned")
        s_ang = g.sem("angles_ready")
        s_sin = g.sem("sines_ready")
        s_fa = g.sem("forget_abs_ready")
        s_fl = g.sem("forget_log_ready")
        s_acts = g.sem("latent_act_steps")
        s_k = g.sem("kpe_and_forget_ready")
        s_st = g.sem("kpe_and_forget_stored")
        s_dve = g.sem("latent_dve_steps")
        TWO_PI = 6.283185307179586
        C1 = 6.28125
        C2 = 0.0019350051879882812
        C3 = TWO_PI - C1 - C2
        MAGIC = 12582912.0
        block = st.enter_context(nc.Block())

        @block.sync
        def _(sp):
            sp.dma_start(posi[:], bcast_rows(io["positions"], S)).then_inc(s_ld, 16)
            sp.dma_start(gains[:, 0:256], bcast_rows(io["g_q_lat"], 256)).then_inc(s_ld, 16)
            sp.dma_start(gains[:, 256:384], bcast_rows(io["g_kv_lat"], 128)).then_inc(s_ld, 16)
            sp.wait_ge(s_k, 1)
            sp.dma_start(t1["kpe_dram"], kpe[:, 0, :]).then_inc(s_st, 16)
            sp.wait_ge(s_k, 2)
            sp.dma_start(t1["fqa_dram"][:, 0, :], fg[:, 4, :]).then_inc(s_st, 16)
            sp.dma_start(t1["fqa_dram"][:, 1, :], fg[:, 3, :]).then_inc(s_st, 16)
            sp.dma_start(t1["fka_dram"][:, 0, :], fg[:, 3, :]).then_inc(s_st, 16)
            sp.dma_start(t1["fka_dram"][:, 1, :], fg[:, 5, :]).then_inc(s_st, 16)
            sp.wait_ge(s_st, 80)

        @block.scalar
        def _(act):
            for t in range(NT):
                nc.scalar.activation(junk[:, t, 0:256], lat[:, t, 0:256], ACT.Square, accum_out=stat[:, 0, t:t + 1])
                nc.scalar.activation(junk[:, t, 256:384], lat[:, t, 256:384], ACT.Square,
                                     accum_out=stat[:, 0, NT + t:NT + t + 1]).then_inc(s_sq, 1)
            act.wait_ge(s_ms, 1)
            nc.scalar.activation(stat[:, 2, :], stat[:, 1, :], ACT.Sqrt).then_inc(s_sq, 1)
            act.wait_ge(s_fa, 1)
            nc.scalar.activation(fg[:, 1, :], fg[:, 0, :], ACT.Exp).then_inc(s_acts, 1)
            act.wait_ge(s_acts, 1)
            nc.scalar.activation(fg[:, 2, :], fg[:, 1, :], ACT.Ln, bias=1.0).then_inc(s_fl, 1)
            act.wait_ge(s_ang, 1)
            nc.scalar.activation(rope[:, 0, :], ang[:, 0, :], ACT.Sin).then_inc(s_sin, 1)
            nc.scalar.activation(rope[:, 1, :], ang[:, 1, :], ACT.Sin).then_inc(s_sin, 1)

        @block.vector
        def _(dve):
            link = Chain(dve, s_dve)
            dve.wait_ge(s_ld, 48)
            dve.wait_ge(s_sq, NT)
            link(nc.vector.tensor_scalar(stat[:, 1, 0:NT], stat[:, 0, 0:NT], 1.0 / Q_LORA, EPS, ALU.mult, ALU.add))
            nc.vector.tensor_scalar(stat[:, 1, NT:2 * NT], stat[:, 0, NT:2 * NT], 1.0 / KV_LORA, EPS,
                                    ALU.mult, ALU.add).then_inc(s_ms, 1)
            nc.vector.scalar_tensor_tensor(fg[:, 0, :], t1["fl"][:], -1.0, t1["fl"][:], ALU.mult, ALU.min).then_inc(s_fa, 1)
            link(nc.vector.tensor_copy(pos[:], posi[:]))
            link(nc.vector.tensor_scalar(ang[:, 2, :], pos[:], g.ropec[:, 0:1], None, ALU.mult))
            for row, turn in ((0, 0.25), (1, 0.0)):
                link(nc.vector.tensor_scalar(ang[:, 3, :], ang[:, 2, :], 1.0 / TWO_PI, turn, ALU.mult, ALU.add))
                link(nc.vector.tensor_scalar(ang[:, 3, :], ang[:, 3, :], MAGIC, None, ALU.add))
                link(nc.vector.tensor_scalar(ang[:, 3, :], ang[:, 3, :], -MAGIC, None, ALU.add))
                link(nc.vector.scalar_tensor_tensor(ang[:, row, :], ang[:, 3, :], -C1, ang[:, 2, :], ALU.mult, ALU.add))
                link(nc.vector.scalar_tensor_tensor(ang[:, row, :], ang[:, 3, :], -C2, ang[:, row, :], ALU.mult, ALU.add))
                link(nc.vector.scalar_tensor_tensor(ang[:, row, :], ang[:, 3, :], -C3, ang[:, row, :], ALU.mult, ALU.add))
                if turn:
                    link(nc.vector.tensor_scalar(ang[:, row, :], ang[:, row, :], TWO_PI / 4, None, ALU.add))
                last = nc.vector.tensor_scalar(ang[:, row, :], ang[:, row, :], 3.1415925, -3.1415925, ALU.min, ALU.max)
            last.then_inc(s_ang, 1)
            dve.wait_ge(s_fl, 1)
            link(nc.vector.scalar_tensor_tensor(fg[:, 0, :], t1["fl"][:], 0.0, fg[:, 2, :], ALU.min, ALU.subtract))
            link(nc.vector.memset(fg[:, 3, :], 1.0))
            link(nc.vector.tensor_tensor_scan(fg[:, 4, :], fg[:, 3, :], fg[:, 0, :], 0.0, ALU.mult, ALU.add))
            link(nc.vector.tensor_scalar(fg[:, 5, :], fg[:, 4, :], -1.0, None, ALU.mult))
            dve.wait_ge(s_sq, NT + 1)
            link(nc.vector.reciprocal(stat[:, 1, :], stat[:, 2, :]))
            for t in range(NT):
                nc.vector.scalar_tensor_tensor(lat[:, t, 0:256], lat[:, t, 0:256], stat[:, 1, t:t + 1],
                                               gains[:, 0:256], ALU.mult, ALU.mult)
                nc.vector.scalar_tensor_tensor(lat[:, t, 256:384], lat[:, t, 256:384], stat[:, 1, NT + t:NT + t + 1],
                                               gains[:, 256:384], ALU.mult, ALU.mult).then_inc(s_n, 1)
            dve.wait_ge(s_sin, 2)
            link(nc.vector.tensor_scalar(rope[:, 1, :], rope[:, 1, :], g.ropec[:, 1:2], None, ALU.mult))
            link(nc.vector.tensor_tensor(kpe[:, 0, :], t1["kr"][:, 0, :], rope[0:32, 0, :], ALU.mult))
            link(nc.vector.tensor_tensor(kpe[:, 1, :], t1["kr"][:, 1, :], rope[0:32, 1, :], ALU.mult))
            nc.vector.tensor_tensor(kpe[:, 0, :], kpe[:, 0, :], kpe[:, 1, :], ALU.add).then_inc(s_k, 2)
            for k in range(3):
                dve.wait_ge(s_t, k + 1)
                nc.vector.tensor_copy(t1["latT"][:, k, :], g.ps[:, k, :])

        @block.tensor
        def _(pe):
            pe.wait_ge(s_n, NT)
            for k in range(3):
                for t in range(NT):
                    tr = nc.tensor.transpose(g.ps[:, k, t * P:t * P + P], lat[:, t, k * P:k * P + P], g.ident[:])
                tr.then_inc(s_t, 1)


def up_stage(g, io, t1):
    nc = g.nc
    MLA_SCALE = 96 ** -0.5
    with g.stage() as st:
        wqn = g.sb("wqn", [P, 2, H1, NOPE], ctx=st)
        wqp = g.sb("wqp", [P, 2, H1, ROPE], ctx=st)
        wqs = g.sb("wqs", [P, 2, H1, ROPE], ctx=st)
        wk = g.sb("wk", [P, H1, NOPE], ctx=st)
        wv = g.sb("wv", [P, H1, DH], ctx=st)
        qn = g.sb("qn", [P, 4, S], ctx=st)
        kn = g.sb("kn", [P, 4, S], ctx=st)
        qp = g.sb("qp", [P, 2, 2, S], ctx=st)
        s_w = g.sem("up_weights_loaded")
        s_ps = g.sem("up_ready")
        s_act = g.sem("up_act_evacuated")
        s_dve = g.sem("up_dve_evacuated")
        s_rot = g.sem("rotated")
        s_dst = g.sem("up_dve_steps")
        s_st = g.sem("up_stored")
        wq = io["w_q_up"][0].rearrange("(k p) (h c) -> p k h c", p=P, c=96)
        wkv = io["w_kv_up"][0].rearrange("p (h c) -> p h c", c=128)
        latT = t1["latT"]
        block = st.enter_context(nc.Block())

        @block.sync
        def _(sp):
            sp.dma_start(wk[:], wkv[:, :, 0:64]).then_inc(s_w, 16)
            sp.dma_start(wv[:], wkv[:, :, 64:128]).then_inc(s_w, 16)
            for k in range(2):
                sp.dma_start(wqn[:, k], wq[:, k, :, 0:64]).then_inc(s_w, 16)
                sp.dma_start(wqp[:, k], wq[:, k, :, 64:96]).then_inc(s_w, 16)
                sp.dma_start(wqs[:, k, :, 0:16], wq[:, k, :, 80:96]).then_inc(s_w, 16)
                sp.dma_start(wqs[:, k, :, 16:32], wq[:, k, :, 64:80]).then_inc(s_w, 16)
            sp.wait_ge(s_act, 4)
            sp.dma_start(t1["qn_dram"].rearrange("(t p) s -> p t s", p=P), qn[:]).then_inc(s_st, 16)
            sp.wait_ge(s_act, 8)
            sp.dma_start(t1["kn_dram"].rearrange("(t p) s -> p t s", p=P), kn[:]).then_inc(s_st, 16)
            sp.wait_ge(s_rot, 2)
            sp.dma_start(t1["qp_dram"].rearrange("(t p) s -> p t s", p=P), qp[:, :, 0, :]).then_inc(s_st, 16)
            sp.wait_ge(s_st, 48)

        @block.tensor
        def _(pe):
            pe.wait_ge(s_w, 160)
            for m in range(4):
                for k in range(2):
                    mm = nc.tensor.matmul(g.ps[:, m, :], wqn[:, k, 2 * m:2 * m + 2, :], latT[:, k, :],
                                          start=k == 0, stop=k == 1)
                mm.then_inc(s_ps, 1)
            for m in range(4):
                wt = (wqp, wqs)[m % 2]
                h = 4 * (m // 2)
                for k in range(2):
                    mm = nc.tensor.matmul(g.ps[:, 4 + m, :], wt[:, k, h:h + 4, :], latT[:, k, :],
                                          start=k == 0, stop=k == 1)
                mm.then_inc(s_ps, 1)
            for m in range(4):
                pe.wait_ge(s_act, m + 1)
                nc.tensor.matmul(g.ps[:, m, :], wk[:, 2 * m:2 * m + 2, :], latT[:, 2, :],
                                 start=True, stop=True).then_inc(s_ps, 1)
            for t in range(NT):
                pe.wait_ge(s_rot, t // 2 + 1)
                nc.tensor.matmul(g.ps[:, 4 + t, :], latT[:, 2, t * P:t * P + P], wv[:],
                                 start=True, stop=True).then_inc(s_ps, 1)

        @block.scalar
        def _(act):
            for m in range(4):
                act.wait_ge(s_ps, m + 1)
                nc.scalar.mul(qn[:, m, :], g.ps[:, m, :], MLA_SCALE).then_inc(s_act, 1)
            for m in range(4):
                act.wait_ge(s_ps, 9 + m)
                nc.scalar.copy(kn[:, m, :], g.ps[:, m, :]).then_inc(s_act, 1)

        @block.vector
        def _(dve):
            link = Chain(dve, s_dst)
            for m in range(2):
                dve.wait_ge(s_ps, 4 + 2 * m + 2)
                link(nc.vector.scalar_tensor_tensor(qp[:, m, 0, :], g.ps[:, 4 + 2 * m, :], MLA_SCALE,
                                                    t1["rope"][:, 0, :], ALU.mult, ALU.mult))
                link(nc.vector.scalar_tensor_tensor(qp[:, m, 1, :], g.ps[:, 5 + 2 * m, :], MLA_SCALE,
                                                    t1["rope"][:, 1, :], ALU.mult, ALU.mult))
                nc.vector.tensor_tensor(qp[:, m, 0, :], qp[:, m, 0, :], qp[:, m, 1, :], ALU.add).then_inc(s_rot, 1)
            for t in range(NT):
                dve.wait_ge(s_ps, 13 + t)
                nc.vector.tensor_copy(t1["v_mla"][:, t, :], g.ps[:, 4 + t, :])


def at_least(eng, sem, base, value):
    if not isinstance(base, int) or base + value > 0:
        eng.wait_ge(sem, base + value)


def turns(eng, heads, body):
    n = heads // 2
    body(0, 0, False)
    if n > 1:
        with eng.Fori(1, n) as i:
            body(i, 8 * i, False)
    body(n, 8 * n, True)


def lagging(base, u, lag, drain):
    if (isinstance(base, int) and base == 0 and u < lag) or (drain and u >= lag):
        return None
    return (u - lag) % 8, u < lag


def fetch_heads(g, eng, heads, q, kk, q_parts, k_parts, s_qk, s_s):
    def fetch(head, j):
        for dst, parts in ((q, q_parts), (kk, k_parts)):
            r = 0
            for src, n, row in parts:
                eng.dma_start(dst[r:r + n, j, :], src[bass.ds(row(head), n), :]).then_inc(s_qk[j], 16)
                r += n

    fetch(0, 0)
    fetch(1, 1)
    with eng.Fori(1, heads // 2) as i:
        for j in range(2):
            eng.wait_ge(s_s, 8 * i - 4 + 4 * j)
            fetch(2 * i + j, j)


def attention_stage(g, name, heads, q_parts, k_parts, v, out, mask, stats=None, beside=None):
    nc = g.nc
    K = sum(n for _, n, _ in q_parts)
    LT, LV = 2, 4
    with g.stage() as st:
        q = g.sb(name + "_q", [K, 2, S], ctx=st)
        kk = g.sb(name + "_k", [K, 2, S], ctx=st)
        p = g.sb(name + "_p", [P, 4, S], ctx=st)
        pt = g.sb(name + "_pt", [P, 4, NT, P], ctx=st)
        stats = g.sb(name + "_stats", [P, 2, 4 * heads], ctx=st) if stats is None else stats
        rl = g.sb(name + "_rl", [P, 8], ctx=st)
        s_qk = [g.sem(f"{name}_qk_loaded{i}") for i in range(2)]
        s_s = g.sem(name + "_scores_ready")
        s_m = g.sem(name + "_max_ready")
        s_p = g.sem(name + "_probs_ready")
        s_t = g.sem(name + "_turned")
        s_pt = g.sem(name + "_turned_copied")
        s_o = g.sem(name + "_values_ready")
        s_rl = g.sem(name + "_reciprocal_ready")
        s_od = g.sem(name + "_out_done")
        loads = 16 * (len(q_parts) + len(k_parts))
        if beside:
            beside.reserve(st)
        block = st.enter_context(nc.Block())

        @block.sync
        def _(sp):
            fetch_heads(g, sp, heads, q, kk, q_parts, k_parts, s_qk, s_s)

        if beside:
            @block.gpsimd
            def _(pool):
                beside.run(pool)

        @block.tensor
        def _(pe):
            def body(i, base, drain):
                for u in range(8):
                    j, t = u // 4, u % 4
                    n = (t + 1) * P
                    if not drain:
                        if t == 0:
                            pe.wait_ge(s_qk[j], loads * i + loads)
                        at_least(pe, s_m, base, u - 3)
                        at_least(pe, s_p, base, u - 3)
                        mk, first = mask(i, t)
                        nc.tensor.matmul(g.ps[:, u % 4, 0:n], q[:, j, t * P:t * P + P], kk[:, j, 0:n],
                                         start=True, stop=False)
                        nc.tensor.matmul(g.ps[:, u % 4, first:n], g.identb[:], mk,
                                         start=False, stop=True).then_inc(s_s, 1)
                    if (at := lagging(base, u, LT, drain)) is not None:
                        a = at[0]
                        at_least(pe, s_p, base, u - LT + 1)
                        at_least(pe, s_pt, base, u - LT - 1)
                        for b in range(a % 4 + 1):
                            tr = nc.tensor.transpose(g.ps[:, 4 + a % 2, b * P:b * P + P], p[:, a % 4, b * P:b * P + P],
                                                     g.ident[:])
                        tr.then_inc(s_t, 1)
                    if (at := lagging(base, u, LV, drain)) is not None:
                        a, head = at[0], 2 * i + at[0] // 4 - 2 * at[1]
                        at_least(pe, s_pt, base, u - LV + 1)
                        at_least(pe, s_od, base, u - LV - 1)
                        for b in range(a % 4 + 1):
                            mm = nc.tensor.matmul(g.ps[:, 6 + a % 2, 0:DH], pt[:, a % 4, b, :], v(b, head),
                                                  start=b == 0, stop=b == a % 4)
                        mm.then_inc(s_o, 1)
            turns(pe, heads, body)

        @block.scalar
        def _(act):
            def body(i, base, drain):
                for u in range(8):
                    n = (u % 4 + 1) * P
                    if not drain:
                        at_least(act, s_t, base, u - 3)
                        at_least(act, s_m, base, u + 1)
                        col = bass.ds(8 * i + u, 1)
                        nc.scalar.activation(p[:, u % 4, 0:n], g.ps[:, u % 4, 0:n], ACT.Exp, bias=stats[:, 0, col],
                                             accum_out=stats[:, 1, col]).then_inc(s_p, 1)
                    if (at := lagging(base, u, LT, drain)) is not None:
                        a = at[0]
                        at_least(act, s_t, base, u - LT + 1)
                        at_least(act, s_o, base, u - LT - 3)
                        nc.scalar.copy(pt[:, a % 4, 0:a % 4 + 1, :],
                                       g.ps[:, 4 + a % 2, 0:(a % 4 + 1) * P].rearrange("p (b s) -> p b s", s=P)
                                       ).then_inc(s_pt, 1)
            turns(act, heads, body)

        @block.vector
        def _(dve):
            def body(i, base, drain):
                for u in range(8):
                    if not drain:
                        at_least(dve, s_s, base, u + 1)
                        nc.vector.tensor_reduce(stats[:, 0, bass.ds(8 * i + u, 1)], g.ps[:, u % 4, 0:(u % 4 + 1) * P],
                                                AX.X, ALU.max, negate=True).then_inc(s_m, 1)
                    if (at := lagging(base, u, LV, drain)) is not None:
                        a, head = at[0], 2 * i + at[0] // 4 - 2 * at[1]
                        at_least(dve, s_p, base, u - LV + 1)
                        nc.vector.reciprocal(rl[:, a:a + 1], stats[:, 1, bass.ds(8 * i + u - LV, 1)]).then_inc(s_rl, 1)
                        at_least(dve, s_rl, base, u - LV + 1)
                        at_least(dve, s_o, base, u - LV + 1)
                        nc.vector.tensor_scalar(out(a % 4, head), g.ps[:, 6 + a % 2, 0:DH], rl[:, a:a + 1], None,
                                                ALU.mult).then_inc(s_od, 1)
            turns(dve, heads, body)


def merge_stage(g, io, oT, gates, merged):
    nc = g.nc
    with g.stage() as st:
        w = SplitWeights(g, "wo", st)
        part = g.sb("merge_part", [P, 2, 2, 512], ctx=st)
        s_ps = g.sem("merge_ready")
        s_ev = g.sem("merge_evacuated")
        s_dve = g.sem("merge_dve_steps")
        block = st.enter_context(nc.Block())

        @block.sync
        def _(sp):
            for q in range(4):
                n, j = q // 2, q % 2
                src = io[("w_o_mla", "w_o_fox")[j]][0].rearrange("(k p) n -> p k n", p=P)
                w.load(sp, src[:, :, n * 512:n * 512 + 512], 0, q)

        @block.tensor
        def _(pe):
            for q in range(4):
                n, j = q // 2, q % 2
                w.ready(pe, 0, q)
                for t in range(NT):
                    if n:
                        pe.wait_ge(s_ev, t + 1)
                    for k in range(4):
                        mm = split_product(nc, g.ps[:, 4 * j + t, :], parts_of(oT, 4 * j + k, t * P, t * P + P),
                                           w.at(q, k, 0, 512), k == 0, k == 3)
                    mm.then_inc(s_ps, 1)

        @block.scalar
        def _(act):
            for q in range(4):
                w.high(act, 0, q, s_ps, NT)

        @block.vector
        def _(dve):
            link = Chain(dve, s_dve)
            for q in range(3):
                w.low(dve, 0, q, s_ps, NT)
            for n in range(2):
                for t in range(NT):
                    dve.wait_ge(s_ps, NT * (2 * n + 1) + t + 1)
                    for j in range(2):
                        col = j * D + n * 512
                        ins = nc.vector.tensor_tensor(part[:, t % 2, j, :], g.ps[:, 4 * j + t, :],
                                                      gates[:, t, col:col + 512], ALU.mult)
                        if j == 0:
                            link(ins)
                    link(ins)
                    nc.vector.tensor_tensor(merged[:, t, n * 512:n * 512 + 512], part[:, t % 2, 0, :],
                                            part[:, t % 2, 1, :], ALU.add).then_inc(s_ev, 1)
                if n == 0:
                    w.low(dve, 0, 3, s_ps, NT)


def add_product_stage(g, name, colsT, w_dram, kt, gate=None):
    nc = g.nc
    kh = kt // 2
    w_d = w_dram.rearrange("(k p) n -> p k n", p=P)
    with g.stage() as st:
        w = SplitWeights(g, name + "_w", st, kh)
        part = g.sb(name + "_part", [P, 4, 512], ctx=st)
        s_ps = g.sem(name + "_ready")
        s_dve = g.sem(name + "_dve_steps")
        block = st.enter_context(nc.Block())

        @block.sync
        def _(sp):
            for q in range(4):
                n, c = q // 2, q % 2
                w.load(sp, w_d[:, kh * c:kh * c + kh, n * 512:n * 512 + 512], 0, q)

        @block.tensor
        def _(pe):
            for q in range(4):
                n, c = q // 2, q % 2
                w.ready(pe, 0, q)
                for t in range(NT):
                    for j in range(kh):
                        k = kh * c + j
                        mm = split_product(nc, g.ps[:, 4 * n + t, :], parts_of(colsT, k, t * P, t * P + P),
                                           w.at(q, j, 0, 512), k == 0, k == kt - 1)
                    mm.then_inc(s_ps, 1)

        @block.scalar
        def _(act):
            for q in range(4):
                w.high(act, 0, q, s_ps, NT)

        @block.vector
        def _(dve):
            link = Chain(dve, s_dve)
            for q in range(4):
                w.low(dve, 0, q, s_ps, NT)
            for n in range(2):
                for t in range(NT):
                    xs = g.x[:, t, n * 512:n * 512 + 512]
                    dve.wait_ge(s_ps, NT * (2 * n + 1) + t + 1)
                    if gate is None:
                        nc.vector.tensor_tensor(xs, g.ps[:, 4 * n + t, :], xs, ALU.add)
                    else:
                        link(nc.vector.tensor_tensor(part[:, t, :], g.ps[:, 4 * n + t, :],
                                                     gate[:, n * 512:n * 512 + 512], ALU.mult))
                        nc.vector.tensor_tensor(xs, part[:, t, :], xs, ALU.add)


def dump(g, dst, src, nm):
    nc = g.nc
    with g.stage() as st:
        s_out = g.sem(nm)
        block = st.enter_context(nc.Block())

        @block.sync
        def _(sp):
            sp.dma_start(dst, src).then_inc(s_out, 16)
            sp.wait_ge(s_out, 16)


def block1_mixer(g, io, dbg):
    nc = g.nc
    with ExitStack() as a:
        fq, fk = g.dram("fq_T", [HW, S]), g.dram("fk_T", [HW, S])
        fqa, fka = g.dram("fq_extra", [H1, 2, S]), g.dram("fk_extra", [H1, 2, S])
        qn, kn, qp, kpe = (g.dram(n, [r, S]) for n, r in (("qn_T", HW), ("kn_T", HW), ("qp_T", H1 * ROPE), ("kpe_T", ROPE)))
        t1 = {"fq_dram": fq, "fk_dram": fk, "fqa_dram": fqa, "fka_dram": fka, "qn_dram": qn, "kn_dram": kn,
              "qp_dram": qp, "kpe_dram": kpe}
        gates = t1["gates"] = g.sb("gates", [P, NT, 2 * D], ctx=a)
        with ExitStack() as b:
            t1["v_fox"] = g.sb("v_fox", [P, NT, HW], ctx=b)
            t1["v_mla"] = g.sb("v_mla", [P, NT, HW], ctx=b)
            with ExitStack() as c:
                t1["lat"] = g.sb("lat", [P, NT, 416], ctx=c)
                t1["fl"] = g.sb("fl", [8, S], ctx=c)
                t1["kr"] = g.sb("kr", [32, 2, S], ctx=c)
                with ExitStack() as d:
                    hT = g.sb("h1T", [P, 2, KD, S], F32R, ctx=d)
                    norm_stage(g, "mix1", io["g_mix_norm"], hT, scale=g.mod[:, D:2 * D], shift=g.mod[:, 0:D])
                    project1_stage(g, io, hT, t1)
                t1["rope"] = g.sb("rope", [P, 2, S], ctx=c)
                t1["latT"] = g.sb("latT", [P, 3, S], ctx=c)
                latent_stage(g, io, t1)
                up_stage(g, io, t1)
            o = g.sb("o1", [P, NT, 2 * HW], ctx=b)

            def causal(i, t):
                return g.mask[:, 0, 384:512], t * P
            attention_stage(g, "mla", H1, [(qn, NOPE, lambda h: h * NOPE), (qp, ROPE, lambda h: h * ROPE)],
                            [(kn, NOPE, lambda h: h * NOPE), (kpe, ROPE, lambda h: h * 0)],
                            lambda b, h: t1["v_mla"][:, b, bass.ds(h * DH, DH)],
                            lambda t, h: o[:, t, bass.ds(h * DH, DH)], causal, beside=ModRest(g, io, "modw_second", 2 * D))
            fqa2, fka2 = fqa.rearrange("h r s -> (h r) s"), fka.rearrange("h r s -> (h r) s")
            attention_stage(g, "fox", H1, [(fq, DH, lambda h: h * DH), (fqa2, 2, lambda h: h * 2)],
                            [(fk, DH, lambda h: h * DH), (fka2, 2, lambda h: h * 2)],
                            lambda b, h: t1["v_fox"][:, b, bass.ds(h * DH, DH)],
                            lambda t, h: o[:, t, bass.ds(h * DH + HW, DH)], causal,
                            beside=ModRest(g, io, "modw_third", 4 * D))
            if "o1" in dbg:
                dump(g, dbg["o1"].rearrange("(t p) d -> p t d", p=P), o[:], "dump_o1")
            mod_rest_stage(g, io)
            oT = g.sb("o1T", [P, 2, KD, S], F32R, ctx=b)
            turn_parts_stage(g, "o1turn", o, 2 * HW, oT)
            merged = o
            merge_stage(g, io, oT, gates, merged)
            turn_parts_stage(g, "mergeturn", merged, D, oT)
            add_product_stage(g, "out1", oT, io["w_out"][0], KD, gate=g.mod[:, 2 * D:3 * D])


def shared_stage(g, io, hT, acc):
    nc = g.nc
    with g.stage() as st:
        w = g.sb("sh_w", [P, 3, 2 * D], ctx=st)
        wp = g.sb("sh_w_parts", [P, 3, 2, 2 * D], F32R, ctx=st)
        sg = g.sb("sh_sig", [P, 2, S], ctx=st)
        hid = g.sb("sh_hid", [P, 2, S], ctx=st)
        hidp = g.sb("sh_hid_parts", [P, 2, 2, S], F32R, ctx=st)
        s_w = [g.sem(f"shared_weights_loaded{i}") for i in range(3)]
        s_hi = g.sem("shared_high_ready")
        s_lo = g.sem("shared_low_ready")
        s_ps = g.sem("shared_ready")
        s_sg = g.sem("shared_sigmoid")
        s_h = g.sem("shared_hidden_ready")
        s_dve = g.sem("shared_dve_steps")
        block = st.enter_context(nc.Block())

        @block.sync
        def _(sp):
            for i, key in enumerate(("w_sh_gate", "w_sh_up", "w_sh_down")):
                sp.dma_start(w[:, i, :].rearrange("p (k n) -> p k n", k=(KD, KD, 2)[i]),
                             io[key][0].rearrange("(k p) n -> p k n", p=P)).then_inc(s_w[i], 16)

        @block.tensor
        def _(pe):
            for m in range(4):
                pe.wait_ge(s_hi, m // 2 + 1)
                pe.wait_ge(s_lo, m // 2 + 1)
                for k in range(KD):
                    c = k * F + (m % 2) * P
                    mm = split_product(nc, g.ps[:, m, :], [wp[:, m // 2, a, c:c + P] for a in range(2)], parts_of(hT, k),
                                       k == 0, k == KD - 1)
                mm.then_inc(s_ps, 1)
            pe.wait_ge(s_hi, 3)
            pe.wait_ge(s_lo, 3)
            pe.wait_ge(s_h, 2)
            for c in range(8):
                t, n = c // 2, c % 2
                for k in range(2):
                    col = k * D + n * 512
                    mm = split_product(nc, g.ps[:, c, :], parts_of(hidp, k, t * P, t * P + P),
                                       [wp[:, 2, a, col:col + 512] for a in range(2)], k == 0, k == 1)
                mm.then_inc(s_ps, 1)

        @block.scalar
        def _(act):
            for i in range(3):
                act.wait_ge(s_w[i], 16)
                nc.scalar.copy(wp[:, i, 0, :], w[:, i, :]).then_inc(s_hi, 1)
            for m in range(2):
                act.wait_ge(s_ps, m + 1)
                nc.scalar.activation(sg[:, m, :], g.ps[:, m, :], ACT.Sigmoid).then_inc(s_sg, 1)
            for c in range(0, 8, 2):
                act.wait_ge(s_ps, 5 + c)
                nc.scalar.copy(acc[:, c // 2, 0:512], g.ps[:, c, :])

        @block.vector
        def _(dve):
            link = Chain(dve, s_dve)
            for i in range(3):
                dve.wait_ge(s_hi, i + 1)
                low_part(nc, wp[:, i, 1, :], w[:, i, :], wp[:, i, 0, :]).then_inc(s_lo, 1)
            for m in range(2):
                dve.wait_ge(s_sg, m + 1)
                link(nc.vector.tensor_tensor(sg[:, m, :], g.ps[:, m, :], sg[:, m, :], ALU.mult))
                dve.wait_ge(s_ps, m + 3)
                link(nc.vector.tensor_tensor(hid[:, m, :], g.ps[:, 2 + m, :], sg[:, m, :], ALU.mult))
                link(nc.vector.tensor_copy(hidp[:, 0, m, :], hid[:, m, :]))
                low_part(nc, hidp[:, 1, m, :], hid[:, m, :], hidp[:, 0, m, :]).then_inc(s_h, 1)
            for c in range(1, 8, 2):
                dve.wait_ge(s_ps, 5 + c)
                nc.vector.tensor_copy(acc[:, c // 2, 512:1024], g.ps[:, c, :])


def route_stage(g, io, hT, r):
    nc = g.nc
    with g.stage() as st:
        w = g.sb("wrouter", [P, KD, E], ctx=st)
        wp = g.sb("wrouter_parts", [P, 2, KD, E], F32R, ctx=st)
        br = g.sb("brouter", [P, E], ctx=st)
        sc = g.sb("scores", [P, NT, E], ctx=st)
        ch = g.sb("choice", [P, NT, E], ctx=st)
        m8 = g.sb("top8", [P, NT, NG, 8], ctx=st)
        gs = g.sb("group_score", [P, NT, NG], ctx=st)
        gi = g.sb("group_index", [P, NT, 8], U32, ctx=st)
        gf = g.sb("group_index_f", [P, NT, 8], ctx=st)
        keep = g.sb("group_keep", [P, NT, NG], ctx=st)
        ei = g.sb("expert_index", [P, NT, 8], U32, ctx=st)
        ef = g.sb("expert_index_f", [P, NT, 8], ctx=st)
        oh = g.sb("onehot", [P, NT, TOPK, E], ctx=st)
        tmp = g.sb("route_tmp", [P, TOPK, E], ctx=st)
        A = g.sb("assigned", [P, NT, E], ctx=st)
        cnt = g.sb("counts", [P, 5, E], ctx=st)
        row = g.sb("expert_row", [P, NT, E], ctx=st)
        gsum = g.sb("gate_sum", [P, 2, NT], ctx=st)
        be = g.sb("block_expert", [P, E + 2], ctx=st)
        asg = g.sb("assignment_ids", [P, NT, TOPK], I32, ctx=st)
        lists = g.sb("row_lists", [P, BLOCKS + 4], I32, ctx=st)
        rb = g.sb("row_blocks", [BLOCKS + 4, P], I32, ctx=st)
        rbf = g.sb("row_blocks_f", [BLOCKS + 4, P], ctx=st)
        s_ld = g.sem("route_loads")
        s_wp = g.sem("wrouter_parts_ready")
        s_ps = g.sem("route_psum_ready")
        s_sc = g.sem("scores_ready")
        s_A = g.sem("assignments_ready")
        s_dve = g.sem("route_dve_steps")
        s_pad = g.sem("pad_rows_written")
        s_dest = g.sem("destinations_ready")
        s_scat = g.sem("rows_scattered")
        s_be = g.sem("block_experts_ready")
        s_bes = g.sem("block_experts_stored")
        s_rb = g.sem("row_blocks_loaded")
        s_rbf = g.sem("row_blocks_float")
        block = st.enter_context(nc.Block())
        NB = BLOCKS + 4

        @block.sync
        def _(sp):
            sp.dma_start(w[:], io["w_router"][0].rearrange("(k p) n -> p k n", p=P)).then_inc(s_ld, 16)
            sp.dma_start(br[:], bcast_rows(io["b_router"], E)).then_inc(s_ld, 16)
            sp.dma_start(asg[:], io["const_assignments"]).then_inc(s_ld, 16)
            sp.dma_start(r["row_asg"], io["const_pad_rows"]).then_inc(s_pad, 16)
            sp.wait_ge(s_be, 1)
            sp.dma_start(r["be_dram"], r["be_col"][0:NB, :]).then_inc(s_bes, 16)
            sp.dma_start(r["n_dram"], r["n_col"][0:1, :]).then_inc(s_bes, 16)
            sp.wait_ge(s_bes, 32)
            sp.dma_start(r["be_row"][:], r["be_dram"].rearrange("b a -> a b")).then_inc(s_bes, 16)
            sp.wait_ge(s_scat, 16 * NT * TOPK)
            sp.dma_start(rb[:], r["row_asg"].rearrange("(b p) a -> b (p a)", p=P)).then_inc(s_rb, 16)
            sp.wait_ge(s_bes, 48)

        @block.gpsimd
        def _(pool):
            pool.wait_ge(s_dest, 1)
            pool.wait_ge(s_ld, 48)
            pool.wait_ge(s_pad, 16)
            for t in range(NT):
                for k in range(TOPK):
                    pool.indirect_dma_start(
                        r["row_asg"], bass.IndirectOffsetOnAxis(ap=r["dest"][:, t, k:k + 1], axis=0),
                        asg[:, t, k:k + 1], None).then_inc(s_scat, 16)

        @block.tensor
        def _(pe):
            pe.wait_ge(s_wp, 2)
            for t in range(NT):
                for k in range(KD):
                    mm = split_product(nc, g.ps[:, t, 0:E], parts_of(hT, k, t * P, t * P + P), parts_of(wp, k, 0, E),
                                       k == 0, k == KD - 1)
                mm.then_inc(s_ps, 1)
            pe.wait_ge(s_A, 1)
            for t in range(NT):
                for b in range(t + 1):
                    mm = nc.tensor.matmul(g.ps[:, 4 + t, 0:E], g.tri[:] if b == t else g.ones[:], A[:, b, :],
                                          start=b == 0, stop=b == t)
                mm.then_inc(s_ps, 1)
            for b in range(NT):
                mm = nc.tensor.matmul(g.ps[:, 0, 0:E], g.ones[:], A[:, b, :], start=b == 0, stop=b == NT - 1)
            mm.then_inc(s_ps, 1)
            pe.wait_ge(s_rbf, 1)
            nc.tensor.transpose(g.ps[:, 1, 0:NB], rbf[:], g.ident[0:NB, 0:NB]).then_inc(s_ps, 1)

        @block.scalar
        def _(act):
            for t in range(NT):
                act.wait_ge(s_ps, t + 1)
                nc.scalar.activation(sc[:, t, :], g.ps[:, t, 0:E], ACT.Sigmoid).then_inc(s_sc, 1)

        @block.vector
        def _(dve):
            v = nc.vector
            link = Chain(dve, s_dve)
            dve.wait_ge(s_ld, 48)
            v.tensor_copy(wp[:, 0], w[:]).then_inc(s_wp, 1)
            dve.wait_ge(s_wp, 1)
            low_part(nc, wp[:, 1], w[:], wp[:, 0]).then_inc(s_wp, 1)
            for t in range(NT):
                dve.wait_ge(s_sc, t + 1)
                link(v.tensor_tensor(ch[:, t, :], sc[:, t, :], br[:], ALU.add))
                for n in range(NG):
                    ins = v.max(m8[:, t, n, :], ch[:, t, n * 8:n * 8 + 8])
                link(ins)
            link(v.tensor_tensor(gs[:], m8[:, :, :, 0], m8[:, :, :, 1], ALU.add))
            for t in range(NT):
                link(v.max(m8[:, t, 0, :], gs[:, t, :]))
                link(v.max_index(gi[:, t, :], m8[:, t, 0, :], gs[:, t, :]))
            link(v.tensor_copy(gf[:], gi[:]))
            link(v.memset(keep[:], 0.0))
            for t in range(NT):
                for k in range(TOPG):
                    link(v.scalar_tensor_tensor(keep[:, t, :], g.iota[:, 0:NG], gf[:, t, k:k + 1], keep[:, t, :],
                                                ALU.is_equal, ALU.add))
            for t in range(NT):
                kb = keep[:, t, :].unsqueeze(2).broadcast_to([P, NG, E // NG])
                c3 = ch[:, t, :].rearrange("p (a b) -> p a b", a=NG)
                link(v.tensor_tensor(c3, c3, kb, ALU.mult))
            link(v.tensor_scalar(keep[:], keep[:], -1.0, -NEG, ALU.add, ALU.mult))
            for t in range(NT):
                kb = keep[:, t, :].unsqueeze(2).broadcast_to([P, NG, E // NG])
                c3 = ch[:, t, :].rearrange("p (a b) -> p a b", a=NG)
                link(v.tensor_tensor(c3, c3, kb, ALU.add))
            for t in range(NT):
                link(v.max(m8[:, t, 0, :], ch[:, t, :]))
                link(v.max_index(ei[:, t, :], m8[:, t, 0, :], ch[:, t, :]))
            link(v.tensor_copy(ef[:], ei[:]))
            for t in range(NT):
                for k in range(TOPK):
                    ins = v.tensor_scalar(oh[:, t, k, :], g.iota[:, 0:E], ef[:, t, k:k + 1], None, ALU.is_equal)
                link(ins)
                ins = v.tensor_reduce(A[:, t, :], oh[:, t].rearrange("p k e -> p e k"), AX.X, ALU.add)
            link(ins)
            v.memset(cnt[:, 4, :], 1.0).then_inc(s_A, 1)
            for t in range(NT):
                link(v.tensor_tensor(tmp[:], oh[:, t], sc[:, t, :].unsqueeze(1).broadcast_to([P, TOPK, E]), ALU.mult))
                link(v.tensor_reduce(r["gate"][:, t, :], tmp[:], AX.X, ALU.add))
                link(v.tensor_reduce(gsum[:, 0, t:t + 1], r["gate"][:, t, :], AX.X, ALU.add))
                link(v.reciprocal(gsum[:, 1, t:t + 1], gsum[:, 0, t:t + 1]))
                link(v.tensor_scalar(r["gate"][:, t, :], r["gate"][:, t, :], gsum[:, 1, t:t + 1], ROUTED_SCALE,
                                     ALU.mult, ALU.mult))
            dve.wait_ge(s_ps, 2 * NT + 1)
            link(v.tensor_copy(cnt[:, 0, :], g.ps[:, 0, 0:E]))
            link(v.tensor_scalar(cnt[:, 1, :], cnt[:, 0, :], 0.0, None, ALU.is_gt))
            for j in range(1, NT):
                link(v.scalar_tensor_tensor(cnt[:, 1, :], cnt[:, 0, :], float(P * j), cnt[:, 1, :], ALU.is_gt, ALU.add))
            link(v.tensor_tensor_scan(cnt[:, 2, :], cnt[:, 4, :], cnt[:, 1, :], 0.0, ALU.mult, ALU.add))
            link(v.tensor_tensor(cnt[:, 3, :], cnt[:, 2, :], cnt[:, 1, :], ALU.subtract))
            link(v.tensor_scalar(cnt[:, 3, :], cnt[:, 3, :], float(P), None, ALU.mult))
            for t in range(NT):
                link(v.tensor_tensor(row[:, t, :], g.ps[:, 4 + t, 0:E], cnt[:, 3, :], ALU.add))
                link(v.tensor_tensor(tmp[:], oh[:, t], row[:, t, :].unsqueeze(1).broadcast_to([P, TOPK, E]), ALU.mult))
                link(v.tensor_reduce(gf[:, t, 0:TOPK], tmp[:], AX.X, ALU.add))
                link(v.tensor_copy(r["dest"][:, t, :], gf[:, t, 0:TOPK]))
            v.tensor_copy(r["n_col"][:], cnt[:, 2, E - 1:E]).then_inc(s_dest, 1)
            link(v.tensor_scalar(be[:, 0:E], cnt[:, 2, :], g.iota[:, P:P + 1], None, ALU.is_le))
            link(v.tensor_reduce(be[:, E:E + 1], be[:, 0:E], AX.X, ALU.add))
            link(v.tensor_scalar(be[:, E:E + 1], be[:, E:E + 1], float(E - 1), None, ALU.min))
            v.tensor_copy(r["be_col"][:], be[:, E:E + 1]).then_inc(s_be, 1)
            dve.wait_ge(s_rb, 16)
            v.tensor_copy(rbf[:], rb[:]).then_inc(s_rbf, 1)
            dve.wait_ge(s_ps, 2 * NT + 2)
            link(v.tensor_copy(lists[:], g.ps[:, 1, 0:NB]))
            v.tensor_copy(r["row_asg_cols"][:], lists[:])
            link(v.tensor_scalar(r["row_tok"][:], lists[:], S - 1, None, ALU.bitwise_and))
            link(v.tensor_scalar(lists[:], lists[:], float(TOPK * S), 4096.0, ALU.is_ge, ALU.mult))
            v.tensor_tensor(r["row_tok"][:], r["row_tok"][:], lists[:], ALU.add)


def expert_stage(g, io, r):
    nc = g.nc
    UNROLL = 4
    STEPS = BLOCKS + 4
    KH = KD // 2
    with g.stage() as st:
        wgu = g.sb("wgu", [P, 2, KD, 2 * F], ctx=st)
        wd = g.sb("wd", [P, 2, 2, D], ctx=st)
        wgup = g.sb("wgu_parts", [P, 2, KD, 2 * F], F32R, ctx=st)
        wdp = g.sb("wd_parts", [P, 2, 2, D], F32R, ctx=st)
        idx = g.sb("row_index", [P, 2], I32, ctx=st)
        oidx = g.sb("out_index", [P, 2], U32, ctx=st)
        xg = g.sb("xg", [P, 2, D], ctx=st)
        xT = g.sb("xgT", [P, 2, 2, KD, P], F32R, ctx=st)
        sg = g.sb("exp_sig", [P, F], ctx=st)
        h = g.sb("exp_h", [P, F], ctx=st)
        hT = g.sb("exp_hT", [P, 2, 2, 2, P], F32R, ctx=st)
        y = g.sb("exp_y", [P, 2, D], ctx=st)
        s_wgu = [g.sem(f"expert_gate_up_loaded{i}") for i in range(2)]
        s_wd = [g.sem(f"expert_down_loaded{i}") for i in range(2)]
        s_hg = g.sem("gate_up_high_ready")
        s_lg = g.sem("gate_up_low_ready")
        s_hd = g.sem("down_high_ready")
        s_ld = g.sem("down_low_ready")
        s_i = g.sem("row_index_ready")
        s_oi = g.sem("out_index_ready")
        s_seen = g.sem("index_seen")
        s_zero = g.sem("row_buffers_zeroed")
        s_x = [g.sem(f"rows_gathered{i}") for i in range(2)]
        s_xt = g.sem("rows_turned")
        s_xh = g.sem("rows_turned_high_ready")
        s_xl = g.sem("rows_turned_low_ready")
        s_half = g.sem("gate_up_half_done")
        s_gu = g.sem("gate_up_done")
        s_sg = g.sem("expert_sigmoid_ready")
        s_g = g.sem("expert_gate_ready")
        s_h = g.sem("expert_hidden_ready")
        s_ht = g.sem("hidden_turned")
        s_hh = g.sem("hidden_turned_high_ready")
        s_hl = g.sem("hidden_turned_low_ready")
        s_dn = g.sem("down_done")
        s_ya = g.sem("y_act_copied")
        s_yd = g.sem("y_dve_copied")
        s_st = [g.sem(f"y_stored{i}") for i in range(2)]
        wg_d = io["w_exp_gate"][0].rearrange("e (p k) f -> e p k f", p=P)
        wu_d = io["w_exp_up"][0].rearrange("e (p k) f -> e p k f", p=P)
        wd_d = io["w_exp_down"][0].rearrange("e (p k) n -> e p k n", p=P)
        halves = [slice(0, KH), slice(KH, KD)]
        block = st.enter_context(nc.Block())

        def steps(eng, body):
            for u in range(UNROLL):
                body(u, u, True, 0)
            with eng.Fori(1, STEPS // UNROLL) as i:
                for u in range(UNROLL):
                    body(UNROLL * i + u, u, False, i)

        def used_steps(eng, step, tail):
            used = used_blocks(eng)

            def body(b, u, first, i):
                if first:
                    step(b, u, True, 0, True)
                    return
                with eng.If(b + 1 < used):
                    step(b, u, False, i, True)
                with eng.If(b + 1 == used):
                    step(b, u, False, i, False)
                with eng.If(b == used):
                    tail(b, u, False, i)
            steps(eng, body)

        def used_blocks(eng):
            return eng.value_load(r["n_col"][0:1, 0:1], min_val=24, max_val=BLOCKS)

        @block.sync
        def _(sp):
            used = used_blocks(sp)

            def fetch(b, u, wait):
                e = sp.value_load(r["be_row"][0:1, bass.ds(b, 1)], min_val=0, max_val=E - 1)
                if wait:
                    sp.wait_ge(s_hg, 2 * b - 2)
                    sp.wait_ge(s_lg, 2 * b - 2)
                s = u % 2
                sp.dma_start(wgu[:, s, :, 0:F], wg_d[bass.ds(e, 1)].rearrange("a p k f -> p (a k) f")).then_inc(s_wgu[s], 16)
                sp.dma_start(wgu[:, s, :, F:2 * F], wu_d[bass.ds(e, 1)].rearrange("a p k f -> p (a k) f")).then_inc(s_wgu[s], 16)
                if wait:
                    sp.wait_ge(s_hd, b - 1)
                    sp.wait_ge(s_ld, b - 1)
                sp.dma_start(wd[:, s], wd_d[bass.ds(e, 1)].rearrange("a p k n -> p (a k) n")).then_inc(s_wd[s], 16)

            def body(b, u, first, i):
                if first:
                    fetch(b, u, u >= 2)
                    return
                with sp.If(b < used):
                    fetch(b, u, True)
            steps(sp, body)

        @block.gpsimd
        def _(pool):
            used = used_blocks(pool)

            def rows_to_move(b):
                middle = pool.value_load(r["row_asg_cols"][P // 2:P // 2 + 1, bass.ds(b, 1)], min_val=0,
                                         max_val=TOPK * S + (BLOCKS + 4) * P)
                with pool.If(middle < TOPK * S):
                    yield P
                with pool.If(middle >= TOPK * S):
                    yield P // 2

            def gather(b, u, first):
                if not (first and u < 2):
                    pool.wait_ge(s_xt, b - 1)
                nc.gpsimd.tensor_copy(idx[:, u % 2:u % 2 + 1], r["row_tok"][:, bass.ds(b, 1)]).then_inc(s_i, 1)
                pool.wait_ge(s_i, b + 1)
                pool.sem_inc(s_seen, 1)
                for n in rows_to_move(b):
                    pool.indirect_dma_start(xg[0:n, u % 2, :], None, r["h"],
                                            bass.IndirectOffsetOnAxis(ap=idx[0:n, u % 2:u % 2 + 1], axis=0),
                                            bounds_check=S - 1, oob_is_err=False).then_inc(s_x[u % 2], 16)

            def scatter(b, u):
                pool.wait_ge(s_ya, b - 3)
                pool.wait_ge(s_yd, b - 3)
                nc.gpsimd.tensor_copy(oidx[:, u % 2:u % 2 + 1], r["row_asg_cols"][:, bass.ds(b - 4, 1)]).then_inc(s_oi, 1)
                pool.wait_ge(s_oi, b - 3)
                pool.sem_inc(s_seen, 1)
                for n in rows_to_move(b - 4):
                    pool.indirect_dma_start(r["y"], bass.IndirectOffsetOnAxis(ap=oidx[0:n, u % 2:u % 2 + 1], axis=0),
                                            y[0:n, u % 2, :], None, bounds_check=TOPK * S - 1,
                                            oob_is_err=False).then_inc(s_st[u % 2], 16)

            def body(b, u, first, i):
                if first:
                    gather(b, u, True)
                    return
                with pool.If(b < used + 4):
                    scatter(b, u)
                with pool.If(b < used):
                    gather(b, u, False)
            nc.gpsimd.memset(xg[:], 0.0).then_inc(s_zero, 1)
            pool.wait_ge(s_zero, 1)
            steps(pool, body)
            pool.wait_ge(s_st[0], ((used + 1) >> 1) * 16)
            pool.wait_ge(s_st[1], (used >> 1) * 16)

        @block.tensor
        def _(pe):
            def turn_rows(b, u, i, start):
                pe.wait_ge(s_x[u % 2], 32 * i + 16 * (u // 2) + 16)
                if not start:
                    pe.wait_ge(s_xh, b)
                    pe.wait_ge(s_xl, b)
                for k in range(KD):
                    tr = nc.tensor.transpose(g.ps[:, k // 4, (k % 4) * P:(k % 4) * P + P],
                                             xg[:, u % 2, k::KD], g.ident[:])
                tr.then_inc(s_xt, 1)

            def gate_up(b, u, half):
                pe.wait_ge(s_hg, 2 * b + half + 1)
                pe.wait_ge(s_lg, 2 * b + half + 1)
                for k in range(KH * half, KH * half + KH):
                    mm = split_product(nc, g.ps[:, 2 + u % 2, :], [xT[:, u % 2, a, k, :] for a in range(2)],
                                       [wgup[:, a, k, :] for a in range(2)], k == 0, k == KD - 1)
                return mm

            def down(b, u, first, i=0):
                pe.wait_ge(s_hd, b)
                pe.wait_ge(s_ld, b)
                pe.wait_ge(s_hh, b)
                pe.wait_ge(s_hl, b)
                if not (first and u == 1):
                    pe.wait_ge(s_ya, b - 1)
                    pe.wait_ge(s_yd, b - 1)
                for n in range(2):
                    for k in range(2):
                        mm = split_product(nc, g.ps[:, 5 + n, :], [hT[:, (u - 1) % 2, a, k, :] for a in range(2)],
                                           [wdp[:, a, k, n * 512:n * 512 + 512] for a in range(2)], k == 0, k == 1)
                mm.then_inc(s_dn, 1)

            def step(b, u, first, i, more):
                if first and u == 0:
                    turn_rows(0, 0, 0, True)
                pe.wait_ge(s_xh, b + 1)
                pe.wait_ge(s_xl, b + 1)
                if not (first and u < 2):
                    pe.wait_ge(s_h, b - 1)
                gate_up(b, u, 0).then_inc(s_half, 1)
                gate_up(b, u, 1).then_inc(s_gu, 1)
                if more:
                    turn_rows(b + 1, u + 1, i, False)
                if not (first and u == 0):
                    down(b, u, first)
                pe.wait_ge(s_h, b + 1)
                for k in range(2):
                    tr = nc.tensor.transpose(g.ps[:, 4, k * P:k * P + P], h[:, k::2], g.ident[:])
                tr.then_inc(s_ht, 1)
            used_steps(pe, step, down)

        @block.scalar
        def _(act):
            def high_gate_up(b, u, i, half, start=False):
                act.wait_ge(s_wgu[u % 2], 64 * i + 32 * (u // 2) + 32)
                if not start:
                    act.wait_ge((s_half, s_gu)[half], b)
                k = halves[half]
                nc.scalar.copy(wgup[:, 0, k, :], wgu[:, u % 2, k, :]).then_inc(s_hg, 1)

            def high_down(b, u, i, start):
                act.wait_ge(s_wd[u % 2], 32 * i + 16 * (u // 2) + 16)
                if not start:
                    act.wait_ge(s_dn, b)
                nc.scalar.copy(wdp[:, 0], wd[:, u % 2]).then_inc(s_hd, 1)

            def high_rows(b, u):
                act.wait_ge(s_xt, b + 1)
                nc.scalar.copy(xT[:, u % 2, 0], g.ps[:, 0:2, :].rearrange("p b (k q) -> p (b k) q", k=4)).then_inc(s_xh, 1)

            def copy_y(b, u, first, i):
                o = (u - 1) % 2
                act.wait_ge(s_dn, b)
                if not (first and u < 3):
                    act.wait_ge(s_st[o], 32 * i + 16 * ((u - 3) // 2) + 16)
                nc.scalar.copy(y[:, o, 0:512], g.ps[:, 5, :]).then_inc(s_ya, 1)

            def step(b, u, first, i, more):
                start = first and u == 0
                if start:
                    high_gate_up(0, 0, 0, 0, True)
                    high_rows(0, 0)
                    high_gate_up(0, 0, 0, 1, True)
                if more:
                    high_gate_up(b + 1, u + 1, i, 0)
                act.wait_ge(s_gu, b + 1)
                if not start:
                    act.wait_ge(s_g, b)
                nc.scalar.activation(sg[:], g.ps[:, 2 + u % 2, 0:F], ACT.Sigmoid).then_inc(s_sg, 1)
                if more:
                    high_rows(b + 1, u + 1)
                    high_gate_up(b + 1, u + 1, i, 1)
                high_down(b, u, i, start)
                if not start:
                    copy_y(b, u, first, i)
                act.wait_ge(s_ht, b + 1)
                nc.scalar.copy(hT[:, u % 2, 0], g.ps[:, 4, 0:2 * P].rearrange("p (k q) -> p k q", k=2)).then_inc(s_hh, 1)
            used_steps(act, step, copy_y)

        @block.vector
        def _(dve):
            def low_gate_up(b, u, half, start=False):
                dve.wait_ge(s_hg, 2 * b + half + 1)
                if not start:
                    dve.wait_ge((s_half, s_gu)[half], b)
                k = halves[half]
                low_part(nc, wgup[:, 1, k, :], wgu[:, u % 2, k, :], wgup[:, 0, k, :]).then_inc(s_lg, 1)

            def low_down(b, u, start):
                dve.wait_ge(s_hd, b + 1)
                if not start:
                    dve.wait_ge(s_dn, b)
                low_part(nc, wdp[:, 1], wd[:, u % 2], wdp[:, 0]).then_inc(s_ld, 1)

            def low_rows(b, u):
                dve.wait_ge(s_xh, b + 1)
                low_part(nc, xT[:, u % 2, 1], g.ps[:, 0:2, :].rearrange("p b (k q) -> p (b k) q", k=4),
                         xT[:, u % 2, 0]).then_inc(s_xl, 1)

            def copy_y(b, u, first, i):
                o = (u - 1) % 2
                dve.wait_ge(s_dn, b)
                if not (first and u < 3):
                    dve.wait_ge(s_st[o], 32 * i + 16 * ((u - 3) // 2) + 16)
                nc.vector.tensor_copy(y[:, o, 512:1024], g.ps[:, 6, :]).then_inc(s_yd, 1)

            def step(b, u, first, i, more):
                start = first and u == 0
                if start:
                    low_gate_up(0, 0, 0, True)
                    low_rows(0, 0)
                    low_gate_up(0, 0, 1, True)
                if more:
                    low_gate_up(b + 1, u + 1, 0)
                bank = g.ps[:, 2 + u % 2, :]
                dve.wait_ge(s_sg, b + 1)
                if not start:
                    dve.wait_ge(s_ht, b)
                nc.vector.tensor_tensor(h[:], bank[:, 0:F], sg[:], ALU.mult).then_inc(s_g, 1)
                dve.wait_ge(s_g, b + 1)
                nc.vector.tensor_tensor(h[:], bank[:, F:2 * F], h[:], ALU.mult).then_inc(s_h, 1)
                if more:
                    low_rows(b + 1, u + 1)
                    low_gate_up(b + 1, u + 1, 1)
                low_down(b, u, start)
                if not start:
                    copy_y(b, u, first, i)
                dve.wait_ge(s_hh, b + 1)
                low_part(nc, hT[:, u % 2, 1], g.ps[:, 4, 0:2 * P].rearrange("p (k q) -> p k q", k=2),
                         hT[:, u % 2, 0]).then_inc(s_hl, 1)
            used_steps(dve, step, copy_y)


def combine_stage(g, r, acc, gate_f, gain):
    nc = g.nc
    with g.stage() as st:
        yk = g.sb("yk", [P, 3, TOPK, D], ctx=st)
        junk = g.sb("final_squares", [P, D], ctx=st)
        gain_sb = g.sb("final_gain", [P, D], ctx=st)
        stat = g.sb("final_stat", [P, 4, NT], ctx=st)
        s_gain = g.sem("final_gain_loaded")
        s_y = [[g.sem(f"y_loaded{i}{h}") for h in range(2)] for i in range(3)]
        s_used = g.sem("y_added")
        s_x = g.sem("x_summed")
        s_sq = g.sem("final_squares_summed")
        s_ms = g.sem("final_mean_square_ready")
        s_rt = g.sem("final_root_ready")
        s_dve = g.sem("combine_dve_steps")
        rows = r["y"].rearrange("(k t p) d -> p t k d", t=NT, p=P)
        block = st.enter_context(nc.Block())

        @block.sync
        def _(sp):
            for t in range(NT):
                if t >= 3:
                    sp.wait_ge(s_used, TOPK * (t - 2))
                for h in range(2):
                    sp.dma_start(yk[:, t % 3, 3 * h:3 * h + 3, :], rows[:, t, 3 * h:3 * h + 3, :]).then_inc(s_y[t % 3][h], 16)
                if t == 0:
                    sp.dma_start(gain_sb[:], bcast_rows(gain, D)).then_inc(s_gain, 16)

        @block.scalar
        def _(act):
            for t in range(NT):
                act.wait_ge(s_x, t + 1)
                nc.scalar.activation(junk[:], g.x[:, t, :], ACT.Square, accum_out=stat[:, 0, t:t + 1]).then_inc(s_sq, 1)
                act.wait_ge(s_ms, t + 1)
                nc.scalar.activation(stat[:, 2, t:t + 1], stat[:, 1, t:t + 1], ACT.Sqrt).then_inc(s_rt, 1)

        @block.vector
        def _(dve):
            link = Chain(dve, s_dve)
            v = nc.vector
            for t in range(NT + 1):
                if t < NT:
                    for k in range(TOPK):
                        dve.wait_ge(s_y[t % 3][k // 3], 16 * (t // 3) + 16)
                        if k:
                            dve.wait_ge(s_used, TOPK * t + k)
                        v.scalar_tensor_tensor(acc[:, t, :], yk[:, t % 3, k, :], r["gate"][:, t, k:k + 1],
                                               acc[:, t, :], ALU.mult, ALU.add).then_inc(s_used, 1)
                if t:
                    dve.wait_ge(s_sq, t)
                    v.tensor_scalar(stat[:, 1, t - 1:t], stat[:, 0, t - 1:t], 1.0 / D, EPS,
                                    ALU.mult, ALU.add).then_inc(s_ms, 1)
                if t < NT:
                    dve.wait_ge(s_used, TOPK * t + TOPK)
                    link(v.tensor_tensor(acc[:, t, :], acc[:, t, :], gate_f, ALU.mult))
                    v.tensor_tensor(g.x[:, t, :], g.x[:, t, :], acc[:, t, :], ALU.add).then_inc(s_x, 1)
                if t:
                    dve.wait_ge(s_rt, t)
                    link(v.reciprocal(stat[:, 3, t - 1:t], stat[:, 2, t - 1:t]))
                    dve.wait_ge(s_gain, 16)
                    v.scalar_tensor_tensor(g.x[:, t - 1, :], g.x[:, t - 1, :], stat[:, 3, t - 1:t], gain_sb[:],
                                           ALU.mult, ALU.mult)


def moe(g, io, dbg):
    with ExitStack() as a:
        r = {"row_asg": g.dram("row_assignments", [(BLOCKS + 4) * P, 1], I32), "be_dram": g.dram("be_d", [BLOCKS + 4, 1], I32),
             "n_dram": g.dram("n_d", [1, 1], I32), "h": g.dram("h2_rows", [S, D]),
             "y": g.dram("y_rows", [TOPK * S, D]),
             "be_row": g.sb("be_row", [1, BLOCKS + 4], I32, ctx=a), "be_col": g.sb("be_col", [P, 1], I32, ctx=a),
             "n_col": g.sb("n_col", [P, 1], I32, ctx=a), "gate": g.sb("gate6", [P, NT, TOPK], ctx=a),
             "dest": g.sb("dest6", [P, NT, TOPK], U32, ctx=a),
             "row_asg_cols": g.sb("row_asg_cols", [P, BLOCKS + 4], U32, ctx=a),
             "row_tok": g.sb("row_tok", [P, BLOCKS + 4], I32, ctx=a)}
        acc = g.sb("moe_acc", [P, NT, D], ctx=a)
        with ExitStack() as b:
            hT = g.sb("h2T", [P, 2, KD, S], F32R, ctx=b)
            norm_stage(g, "ffn1", io["g_ffn_norm"], hT, scale=g.mod[:, 4 * D:5 * D], shift=g.mod[:, 3 * D:4 * D],
                       h_dram=r["h"])
            shared_stage(g, io, hT, acc)
            route_stage(g, io, hT, r)
        expert_stage(g, io, r)
        combine_stage(g, r, acc, g.mod[:, 5 * D:6 * D], io["g_final"].rearrange("(a d) -> a d", a=1))


def project2_stage(g, io, hT, p2):
    nc = g.nc
    w_in = io["w_in_2"][0].rearrange("(k p) n -> p k n", p=P)
    groups = [(c, min(512, W2 - c)) for c in range(0, W2, 512)]
    with g.stage() as st:
        w = SplitWeights(g, "win2", st)
        s_ps = g.sem("proj2_ready")
        s_act = g.sem("proj2_act_evacuated")
        s_dve = g.sem("proj2_dve_evacuated")
        block = st.enter_context(nc.Block())
        n = len(groups)

        @block.sync
        def _(sp):
            for s, (c, width) in enumerate(groups):
                for half in range(2):
                    w.load(sp, w_in[:, 4 * half:4 * half + 4, c:c + width], 0, 2 * s + half, width)

        @block.tensor
        def _(pe):
            for s, (_, width) in enumerate(groups):
                for half in range(2):
                    q = 2 * s + half
                    w.ready(pe, 0, q)
                    for t in range(NT):
                        if s >= 2 and half == 0:
                            pe.wait_ge((s_act, s_dve)[t // 2], 2 * (s - 2) + t % 2 + 1)
                        for j in range(4):
                            k = 4 * half + j
                            mm = split_product(nc, g.ps[:, (s % 2) * 4 + t, 0:width], parts_of(hT, k, t * P, t * P + P),
                                               w.at(q, j, 0, width), k == 0, k == KD - 1)
                        mm.then_inc(s_ps, 1)

        @block.scalar
        def _(act):
            for s in range(-1, n):
                for half in range(2):
                    if s + 1 < n:
                        w.high(act, 0, 2 * s + 2 + half, s_ps, 4, groups[s + 1][1])
                for t in range(2 if s >= 0 else 0):
                    c, width = groups[s]
                    act.wait_ge(s_ps, 8 * s + 4 + t + 1)
                    nc.scalar.copy(p2[:, t, c:c + width], g.ps[:, (s % 2) * 4 + t, 0:width]).then_inc(s_act, 1)

        @block.vector
        def _(dve):
            for s in range(-1, n):
                for half in range(2):
                    if s + 1 < n:
                        w.low(dve, 0, 2 * s + 2 + half, s_ps, 4, groups[s + 1][1])
                for t in range(2, NT if s >= 0 else 2):
                    c, width = groups[s]
                    dve.wait_ge(s_ps, 8 * s + 4 + t + 1)
                    nc.vector.tensor_copy(p2[:, t, c:c + width], g.ps[:, (s % 2) * 4 + t, 0:width]).then_inc(s_dve, 1)


Q_NSA, K_SEL, K_WIN, Q_DIL, K_DIL, Q_SB, K_SB, KV_CMP = 0, 4, 5, 6, 12, 18, 24, 30
N_COLS = 32


def heads2_stage(g, io, p2, qk, gates):
    nc = g.nc
    NH = Q_SB
    groups = [(0, Q_NSA, 4, 0), (C2_KV + 128, K_SEL, 1, 1), (C2_KV + 256, K_WIN, 1, 2), (C2_B, Q_DIL, 6, 3),
              (C2_B + 384, K_DIL, 6, 4)]
    with g.stage() as st:
        sq = g.sb("head_squares", [P, NT, NH * DH], ctx=st)
        gn = g.sb("head_gains", [P, 5, DH], ctx=st)
        ss = g.sb("head_stats", [P, 3, NT * NH], ctx=st)
        s_ld = g.sem("head_gains_loaded")
        s_ms = g.sem("head_mean_squares")
        s_rt = g.sem("head_roots")
        s_dve = g.sem("heads_dve_steps")
        block = st.enter_context(nc.Block())

        @block.sync
        def _(sp):
            for i, row in enumerate((io["qk_gain_nsa_2"][0, 0:1], io["qk_gain_nsa_2"][0, 2:3], io["qk_gain_nsa_2"][0, 3:4],
                                     io["qk_gain_dil_2"][0, 0:1], io["qk_gain_dil_2"][0, 1:2])):
                sp.dma_start(gn[:, i, :], bcast_rows(row, DH)).then_inc(s_ld, 16)

        @block.scalar
        def _(act):
            nc.scalar.mul(qk[:, :, Q_SB * DH:K_SB * DH], p2[:, :, C2_C:C2_C + 384], DH ** -0.5)
            nc.scalar.copy(qk[:, :, K_SB * DH:KV_CMP * DH], p2[:, :, C2_C + 384:C2_C + 768])
            nc.scalar.copy(qk[:, :, KV_CMP * DH:], p2[:, :, C2_KV:C2_KV + 128])
            nc.scalar.activation(gates[:], p2[:, :, C2_G:C2_G + 12], ACT.Sigmoid)
            act.wait_ge(s_ms, 1)
            nc.scalar.activation(ss[:, 2, :], ss[:, 1, :], ACT.Sqrt).then_inc(s_rt, 1)

        @block.vector
        def _(dve):
            link = Chain(dve, s_dve)
            v = nc.vector
            for src, dst, n, _ in groups:
                x = p2[:, :, src:src + n * DH]
                ins = v.tensor_tensor(sq[:, :, dst * DH:(dst + n) * DH], x, x, ALU.mult)
            link(ins)
            link(v.tensor_reduce(ss[:, 0, :], sq[:].rearrange("p t (h d) -> p (t h) d", d=DH), AX.X, ALU.add))
            v.tensor_scalar(ss[:, 1, :], ss[:, 0, :], 1.0 / DH, EPS, ALU.mult, ALU.add).then_inc(s_ms, 1)
            dve.wait_ge(s_ld, 80)
            v.tensor_scalar(gn[:, 0, :], gn[:, 0, :], DH ** -0.5, None, ALU.mult)
            v.tensor_scalar(gn[:, 3, :], gn[:, 3, :], DH ** -0.5, None, ALU.mult)
            dve.wait_ge(s_rt, 1)
            link(v.reciprocal(ss[:, 1, :], ss[:, 2, :]))
            for t in range(NT):
                for src, dst, n, _ in groups:
                    root = ss[:, 1, t * NH + dst:t * NH + dst + n].unsqueeze(2).broadcast_to([P, n, DH])
                    ins = v.tensor_tensor(qk[:, t, dst * DH:(dst + n) * DH].rearrange("p (h d) -> p h d", d=DH),
                                          p2[:, t, src:src + n * DH].rearrange("p (h d) -> p h d", d=DH), root, ALU.mult)
                link(ins)
                for src, dst, n, gain in groups:
                    y = qk[:, t, dst * DH:(dst + n) * DH].rearrange("p (h d) -> p h d", d=DH)
                    v.tensor_tensor(y, y, gn[:, gain:gain + 1, :].broadcast_to([P, n, DH]), ALU.mult)


def compressed_stage(g, io, kvT, qT, o_c):
    nc = g.nc
    N = N_CMP
    L = 32
    with g.stage() as st:
        w1 = g.sb("cmp_w1", [P, L, P], ctx=st)
        w2 = g.sb("cmp_w2", [P, 2, DH], ctx=st)
        pe_ = g.sb("cmp_pe", [P, L], ctx=st)
        un = g.sb("cmp_windows", [P, L, N], ctx=st)
        hid = g.sb("cmp_hidden", [P, 3, 2, N], ctx=st)
        kc = g.sb("kc_rows", [N, 3, DH], ctx=st)
        vc = g.sb("vc_rows", [N, DH], ctx=st)
        gain = g.sb("kc_gain", [N, DH], ctx=st)
        ms = g.sb("kc_stat", [N, 4], ctx=st)
        kcT = g.sb("kc_cols", [DH + 2, 32], ctx=st)
        q = g.sb("cmp_q", [DH + 2, H_NSA, S], ctx=st)
        mk = g.sb("cmp_mask", [P, 2, NT, 32], ctx=st)
        p = g.sb("cmp_p", [P, 4 * H_NSA, N], ctx=st)
        m = g.sb("cmp_max", [P, 3, 4 * H_NSA], ctx=st)
        pT = g.sb("cmp_pT", [N, 4 * H_NSA, P], ctx=st)
        s_w = g.sem("cmp_loads")
        s_un = g.sem("cmp_windows_ready")
        s_hid = g.sem("cmp_hidden_ready")
        s_th = g.sem("cmp_tanh_in")
        s_tg = g.sem("cmp_tanh_out")
        s_ge = g.sem("cmp_gelu_ready")
        s_kv = g.sem("cmp_kv_ready")
        s_ms = g.sem("kc_mean_square")
        s_rt = g.sem("kc_root")
        s_kn = g.sem("kc_normed")
        s_kt = g.sem("kc_turned")
        s_kc = g.sem("kc_cols_ready")
        s_s = g.sem("cmp_scores_ready")
        s_e = g.sem("cmp_exponents_ready")
        s_x = g.sem("cmp_exponentials_ready")
        s_p = g.sem("cmp_probs_ready")
        s_t = g.sem("cmp_turned")
        s_tc = g.sem("cmp_turned_copied")
        s_o = g.sem("cmp_values_ready")
        s_dve = g.sem("cmp_dve_steps")
        block = st.enter_context(nc.Block())

        @block.sync
        def _(sp):
            for c in range(2):
                sp.dma_start(w1[c * DH:c * DH + DH], io["cmp_w1_2"][0, c].rearrange("(l d) h -> d l h", d=DH)).then_inc(s_w, 16)
                sp.dma_start(pe_[c * DH:c * DH + DH, :], io["cmp_pe_2"][0, c].rearrange("l d -> d l"),
                             allow_slow_non_contiguous=True).then_inc(s_w, 16)
            sp.dma_start(w2[:], io["cmp_w2_2"][0].rearrange("c h d -> h c d")).then_inc(s_w, 16)
            sp.dma_start(gain[:], io["qk_gain_nsa_2"][0, 1:2].broadcast_to([N, DH])).then_inc(s_w, 16)
            sp.dma_start(kcT[DH:DH + 2, :], io["const_alibi_c"]).then_inc(s_w, 16)
            sp.dma_start(mk[:], io["const_cmp_mask"]).then_inc(s_w, 16)
            sp.dma_start(q[0:DH], qT[Q_NSA * DH:(Q_NSA + H_NSA) * DH, :].rearrange("(h d) s -> d h s", d=DH)).then_inc(s_w, 16)
            sp.dma_start(q[DH:DH + 2], io["const_alibi_q"][2 * H_DIL:2 * H_DIL + 2 * H_NSA, :].rearrange("(h r) s -> r h s", r=2)).then_inc(s_w, 16)

        @block.tensor
        def _(pe):
            pe.wait_ge(s_un, 1)
            for c in range(2):
                rows = slice(c * DH, c * DH + DH)
                for i in range(L):
                    mm = nc.tensor.matmul(g.ps[:, c, 0:N], w1[rows, i, :], un[rows, i, :], start=i == 0, stop=i == L - 1)
                mm.then_inc(s_hid, 1)
            pe.wait_ge(s_ge, 1)
            for c in range(2):
                nc.tensor.matmul(g.ps[0:N, 2 + c, 0:DH], hid[:, 0, c, :], w2[:, c, :], start=True, stop=True).then_inc(s_kv, 1)
            pe.wait_ge(s_kn, 1)
            nc.tensor.transpose(g.ps[0:DH, 4, 0:N], kc[:, 0, :], g.ident[0:N, 0:N]).then_inc(s_kt, 1)
            pe.wait_ge(s_kc, 1)
            for i in range(4 * H_NSA):
                mm = nc.tensor.matmul(g.ps[:, 5, i * N:i * N + N], q[:, i // 4, (i % 4) * P:(i % 4) * P + P],
                                      kcT[:, 0:N], start=True, stop=True)
            mm.then_inc(s_s, 1)
            pe.wait_ge(s_p, 1)
            for b in range(4):
                for i in range(4 * b, 4 * b + 4):
                    tr = nc.tensor.transpose(g.ps[0:N, b, (i % 4) * P:(i % 4) * P + P], p[:, i, :], g.ident[:])
                tr.then_inc(s_t, 1)
            for i in range(4 * H_NSA):
                if i % 4 == 0:
                    pe.wait_ge(s_tc, i // 4 + 1)
                mm = nc.tensor.matmul(g.ps[:, 6 + i // 8, (i % 8) * DH:(i % 8) * DH + DH], pT[:, i, :], vc[:],
                                      start=True, stop=True)
                if i % 8 == 7:
                    mm.then_inc(s_o, 1)

        @block.scalar
        def _(act):
            act.wait_ge(s_th, 1)
            nc.scalar.activation(hid[:, 1], hid[:, 1], ACT.Tanh, scale=0.7978845608028654).then_inc(s_tg, 1)
            act.wait_ge(s_ms, 1)
            nc.scalar.activation(ms[:, 2:3], ms[:, 1:2], ACT.Sqrt).then_inc(s_rt, 1)
            act.wait_ge(s_e, 1)
            nc.scalar.activation(p[:], p[:], ACT.Exp).then_inc(s_x, 1)
            for b in range(4):
                act.wait_ge(s_t, b + 1)
                nc.scalar.copy(pT[:, 4 * b:4 * b + 4, :], g.ps[0:N, b, :].rearrange("p (i q) -> p i q", q=P)).then_inc(s_tc, 1)

        @block.vector
        def _(dve):
            link = Chain(dve, s_dve)
            v = nc.vector
            dve.wait_ge(s_w, 160)
            src = kvT.rearrange("p (n b) -> p b n", b=16)
            for a in range(2):
                link(v.tensor_tensor(un[:, 16 * a:16 * a + 16, :], src[:, :, a:a + N],
                                     pe_[:, 16 * a:16 * a + 16].unsqueeze(2).broadcast_to([P, 16, N]), ALU.add))
            dve.sem_inc(s_un, 1)
            dve.wait_ge(s_hid, 2)
            link(v.tensor_copy(hid[:, 0], g.ps[:, 0:2, 0:N]))
            link(v.tensor_tensor(hid[:, 1], hid[:, 0], hid[:, 0], ALU.mult))
            link(v.tensor_scalar(hid[:, 1], hid[:, 1], 0.044715, 1.0, ALU.mult, ALU.add))
            v.tensor_tensor(hid[:, 1], hid[:, 1], hid[:, 0], ALU.mult).then_inc(s_th, 1)
            dve.wait_ge(s_tg, 1)
            link(v.tensor_scalar(hid[:, 1], hid[:, 1], 1.0, 0.5, ALU.add, ALU.mult))
            v.tensor_tensor(hid[:, 0], hid[:, 0], hid[:, 1], ALU.mult).then_inc(s_ge, 1)
            dve.wait_ge(s_kv, 2)
            v.tensor_copy(vc[:], g.ps[0:N, 3, 0:DH])
            link(v.tensor_copy(kc[:, 1, :], g.ps[0:N, 2, 0:DH]))
            link(v.tensor_tensor(kc[:, 2, :], kc[:, 1, :], kc[:, 1, :], ALU.mult))
            link(v.tensor_reduce(ms[:, 0:1], kc[:, 2, :], AX.X, ALU.add))
            v.tensor_scalar(ms[:, 1:2], ms[:, 0:1], 1.0 / DH, EPS, ALU.mult, ALU.add).then_inc(s_ms, 1)
            dve.wait_ge(s_rt, 1)
            link(v.reciprocal(ms[:, 3:4], ms[:, 2:3]))
            v.scalar_tensor_tensor(kc[:, 0, :], kc[:, 1, :], ms[:, 3:4], gain[:], ALU.mult, ALU.mult).then_inc(s_kn, 1)
            dve.wait_ge(s_kt, 1)
            v.tensor_copy(kcT[0:DH, 0:N], g.ps[0:DH, 4, 0:N]).then_inc(s_kc, 1)
            dve.wait_ge(s_s, 1)
            for h in range(H_NSA):
                ins = v.tensor_tensor(p[:, 4 * h:4 * h + 4, :], g.ps[:, 5, 4 * h * N:4 * (h + 1) * N].rearrange("p (i n) -> p i n", n=N),
                                      mk[:, 1, :, 0:N], ALU.add)
            link(ins)
            link(v.tensor_reduce(m[:, 0, :], p[:], AX.X, ALU.max))
            v.tensor_tensor(p[:], p[:], m[:, 0, :].unsqueeze(2).broadcast_to([P, 16, N]), ALU.subtract).then_inc(s_e, 1)
            dve.wait_ge(s_x, 1)
            for h in range(H_NSA):
                ins = v.tensor_tensor(p[:, 4 * h:4 * h + 4, :], p[:, 4 * h:4 * h + 4, :], mk[:, 0, :, 0:N], ALU.mult)
            link(ins)
            link(v.tensor_reduce(m[:, 1, :], p[:], AX.X, ALU.add))
            link(v.tensor_scalar(m[:, 1, :], m[:, 1, :], 1e-30, None, ALU.max))
            link(v.reciprocal(m[:, 2, :], m[:, 1, :]))
            v.tensor_tensor(p[:], p[:], m[:, 2, :].unsqueeze(2).broadcast_to([P, 16, N]), ALU.mult).then_inc(s_p, 1)
            for b in range(2):
                dve.wait_ge(s_o, b + 1)
                v.tensor_copy(o_c[:, 8 * b:8 * b + 8, :], g.ps[:, 6 + b, :].rearrange("p (i d) -> p i d", d=DH))


def stick_stage(g, heads, q_parts, k_parts, v, out, mask):
    nc = g.nc
    LT, LV = 3, 5
    with g.stage() as st:
        q = g.sb("sb_q", [DH, 2, S], ctx=st)
        kk = g.sb("sb_k", [DH, 2, S], ctx=st)
        la = g.sb("sb_log", [P, 4, S], ctx=st)
        sp_ = g.sb("sb_softplus", [P, 2, S], ctx=st)
        su = g.sb("sb_sums", [P, 4, S], ctx=st)
        ones = g.sb("sb_ones", [P, S], ctx=st)
        p = g.sb("sb_p", [P, 4, S], ctx=st)
        pt = g.sb("sb_pt", [P, 4, NT, P], ctx=st)
        s_qk = [g.sem(f"sb_qk_loaded{i}") for i in range(2)]
        s_s = g.sem("sb_scores_ready")
        s_ab = g.sem("sb_abs_ready")
        s_ex = g.sem("sb_exp_ready")
        s_ln = g.sem("sb_log_ready")
        s_sp = g.sem("sb_softplus_ready")
        s_su = g.sem("sb_sums_ready")
        s_x = g.sem("sb_exponents_ready")
        s_p = g.sem("sb_weights_ready")
        s_t = g.sem("sb_turned")
        s_pt = g.sem("sb_turned_copied")
        s_o = g.sem("sb_values_ready")
        s_od = g.sem("sb_out_done")
        s_one = g.sem("sb_ones_ready")
        loads = 16 * (len(q_parts) + len(k_parts))
        block = st.enter_context(nc.Block())

        @block.sync
        def _(sp):
            fetch_heads(g, sp, heads, q, kk, q_parts, k_parts, s_qk, s_s)

        @block.tensor
        def _(pe):
            def body(i, base, drain):
                for u in range(8):
                    j, t = u // 4, u % 4
                    n = (t + 1) * P
                    if not drain:
                        if t == 0:
                            pe.wait_ge(s_qk[j], loads * i + loads)
                        at_least(pe, s_ab, base, u - 3)
                        at_least(pe, s_x, base, u - 3)
                        mk, first = mask(i, t)
                        nc.tensor.matmul(g.ps[:, u % 4, 0:n], q[:, j, t * P:t * P + P], kk[:, j, 0:n],
                                         start=True, stop=False)
                        nc.tensor.matmul(g.ps[:, u % 4, first:n], g.identb[:], mk,
                                         start=False, stop=True).then_inc(s_s, 1)
                    if (at := lagging(base, u, LT, drain)) is not None:
                        a = at[0]
                        at_least(pe, s_p, base, u - LT + 1)
                        at_least(pe, s_pt, base, u - LT - 1)
                        for b in range(a % 4 + 1):
                            tr = nc.tensor.transpose(g.ps[:, 4 + a % 2, b * P:b * P + P], p[:, a % 4, b * P:b * P + P],
                                                     g.ident[:])
                        tr.then_inc(s_t, 1)
                    if (at := lagging(base, u, LV, drain)) is not None:
                        a, head = at[0], 2 * i + at[0] // 4 - 2 * at[1]
                        at_least(pe, s_pt, base, u - LV + 1)
                        at_least(pe, s_od, base, u - LV - 1)
                        for b in range(a % 4 + 1):
                            mm = nc.tensor.matmul(g.ps[:, 6 + a % 2, 0:DH], pt[:, a % 4, b, :], v(b, head),
                                                  start=b == 0, stop=b == a % 4)
                        mm.then_inc(s_o, 1)
            turns(pe, heads, body)

        @block.scalar
        def _(act):
            def body(i, base, drain):
                if drain:
                    return
                for first in (0, 4):
                    places = range(first, first + 4)
                    for u in places:
                        z, l = g.ps[:, u % 4, 0:(u % 4 + 1) * P], la[:, u % 4, 0:(u % 4 + 1) * P]
                        at_least(act, s_s, base, u + 1)
                        at_least(act, s_sp, base, u - 3)
                        nc.scalar.activation(l, z, ACT.Abs).then_inc(s_ab, 1)
                        at_least(act, s_ab, base, u + 1)
                        nc.scalar.activation(l, l, ACT.Exp, scale=-1.0).then_inc(s_ex, 1)
                    for u in places:
                        l = la[:, u % 4, 0:(u % 4 + 1) * P]
                        at_least(act, s_ex, base, u + 1)
                        nc.scalar.activation(l, l, ACT.Ln, bias=1.0).then_inc(s_ln, 1)
                    for u in places:
                        n = (u % 4 + 1) * P
                        at_least(act, s_x, base, u + 1)
                        at_least(act, s_t, base, u - 3)
                        nc.scalar.activation(p[:, u % 4, 0:n], su[:, u % 4, 0:n], ACT.Exp).then_inc(s_p, 1)
            turns(act, heads, body)

        @block.vector
        def _(dve):
            nc.vector.memset(ones[:], 1.0).then_inc(s_one, 1)
            dve.wait_ge(s_one, 1)

            def body(i, base, drain):
                for u in range(8):
                    n = (u % 4 + 1) * P
                    if (at := lagging(base, u, LT, drain)) is not None:
                        a = at[0]
                        at_least(dve, s_t, base, u - LT + 1)
                        at_least(dve, s_o, base, u - LT - 3)
                        nc.vector.tensor_copy(pt[:, a % 4, 0:a % 4 + 1, :],
                                              g.ps[:, 4 + a % 2, 0:(a % 4 + 1) * P].rearrange("p (b s) -> p b s", s=P)
                                              ).then_inc(s_pt, 1)
                    if (at := lagging(base, u, LV, drain)) is not None:
                        a, head = at[0], 2 * i + at[0] // 4 - 2 * at[1]
                        at_least(dve, s_o, base, u - LV + 1)
                        nc.vector.tensor_copy(out(a % 4, head), g.ps[:, 6 + a % 2, 0:DH]).then_inc(s_od, 1)
                    if not drain:
                        z = g.ps[:, u % 4, 0:n]
                        s, c = sp_[:, u % 2, 0:n], su[:, u % 4, 0:n]
                        at_least(dve, s_ln, base, u + 1)
                        nc.vector.scalar_tensor_tensor(s, z, 0.0, la[:, u % 4, 0:n], ALU.max, ALU.add).then_inc(s_sp, 1)
                        at_least(dve, s_sp, base, u + 1)
                        at_least(dve, s_p, base, u - 3)
                        nc.vector.tensor_tensor_scan(c[:, ::-1], ones[:, 0:n], s[:, ::-1], 0.0, ALU.mult,
                                                     ALU.add).then_inc(s_su, 1)
                        at_least(dve, s_su, base, u + 1)
                        nc.vector.tensor_tensor(c, z, c, ALU.subtract).then_inc(s_x, 1)
            turns(dve, heads, body)


def gather_heads_stage(g, o_c, o_nsa, o_dil, stats, gates, cat):
    nc = g.nc
    with g.stage() as st:
        lse = g.sb("lse", [P, 24], ctx=st)
        tmp = g.sb("gated", [P, 2, H_NSA, DH], ctx=st)
        al = g.sb("alpha", [P, 3, 8], ctx=st)
        mx = g.sb("lse_max", [P, 3, 8], ctx=st)
        s_ln = g.sem("log_sums_ready")
        s_e = g.sem("lse_exponents_ready")
        s_x = g.sem("lse_exponentials_ready")
        s_dve = g.sem("gather_dve_steps")
        block = st.enter_context(nc.Block())

        @block.scalar
        def _(act):
            nc.scalar.activation(lse[:], stats[:, 1, :], ACT.Ln).then_inc(s_ln, 1)
            act.wait_ge(s_e, 1)
            nc.scalar.activation(al[:], al[:], ACT.Exp).then_inc(s_x, 1)

        @block.vector
        def _(dve):
            link = Chain(dve, s_dve)
            v = nc.vector
            dve.wait_ge(s_ln, 1)
            link(v.tensor_tensor(lse[:], lse[:], stats[:, 0, :], ALU.subtract))
            link(v.tensor_tensor(mx[:, 0, :], lse[:, 0:8], lse[:, 8:16], ALU.max))
            link(v.tensor_tensor(mx[:, 0, :], mx[:, 0, :], lse[:, 16:24], ALU.max))
            v.tensor_tensor(al[:], lse[:].rearrange("p (g a) -> p g a", a=8), mx[:, 0:1, :].broadcast_to([P, 3, 8]),
                            ALU.subtract).then_inc(s_e, 1)
            for t in range(NT):
                gt = gates[:, t, :].rearrange("p (h b) -> p h b", b=3)
                c3 = cat[:, t, 0:256].rearrange("p (h d) -> p h d", d=DH)
                branches = [o_c[:].rearrange("p (h t) d -> p t h d", t=NT)[:, t]]
                branches += [o_nsa[:, t, 256 * j:256 * j + 256].rearrange("p (h d) -> p h d", d=DH) for j in range(2)]
                for j, o in enumerate(branches):
                    gb = gt[:, :, j:j + 1].broadcast_to([P, H_NSA, DH])
                    if j == 0:
                        link(v.tensor_tensor(c3, o, gb, ALU.mult))
                    else:
                        link(v.tensor_tensor(tmp[:, 0], o, gb, ALU.mult))
                        link(v.tensor_tensor(c3, c3, tmp[:, 0], ALU.add))
            dve.wait_ge(s_x, 1)
            link(v.tensor_tensor(mx[:, 1, :], al[:, 0, :], al[:, 1, :], ALU.add))
            link(v.tensor_tensor(mx[:, 1, :], mx[:, 1, :], al[:, 2, :], ALU.add))
            link(v.reciprocal(mx[:, 2, :], mx[:, 1, :]))
            link(v.tensor_tensor(al[:], al[:], mx[:, 2:3, :].broadcast_to([P, 3, 8]), ALU.mult))
            for t in range(NT):
                for h in range(2):
                    dst = cat[:, t, 256 + h * DH:256 + h * DH + DH]
                    a = 4 * h + t
                    for grp in range(3):
                        o = o_dil[:, t, (2 * grp + h) * DH:(2 * grp + h) * DH + DH]
                        if grp == 0:
                            link(v.tensor_scalar(dst, o, al[:, 0, a:a + 1], None, ALU.mult))
                        else:
                            link(v.scalar_tensor_tensor(dst, o, al[:, grp, a:a + 1], dst, ALU.mult, ALU.add))


def mlp_up_stage(g, io, hT, u):
    nc = g.nc
    TURNS = FF // 1024
    w_up = io["w_up_2"][0].rearrange("(k p) n -> p k n", p=P)
    with g.stage() as st:
        w = SplitWeights(g, "w_up", st)
        s_ps = g.sem("mlp_up_ready")
        s_re = g.sem("relu_ready")
        s_sq = g.sem("square_ready")
        block = st.enter_context(nc.Block())

        def turns_of(eng, body):
            body(0, 0)
            with eng.Fori(1, TURNS) as i:
                body(i, 4 * i)

        def strip(i, c):
            return u[:, bass.ds(8 * i + c, 1), :].rearrange("p a s -> p (a s)")

        @block.sync
        def _(sp):
            def body(i, base):
                for q in range(4):
                    half = q % 2
                    w.load(sp, w_up[:, 4 * half:4 * half + 4, bass.ds(1024 * i + 512 * (q // 2), 512)], base, q)
            turns_of(sp, body)

        @block.tensor
        def _(pe):
            def body(i, base):
                for q in range(4):
                    half = q % 2
                    w.ready(pe, base, q)
                    for m in range(4):
                        c = 4 * (q // 2) + m
                        if half == 0:
                            at_least(pe, s_sq, 2 * base, c - 7)
                        for j in range(4):
                            k = 4 * half + j
                            mm = split_product(nc, g.ps[:, c, :], w.at(q, j, m * P, m * P + P), parts_of(hT, k),
                                               k == 0, k == KD - 1)
                        mm.then_inc(s_ps, 1)
            turns_of(pe, body)

        @block.scalar
        def _(act):
            def relus(i, base, grp):
                for m in range(4):
                    c = 4 * grp + m
                    act.wait_ge(s_ps, 4 * base + 8 * grp + 4 + m + 1)
                    nc.scalar.activation(strip(i, c), g.ps[:, c % 8, :], ACT.Relu).then_inc(s_re, 1)

            def body(i, base):
                for grp in range(2):
                    w.high(act, base, 2 * grp, s_ps, 4)
                    w.high(act, base, 2 * grp + 1, s_ps, 4)
                    if grp or not isinstance(base, int):
                        relus(i, base, grp - 1)
            turns_of(act, body)
            relus(TURNS, 4 * TURNS, -1)

        @block.vector
        def _(dve):
            def squares(i, base, grp):
                for m in range(4):
                    c = 4 * grp + m
                    dve.wait_ge(s_re, 2 * base + c + 1)
                    nc.vector.tensor_tensor(strip(i, c), strip(i, c), strip(i, c), ALU.mult).then_inc(s_sq, 1)

            def body(i, base):
                for grp in range(2):
                    w.low(dve, base, 2 * grp, s_ps, 4)
                    w.low(dve, base, 2 * grp + 1, s_ps, 4)
                    if grp or not isinstance(base, int):
                        squares(i, base, grp - 1)
            turns_of(dve, body)
            squares(TURNS, 4 * TURNS, -1)


def mlp_down_stage(g, io, u, out):
    nc = g.nc
    TURNS = FF // P // 8
    w_down = io["w_down_2"][0].rearrange("(k p) n -> p k n", p=P)
    with g.stage() as st:
        w = SplitWeights(g, "w_down", st)
        up = g.sb("hidden2_parts", [P, 2, 2, 4, S], F32R, ctx=st)
        s_uh = g.sem("hidden2_high_ready")
        s_ul = g.sem("hidden2_low_ready")
        s_ps = g.sem("mlp_down_ready")
        s_x = g.sem("x_ready")
        s_out = g.sem("out_stored")
        out_d = out.rearrange("(t p) d -> p t d", p=P)
        block = st.enter_context(nc.Block())

        def turns_of(eng, body):
            body(0, 0, 0)
            with eng.Fori(1, TURNS - 1) as i:
                body(i, 4 * i, 1)
            body(TURNS - 1, 4 * (TURNS - 1), 2)

        @block.sync
        def _(sp):
            def body(i, base, place):
                for q in range(4):
                    n = q % 2
                    w.load(sp, w_down[:, bass.ds(8 * i + 4 * (q // 2), 4), n * 512:n * 512 + 512], base, q)
            turns_of(sp, body)
            for t in range(NT):
                sp.wait_ge(s_x, NT + t + 1)
                sp.dma_start(out_d[:, t, :], g.x[:, t, :]).then_inc(s_out, 16)
            sp.wait_ge(s_out, 16 * NT)

        @block.tensor
        def _(pe):
            def body(i, base, place):
                for q in range(4):
                    c, n = q // 2, q % 2
                    if n == 0:
                        pe.wait_ge(s_uh, 2 * i + c + 1)
                        pe.wait_ge(s_ul, 2 * i + c + 1)
                    w.ready(pe, base, q)
                    for t in range(NT):
                        for k in range(4):
                            left = [up[:, c, a, k, t * P:t * P + P] for a in range(2)]
                            mm = split_product(nc, g.ps[:, 4 * n + t, :], left, w.at(q, k, 0, 512),
                                               place == 0 and c == 0 and k == 0, place == 2 and c == 1 and k == 3)
                        mm.then_inc(s_ps, 1)
            turns_of(pe, body)

        @block.scalar
        def _(act):
            def body(i, base, place):
                for c in range(2):
                    at_least(act, s_ps, 4 * base, 8 * c - 8)
                    nc.scalar.copy(up[:, c, 0], u[:, bass.ds(8 * i + 4 * c, 4), :]).then_inc(s_uh, 1)
                    w.high(act, base, 2 * c, s_ps, 4)
                    w.high(act, base, 2 * c + 1, s_ps, 4)
            turns_of(act, body)

        @block.vector
        def _(dve):
            def body(i, base, place):
                for c in range(2):
                    at_least(dve, s_ps, 4 * base, 8 * c - 8)
                    dve.wait_ge(s_uh, 2 * i + c + 1)
                    low_part(nc, up[:, c, 1], u[:, bass.ds(8 * i + 4 * c, 4), :], up[:, c, 0]).then_inc(s_ul, 1)
                    w.low(dve, base, 2 * c, s_ps, 4)
                    w.low(dve, base, 2 * c + 1, s_ps, 4)
            turns_of(dve, body)
            for n in range(2):
                for t in range(NT):
                    dve.wait_ge(s_ps, 16 * TURNS - 8 + 4 * n + t + 1)
                    xs = g.x[:, t, n * 512:n * 512 + 512]
                    nc.vector.tensor_tensor(xs, g.ps[:, 4 * n + t, :], xs, ALU.add).then_inc(s_x, 1)


def block2(g, io, dbg, out):
    colsT = g.dram("heads_T", [N_COLS * DH, S])
    with ExitStack() as a:
        o_c = g.sb("o_cmp", [P, 4 * H_NSA, DH], ctx=a)
        gates = g.sb("nsa_gates", [P, NT, 12], ctx=a)
        p2 = g.sb("p2", [P, NT, W2], ctx=a)
        with ExitStack() as b:
            hT = g.sb("h3T", [P, 2, KD, S], F32R, ctx=b)
            norm_stage(g, "mix2", io["norm_mix_2"], hT)
            project2_stage(g, io, hT, p2)
        with ExitStack() as b:
            cols = g.sb("cols2", [P, N_COLS // 2, S], ctx=b)
            with ExitStack() as c:
                qk = g.sb("qk2", [P, NT, N_COLS * DH], ctx=c)
                heads2_stage(g, io, p2, qk, gates)
                turn_stage(g, "heads2", qk, N_COLS * DH, cols, dram=colsT)
            compressed_stage(g, io, cols[:, N_COLS // 2 - 1, :], colsT, o_c)
        o_nsa = g.sb("o_nsa", [P, NT, 2 * H_NSA * DH], ctx=a)
        o_dil = g.sb("o_dil", [P, NT, H_DIL * DH], ctx=a)
        cat = g.sb("cat", [P, NT, D_CAT], ctx=a)
        stats = g.sb("dil_stats", [P, 2, 4 * H_DIL], ctx=a)
        aq, ak = io["const_alibi_q"], io["const_alibi_k"]

        def causal(i, t):
            return g.mask[:, 0, 384:512], t * P
        for j, (nm, kh) in enumerate((("sel", K_SEL), ("win", K_WIN))):
            attention_stage(g, nm, H_NSA, [(colsT, DH, lambda h: (h + Q_NSA) * DH), (aq, 2, lambda h: (h + H_DIL) * 2)],
                            [(colsT, DH, lambda h, kh=kh: h * 0 + kh * DH), (ak, 2, lambda h: h * 0)],
                            lambda b, h, j=j: p2[:, b, C2_KV + (3 + 2 * j) * DH:C2_KV + (4 + 2 * j) * DH],
                            lambda t, h, j=j: o_nsa[:, t, bass.ds(h * DH + 256 * j, DH)], causal)
        attention_stage(g, "dil", H_DIL, [(colsT, DH, lambda h: (h + Q_DIL) * DH), (aq, 2, lambda h: h * 2)],
                        [(colsT, DH, lambda h: (h + K_DIL) * DH), (ak, 2, lambda h: h * 0)],
                        lambda b, h: p2[:, b, bass.ds(h * DH + C2_B + 768, DH)],
                        lambda t, h: o_dil[:, t, bass.ds(h * DH, DH)],
                        lambda i, t: (g.mask[:, bass.ds(i + 2, 1), 384 - t * P:512].rearrange("p a s -> p (a s)"), 0),
                        stats=stats)
        stick_stage(g, H_SB, [(colsT, DH, lambda h: (h + Q_SB) * DH)], [(colsT, DH, lambda h: (h + K_SB) * DH)],
                    lambda b, h: p2[:, b, bass.ds(h * DH + C2_C + 768, DH)],
                    lambda t, h: cat[:, t, bass.ds(h * DH + 384, DH)],
                    lambda i, t: (g.mask[:, 1, 384:512], t * P))
        gather_heads_stage(g, o_c, o_nsa, o_dil, stats, gates, cat)
        if "cat" in dbg:
            dump(g, dbg["cat"].rearrange("(t p) d -> p t d", p=P), cat[:], "dump_cat")
        with ExitStack() as b:
            catT = g.sb("catT", [P, 2, D_CAT // P, S], F32R, ctx=b)
            turn_parts_stage(g, "catturn", cat, D_CAT, catT)
            add_product_stage(g, "out2", catT, io["w_out_2"][0], D_CAT // P)
    if "x4" in dbg:
        dump(g, dbg["x4"].rearrange("(t p) d -> p t d", p=P), g.x[:], "dump_x4")
    with ExitStack() as a:
        u = g.sb("hidden2", [P, FF // P, S], ctx=a)
        with ExitStack() as b:
            hT = g.sb("h4T", [P, 2, KD, S], F32R, ctx=b)
            norm_stage(g, "mlp2", io["norm_mlp_2"], hT)
            mlp_up_stage(g, io, hT, u)
        mlp_down_stage(g, io, u, out)


def build(nc, io, out, dbg={}, upto=9):
    with ExitStack() as ctx:
        g = Ctx(nc, ctx)
        g.ps = ctx.enter_context(nc.psum_tensor("ps", [P, 8, 512], F32))
        g.x = g.sb("x", [P, NT, D])
        g.ident = g.sb("ident", [P, P])
        g.identb = g.sb("identb", [P, P], BF16)
        g.tri = g.sb("tri", [P, P])
        g.ones = g.sb("ones", [P, P])
        g.mask = g.sb("mask", [P, 5, 512], BF16)
        g.iota = g.sb("iota", [P, P + 8])
        g.ropec = g.sb("ropec", [P, 2])
        g.cond = g.sb("silu_c", [P, KD])
        with ExitStack() as b1:
            g.mod = g.sb("mod", [P, 6 * D], ctx=b1)
            setup_stage(g, io)
            block1_mixer(g, io, dbg)
            if "x1" in dbg:
                dump(g, dbg["x1"].rearrange("(t p) d -> p t d", p=P), g.x[:], "dump_x1")
            if upto >= 2:
                moe(g, io, dbg)
        if upto >= 2:
            if "x3" in dbg:
                dump(g, dbg["x3"].rearrange("(t p) d -> p t d", p=P), g.x[:], "dump_x3")
        if upto >= 3:
            block2(g, io, dbg, out)
        else:
            dump(g, out.rearrange("(t p) d -> p t d", p=P), g.x[:], "stored_x")


_INS = ["x", "c", "positions", "w_mod", "b_mod", "g_mix_norm", "w_in", "b_forget", "g_q_lat", "w_q_up", "g_kv_lat",
        "w_kv_up", "w_o_mla", "w_o_fox", "w_out", "g_ffn_norm", "w_router", "b_router", "w_exp_gate", "w_exp_up",
        "w_exp_down", "w_sh_gate", "w_sh_up", "w_sh_down", "g_final", "norm_mix_2", "norm_mlp_2", "w_in_2",
        "qk_gain_nsa_2", "qk_gain_dil_2", "cmp_pe_2", "cmp_w1_2", "cmp_w2_2", "w_out_2", "w_up_2", "w_down_2"]


def constants():
    import numpy as np
    f = np.float32
    q = np.arange(P)[:, None]
    dist = q - (np.arange(512)[None, :] - 384)
    keep = [dist >= 0, dist > 0, (dist >= 0) & (dist <= 128), (dist >= 0) & (dist % 4 == 0), (dist >= 0) & (dist % 16 == 0)]
    mask = np.stack([np.where(m, 0, NEG) for m in keep], axis=1).astype(f)
    freq = np.power(f(10000.0), -(np.arange(16, dtype=f) / f(16)))
    rope = np.stack([freq[np.arange(P) % 16], np.where(np.arange(P) % 32 < 16, -1, 1)], axis=1).astype(f)
    iota = np.concatenate([np.broadcast_to(np.arange(P), (P, P)), np.arange(P)[:, None] + P * np.arange(8)[None]], axis=1).astype(f)
    slopes = np.exp2(f(-8.0) * np.arange(1, 11, dtype=f) / f(10)).astype(f)
    t = np.arange(S, dtype=f)
    alibi_q = np.stack([-slopes[:, None] * t, np.broadcast_to(slopes[:, None], (10, S))], axis=1).astype(f)
    alibi_k = np.stack([np.ones(S), t]).astype(f)
    ends = 16 * np.arange(32) + 31
    alibi_c = np.stack([np.ones(32), ends]).astype(f)
    tok = np.arange(S).reshape(NT, P).T[:, :, None]
    seen = ((tok >= ends) & (np.arange(32) < N_CMP))
    cmp_mask = np.stack([seen.astype(f), np.where(seen, 0, NEG).astype(f)], axis=1)
    return {"const_ident": np.eye(P, dtype=f), "const_tri": np.triu(np.ones((P, P), f), 1), "const_mask": mask,
            "const_rope": rope, "const_iota": iota, "const_alibi_q": alibi_q.reshape(20, S), "const_alibi_k": alibi_k,
            "const_alibi_c": alibi_c, "const_cmp_mask": cmp_mask.astype(f),
            "const_assignments": (np.arange(TOPK * S, dtype=np.int32).reshape(TOPK, NT, P).transpose(2, 1, 0)).copy(),
            "const_pad_rows": TOPK * S + np.arange((BLOCKS + 4) * P, dtype=np.int32)[:, None]}


def kernel(**inputs):
    import numpy as _np
    import concourse.bacc as _bacc
    from concourse.bass_utils import run_bass_kernel_spmd as _run

    nc = _bacc.Bacc("TRN2", target_bir_lowering=False, num_devices=1)
    arrays, io = {}, {}
    for name, a in [(n, inputs[n]) for n in _INS] + list(constants().items()):
        a = _np.ascontiguousarray(a)
        arrays[f"in_{name}"] = a
        io[name] = nc.dram_tensor(f"in_{name}", a.shape, mybir.dt.from_np(a.dtype), kind="ExternalInput").ap()
    out = nc.dram_tensor("out_0", (S, D), F32, kind="ExternalOutput").ap()
    build(nc, io, out)
    r = _run(nc, [arrays], core_ids=[0])
    return r.results[0]["out_0"].reshape(1, S, D)
```
